# Optimizing a Trainium2 kernel written in Bass

```python
import jax, jax.numpy as jnp
from jax import lax
import numpy as np

D_MODEL = 1024
BATCH = 1
SEQ = 128
DEPTH = 1
DEC_BATCH = 1
DEC_SEQ = 512
PAST_LEN = 128

GRID_W = 64
CHUNK = 128
EPS = 1e-6
N_MOD = 6
N_BRANCH = 2
SSD_HEADS = 16
SSD_HEAD_DIM = 64
SSD_WIDTH = SSD_HEADS * SSD_HEAD_DIM
SSD_STATE = 128
SSD_GROUPS = 4
CONV_K = 3
CONV_CH = SSD_WIDTH + 2 * SSD_GROUPS * SSD_STATE
MLSTM_HEADS = 4
MLSTM_HEAD_DIM = 256
MLSTM_WIDTH = MLSTM_HEADS * MLSTM_HEAD_DIM
PEER_HEADS = 8
PEER_KEY_DIM = 256
PEER_N_KEYS = 128
PEER_TOPK = 16
PEER_EXPERTS = PEER_N_KEYS * PEER_N_KEYS
PEER_BLOCK = 128
IN_SPLITS = (SSD_WIDTH, CONV_CH, 2 * SSD_HEADS, MLSTM_WIDTH, MLSTM_WIDTH, MLSTM_WIDTH, MLSTM_WIDTH, 4 * MLSTM_HEADS, N_BRANCH * D_MODEL)
IN_COLS = SSD_WIDTH + CONV_CH + 2 * SSD_HEADS + 4 * MLSTM_WIDTH + 4 * MLSTM_HEADS + N_BRANCH * D_MODEL

kernel_name = 'bidir_ssd_mlstm_peer_prefix_step'

def rms_norm(x, g):
    xf = x.astype(jnp.float32)
    y = xf * lax.rsqrt(jnp.mean(xf * xf, axis=-1, keepdims=True) + EPS)
    return (y * g.astype(jnp.float32)).astype(x.dtype)

def flip(t):
    return jnp.flip(t, axis=1)

def adaln(cvec, w, b):
    return jax.nn.silu(cvec) @ w + b

def dwconv_centred(u, w, b):
    pad = CONV_K // 2
    n = u.shape[-2]
    up = jnp.pad(u, [(0, 0)] * (u.ndim - 2) + [(pad, pad), (0, 0)])
    out = b + w[0] * up[..., 0:n, :]
    for j in range(1, CONV_K):
        out = out + w[j] * up[..., j:j + n, :]
    return out

def ssd_scan(x, dt, a, b_in, c_in, h0):
    bsz, n, nh, hp = x.shape
    nc = n // CHUNK
    rep = nh // b_in.shape[2]
    x = x.astype(jnp.float32)
    dt = dt.astype(jnp.float32)
    bh = jnp.repeat(b_in.astype(jnp.float32), rep, axis=2).reshape(bsz, nc, CHUNK, nh, -1)
    ch = jnp.repeat(c_in.astype(jnp.float32), rep, axis=2).reshape(bsz, nc, CHUNK, nh, -1)
    xdt = (x * dt[..., None]).reshape(bsz, nc, CHUNK, nh, hp)
    acs = jnp.cumsum((dt * a).reshape(bsz, nc, CHUNK, nh).transpose(0, 3, 1, 2), axis=-1)
    causal = jnp.tril(jnp.ones((CHUNK, CHUNK), dtype=bool))
    lmat = jnp.exp(jnp.where(causal, acs[..., :, None] - acs[..., None, :], -jnp.inf))
    scores = jnp.einsum('bclhn,bcshn->bhcls', ch, bh) * lmat
    y_diag = jnp.einsum('bhcls,bcshp->bclhp', scores, xdt)
    decay_end = jnp.exp(acs[..., -1:] - acs)
    chunk_states = jnp.einsum('bclhn,bhcl,bclhp->bchpn', bh, decay_end, xdt)
    chunk_decay = jnp.exp(acs[..., -1])

    def step(h, inp):
        s_c, d_c = inp
        return d_c[..., None, None] * h + s_c, h

    h_fin, h_prev = lax.scan(step, h0.astype(jnp.float32),
                             (chunk_states.transpose(1, 0, 2, 3, 4), chunk_decay.transpose(2, 0, 1)))
    h_prev = h_prev.transpose(1, 0, 2, 3, 4)
    y_off = jnp.einsum('bclhn,bchpn,bhcl->bclhp', ch, h_prev, jnp.exp(acs))
    return (y_diag + y_off).reshape(bsz, n, nh, hp), h_fin

def mlstm_scan(q, k, v, log_i, log_f, c0, n0, m0):
    bsz, n, nh, dh = q.shape
    nc = n // CHUNK

    def chunks(t):
        return t.astype(jnp.float32).reshape(bsz, nc, CHUNK, nh, dh).transpose(0, 3, 1, 2, 4)

    qc, kc, vc = chunks(q), chunks(k) * (dh ** -0.5), chunks(v)
    ic = log_i.astype(jnp.float32).reshape(bsz, nc, CHUNK, nh).transpose(0, 3, 1, 2)
    fc = log_f.astype(jnp.float32).reshape(bsz, nc, CHUNK, nh).transpose(0, 3, 1, 2)
    bcum = jnp.cumsum(fc, axis=-1)
    causal = jnp.tril(jnp.ones((CHUNK, CHUNK), dtype=bool))
    dlog = jnp.where(causal, bcum[..., :, None] - bcum[..., None, :] + ic[..., None, :], -jnp.inf)
    g = bcum[..., -1:] - bcum + ic
    m_loc = jnp.max(g, axis=-1)
    w_loc = jnp.exp(g - m_loc[..., None])
    c_loc = jnp.einsum('bhcs,bhcsk,bhcsv->bhckv', w_loc, kc, vc)
    n_loc = jnp.einsum('bhcs,bhcsk->bhck', w_loc, kc)
    f_tot = bcum[..., -1]

    def step(carry, inp):
        cm, nm, mm = carry
        cl, nl, ml, ft = inp
        m_new = jnp.maximum(ft + mm, ml)
        wa = jnp.exp(ft + mm - m_new)
        wb = jnp.exp(ml - m_new)
        c_new = wa[..., None, None] * cm + wb[..., None, None] * cl
        n_new = wa[..., None] * nm + wb[..., None] * nl
        return (c_new, n_new, m_new), (cm, nm, mm)

    init = (c0.astype(jnp.float32), n0.astype(jnp.float32), m0.astype(jnp.float32))
    (c_f, n_f, m_f), (c_p, n_p, m_p) = lax.scan(
        step, init, (c_loc.transpose(2, 0, 1, 3, 4), n_loc.transpose(2, 0, 1, 3),
                     m_loc.transpose(2, 0, 1), f_tot.transpose(2, 0, 1)))
    c_p = c_p.transpose(1, 2, 0, 3, 4)
    n_p = n_p.transpose(1, 2, 0, 3)
    m_p = m_p.transpose(1, 2, 0)
    inter = bcum + m_p[..., None]
    m_t = jnp.maximum(inter, jnp.max(dlog, axis=-1))
    s = jnp.einsum('bhcld,bhcsd->bhcls', qc, kc) * jnp.exp(dlog - m_t[..., None])
    w_int = jnp.exp(inter - m_t)
    num = jnp.einsum('bhcls,bhcsd->bhcld', s, vc) + w_int[..., None] * jnp.einsum('bhcld,bhcdv->bhclv', qc, c_p)
    den = jnp.sum(s, axis=-1) + w_int * jnp.einsum('bhcld,bhcd->bhcl', qc, n_p)
    h = num / jnp.maximum(jnp.abs(den), jnp.exp(-m_t))[..., None]
    h = h.transpose(0, 2, 3, 1, 4).reshape(bsz, n, nh, dh)
    return h, (c_f, n_f, m_f)

def peer_ffn(h, w_q, keys1, keys2, u_tab, v_tab):
    bsz, n, d = h.shape
    tok = h.reshape(-1, PEER_BLOCK, d)

    def block(xb):
        q = (xb @ w_q).reshape(PEER_BLOCK, PEER_HEADS, 2, PEER_KEY_DIM // 2).astype(jnp.float32)
        s1 = jnp.einsum('thd,nd->thn', q[:, :, 0], keys1.astype(jnp.float32))
        s2 = jnp.einsum('thd,nd->thn', q[:, :, 1], keys2.astype(jnp.float32))
        v1, i1 = lax.top_k(s1, PEER_TOPK)
        v2, i2 = lax.top_k(s2, PEER_TOPK)
        cand = (v1[..., :, None] + v2[..., None, :]).reshape(PEER_BLOCK, PEER_HEADS, PEER_TOPK * PEER_TOPK)
        sc, ci = lax.top_k(cand, PEER_TOPK)
        e = (jnp.take_along_axis(i1, ci // PEER_TOPK, axis=-1) * PEER_N_KEYS
             + jnp.take_along_axis(i2, ci % PEER_TOPK, axis=-1))
        gate = jax.nn.softmax(sc, axis=-1)
        act = jax.nn.gelu(jnp.einsum('thkd,td->thk', u_tab[e], xb), approximate=False)
        return jnp.einsum('thk,thkd->td', gate * act, v_tab[e])

    return lax.map(block, tok).reshape(bsz, n, d)

def trunk_layer(x, mod, on_grid, ssd_h0, mlstm_c0, mlstm_n0, mlstm_m0, lp):
    bsz, n, _ = x.shape
    sh_a, sc_a, gt_a, sh_f, sc_f, gt_f = jnp.split(mod[:, None, :], N_MOD, axis=-1)
    h = rms_norm(x, lp['g_mix_pre']) * (1.0 + sc_a) + sh_a
    proj = h @ lp['w_in']
    z, xbc, dt_raw, q, k, v, o, gate_raw, merge_raw = jnp.split(
        proj, np.cumsum(IN_SPLITS)[:-1].tolist(), axis=-1)
    if on_grid:
        rows = n // GRID_W
        xbc = dwconv_centred(xbc.reshape(bsz, rows, GRID_W, CONV_CH), lp['conv_w'], lp['conv_b']).reshape(bsz, n, CONV_CH)
    else:
        xbc = dwconv_centred(xbc, lp['conv_w'], lp['conv_b'])
    xbc = jax.nn.silu(xbc)
    xs, bs, cs = jnp.split(xbc, [SSD_WIDTH, SSD_WIDTH + SSD_GROUPS * SSD_STATE], axis=-1)
    xs = xs.reshape(bsz, n, SSD_HEADS, SSD_HEAD_DIM)
    bs = bs.reshape(bsz, n, SSD_GROUPS, SSD_STATE)
    cs = cs.reshape(bsz, n, SSD_GROUPS, SSD_STATE)
    dt = jax.nn.softplus(dt_raw.reshape(bsz, n, 2, SSD_HEADS).astype(jnp.float32) + lp['ssd_dt_bias'].astype(jnp.float32))
    a = -jnp.exp(lp['ssd_a_log'].astype(jnp.float32))
    y_f, ssd_f = ssd_scan(xs, dt[:, :, 0], a[0], bs, cs, ssd_h0[:, 0])
    y_b, ssd_b = ssd_scan(flip(xs), flip(dt[:, :, 1]), a[1], flip(bs), flip(cs), ssd_h0[:, 1])
    y = y_f + flip(y_b) + (lp['ssd_d'][0] + lp['ssd_d'][1])[:, None] * xs
    y = rms_norm(y.reshape(bsz, n, SSD_WIDTH) * jax.nn.silu(z), lp['ssd_norm_g'])
    y_ssd = y @ lp['w_ssd_out']
    q = q.reshape(bsz, n, MLSTM_HEADS, MLSTM_HEAD_DIM)
    k = k.reshape(bsz, n, MLSTM_HEADS, MLSTM_HEAD_DIM)
    v = v.reshape(bsz, n, MLSTM_HEADS, MLSTM_HEAD_DIM)
    g = gate_raw.reshape(bsz, n, 2, 2, MLSTM_HEADS).astype(jnp.float32)
    log_i = g[:, :, :, 0] + lp['mlstm_i_bias']
    log_f = jax.nn.log_sigmoid(g[:, :, :, 1] + lp['mlstm_f_bias'])
    hm_f, (cf, nf, mf) = mlstm_scan(q, k, v, log_i[:, :, 0], log_f[:, :, 0],
                                    mlstm_c0[:, 0], mlstm_n0[:, 0], mlstm_m0[:, 0])
    hm_b, (cb, nb, mb) = mlstm_scan(flip(q), flip(k), flip(v), flip(log_i[:, :, 1]), flip(log_f[:, :, 1]),
                                    mlstm_c0[:, 1], mlstm_n0[:, 1], mlstm_m0[:, 1])
    hm = rms_norm(hm_f + flip(hm_b), lp['mlstm_norm_g'].reshape(MLSTM_HEADS, MLSTM_HEAD_DIM))
    hm = hm.reshape(bsz, n, MLSTM_WIDTH) * jax.nn.sigmoid(o)
    y_ml = hm @ lp['w_mlstm_out']
    gate_ssd, gate_ml = jnp.split(jax.nn.sigmoid(merge_raw), N_BRANCH, axis=-1)
    mixed = (gate_ssd * y_ssd + gate_ml * y_ml) @ lp['w_out']
    x1 = x + gt_a * rms_norm(mixed, lp['g_mix_post'])
    h2 = rms_norm(x1, lp['g_ffn_pre']) * (1.0 + sc_f) + sh_f
    f = peer_ffn(h2, lp['peer_w_q'], lp['peer_keys1'], lp['peer_keys2'], lp['peer_u'], lp['peer_v'])
    x2 = x1 + gt_f * rms_norm(f, lp['g_ffn_post'])
    return (x2.astype(x.dtype), jnp.stack([ssd_f, ssd_b], axis=1), jnp.stack([cf, cb], axis=1),
            jnp.stack([nf, nb], axis=1), jnp.stack([mf, mb], axis=1))

def setup_inputs(seed: int = 0) -> dict:
    key = jax.random.key(seed)
    ks = jax.random.split(key, 40)

    def nrm(k, shape, scale):
        return jax.random.normal(k, shape, jnp.float32) * scale

    def gain(k, shape):
        return 1.0 + nrm(k, shape, 0.02)

    dt0 = jnp.exp(jax.random.uniform(ks[18], (DEPTH, 2, SSD_HEADS), jnp.float32, np.log(1e-3), np.log(1e-1)))
    return {
        'x_prompt': nrm(ks[0], (BATCH, SEQ, D_MODEL), 1.0),
        'x_sample': nrm(ks[1], (DEC_BATCH, DEC_SEQ, D_MODEL), 1.0),
        'c': nrm(ks[2], (DEC_BATCH, D_MODEL), 1.0),
        'state_ssd': nrm(ks[3], (DEC_BATCH, DEPTH, 2, SSD_HEADS, SSD_HEAD_DIM, SSD_STATE), 0.1),
        'state_mlstm_c': nrm(ks[4], (DEC_BATCH, DEPTH, 2, MLSTM_HEADS, MLSTM_HEAD_DIM, MLSTM_HEAD_DIM), 0.1),
        'state_mlstm_n': nrm(ks[5], (DEC_BATCH, DEPTH, 2, MLSTM_HEADS, MLSTM_HEAD_DIM), 0.1),
        'state_mlstm_m': nrm(ks[6], (DEC_BATCH, DEPTH, 2, MLSTM_HEADS), 1.0),
        'c_ctx': nrm(ks[7], (D_MODEL,), 1.0),
        'w_mod': nrm(ks[8], (DEPTH, D_MODEL, N_MOD * D_MODEL), 0.5 * D_MODEL ** -0.5),
        'b_mod': nrm(ks[9], (DEPTH, N_MOD * D_MODEL), 0.02),
        'g_mix_pre': gain(ks[10], (DEPTH, D_MODEL)),
        'g_mix_post': gain(ks[11], (DEPTH, D_MODEL)),
        'g_ffn_pre': gain(ks[12], (DEPTH, D_MODEL)),
        'g_ffn_post': gain(ks[13], (DEPTH, D_MODEL)),
        'w_in': nrm(ks[14], (DEPTH, D_MODEL, IN_COLS), D_MODEL ** -0.5),
        'conv_w': nrm(ks[15], (DEPTH, CONV_K, CONV_CH), CONV_K ** -0.5),
        'conv_b': nrm(ks[16], (DEPTH, CONV_CH), 0.02),
        'ssd_a_log': jnp.log(jax.random.uniform(ks[17], (DEPTH, 2, SSD_HEADS), jnp.float32, 1.0, 16.0)),
        'ssd_dt_bias': dt0 + jnp.log(-jnp.expm1(-dt0)),
        'ssd_d': 1.0 + nrm(ks[19], (DEPTH, 2, SSD_HEADS), 0.1),
        'ssd_norm_g': gain(ks[20], (DEPTH, SSD_WIDTH)),
        'w_ssd_out': nrm(ks[21], (DEPTH, SSD_WIDTH, D_MODEL), SSD_WIDTH ** -0.5),
        'mlstm_i_bias': nrm(ks[22], (DEPTH, 2, MLSTM_HEADS), 0.1),
        'mlstm_f_bias': jnp.linspace(3.0, 6.0, MLSTM_HEADS, dtype=jnp.float32) + nrm(ks[23], (DEPTH, 2, MLSTM_HEADS), 0.1),
        'mlstm_norm_g': gain(ks[24], (DEPTH, MLSTM_WIDTH)),
        'w_mlstm_out': nrm(ks[25], (DEPTH, MLSTM_WIDTH, D_MODEL), MLSTM_WIDTH ** -0.5),
        'w_out': nrm(ks[26], (DEPTH, D_MODEL, D_MODEL), D_MODEL ** -0.5),
        'peer_w_q': nrm(ks[27], (DEPTH, D_MODEL, PEER_HEADS * PEER_KEY_DIM), D_MODEL ** -0.5),
        'peer_keys1': nrm(ks[28], (DEPTH, PEER_N_KEYS, PEER_KEY_DIM // 2), (PEER_KEY_DIM // 2) ** -0.5),
        'peer_keys2': nrm(ks[29], (DEPTH, PEER_N_KEYS, PEER_KEY_DIM // 2), (PEER_KEY_DIM // 2) ** -0.5),
        'peer_u': nrm(ks[30], (DEPTH, PEER_EXPERTS, D_MODEL), D_MODEL ** -0.5),
        'peer_v': nrm(ks[31], (DEPTH, PEER_EXPERTS, D_MODEL), PEER_HEADS ** -0.5),
    }

def reference(x_prompt, x_sample, c, state_ssd, state_mlstm_c, state_mlstm_n, state_mlstm_m, c_ctx,
              w_mod, b_mod, g_mix_pre, g_mix_post, g_ffn_pre, g_ffn_post, w_in, conv_w, conv_b,
              ssd_a_log, ssd_dt_bias, ssd_d, ssd_norm_g, w_ssd_out, mlstm_i_bias, mlstm_f_bias,
              mlstm_norm_g, w_mlstm_out, w_out, peer_w_q, peer_keys1, peer_keys2, peer_u, peer_v):
    bp = x_prompt.shape[0]
    yp = x_prompt
    ys = x_sample
    out_ssd, out_c, out_n, out_m = [], [], [], []
    for l in range(DEPTH):
        lp = {
            'g_mix_pre': g_mix_pre[l], 'g_mix_post': g_mix_post[l],
            'g_ffn_pre': g_ffn_pre[l], 'g_ffn_post': g_ffn_post[l],
            'w_in': w_in[l], 'conv_w': conv_w[l], 'conv_b': conv_b[l],
            'ssd_a_log': ssd_a_log[l], 'ssd_dt_bias': ssd_dt_bias[l], 'ssd_d': ssd_d[l],
            'ssd_norm_g': ssd_norm_g[l], 'w_ssd_out': w_ssd_out[l],
            'mlstm_i_bias': mlstm_i_bias[l], 'mlstm_f_bias': mlstm_f_bias[l],
            'mlstm_norm_g': mlstm_norm_g[l], 'w_mlstm_out': w_mlstm_out[l], 'w_out': w_out[l],
            'peer_w_q': peer_w_q[l], 'peer_keys1': peer_keys1[l], 'peer_keys2': peer_keys2[l],
            'peer_u': peer_u[l], 'peer_v': peer_v[l],
        }
        mod_ctx = jnp.broadcast_to(adaln(c_ctx, w_mod[l], b_mod[l])[None, :], (bp, N_MOD * D_MODEL))
        ssd0 = jnp.zeros((bp, 2, SSD_HEADS, SSD_HEAD_DIM, SSD_STATE), jnp.float32)
        c0 = jnp.zeros((bp, 2, MLSTM_HEADS, MLSTM_HEAD_DIM, MLSTM_HEAD_DIM), jnp.float32)
        n0 = jnp.zeros((bp, 2, MLSTM_HEADS, MLSTM_HEAD_DIM), jnp.float32)
        m0 = jnp.zeros((bp, 2, MLSTM_HEADS), jnp.float32)
        yp, s_ssd, s_c, s_n, s_m = trunk_layer(yp, mod_ctx, False, ssd0, c0, n0, m0, lp)
        out_ssd.append(s_ssd)
        out_c.append(s_c)
        out_n.append(s_n)
        out_m.append(s_m)
        mod_lat = adaln(c, w_mod[l], b_mod[l])
        ys, _, _, _, _ = trunk_layer(ys, mod_lat, True, state_ssd[:, l], state_mlstm_c[:, l],
                                     state_mlstm_n[:, l], state_mlstm_m[:, l], lp)
    new_state_ssd = jnp.stack(out_ssd, axis=1)
    new_state_mlstm_c = jnp.stack(out_c, axis=1)
    new_state_mlstm_n = jnp.stack(out_n, axis=1)
    new_state_mlstm_m = jnp.stack(out_m, axis=1)
    return (yp, ys, new_state_ssd, new_state_mlstm_c, new_state_mlstm_n, new_state_mlstm_m)


_drawn_inputs = setup_inputs


def setup_inputs(seed=0):
    import zlib

    import numpy as np

    out = dict(_drawn_inputs(seed))
    spreads = {}
    factors = {'g_ffn_post': 8.0, 'mlstm_norm_g': 3.079}
    for name, (base, spread) in spreads.items():
        noise = np.random.default_rng([zlib.crc32(name.encode()), seed]).standard_normal(out[name].shape)
        drawn = base * np.exp(spread * noise) if base else spread * noise
        out[name] = __import__('jax').numpy.asarray(drawn.astype(out[name].dtype))
    for name, factor in factors.items():
        out[name] = (out[name] * factor).astype(out[name].dtype)
    return out
```

```python
from contextlib import ExitStack

import concourse.bass as bass
from concourse import mybir

P = 128
D = 1024
KT = D // P
BLOCKS = 5
CHUNKS = BLOCKS - 1
TOK = BLOCKS * P
LAT = CHUNKS * P
GRID_W = 64
EPS = 1e-6
HS, PS, NG = 16, 64, 4
HM, DM = 4, 256
CE = DM + 1
HP, TOPK = 8, 16
SLOTS = HP * TOPK
NEG = -1.0e30

ALU = mybir.AluOpType
ACT = mybir.ActivationFunctionType
AX = mybir.AxisListType.X
F32 = mybir.dt.float32
U32 = mybir.dt.uint32

COL_Z, COL_V, COL_O, COL_M, COLS_T = 0, D, 2 * D, 3 * D, 5 * D
G_DA, G_LI, G_NACS, G_EA, G_WD, G_ED, G_E, G_DT, G_BC, G_TOT, G_LF = 0, 32, 40, 72, 104, 136, 168, 176, 208, 216, 224
G_N = 232
R_ALOG, R_DTB, R_SKIP, R_IB, R_FB, R_M0 = 0, 32, 64, 96, 104, 112
R_N = 120
V_SCALE_A, V_SHIFT_A, V_GATE_A, V_SCALE_F, V_SHIFT_F, V_GATE_F = range(6)


def bc_last(ap, n):
    shape = list(ap.shape) + [n]
    return ap.unsqueeze(len(ap.shape)).to_broadcast(shape)


def semaphores(nc, ctx, prefix=""):
    taken = []

    def sem(name):
        taken.append(nc.alloc_semaphore(prefix + name))
        return taken[-1]

    def give_back():
        nc.clear_and_free_semaphores(taken)
        nc.all_engine_barrier()

    ctx.callback(give_back)
    return sem


def row(ap):
    return ap.rearrange("o p f -> p (o f)")


def constants(nc, t):
    with ExitStack() as ctx:
        ready = semaphores(nc, ctx)("const_step")
        block = ctx.enter_context(nc.Block())

        @block.gpsimd
        def _(pool):
            nc.gpsimd.memset(t["ones"][:, :], 1.0).then_inc(ready, 1)
            nc.gpsimd.iota(t["iota_i"][:, :], [[1, TOPK]], base=0, channel_multiplier=0).then_inc(ready, 1)
            pool.wait_ge(ready, 2)
            nc.gpsimd.affine_select(out=t["triF"][:, :], in_=t["ones"][:, :], pattern=[[1, P]], compare_op=ALU.is_ge,
                                    fill=0.0, base=0, channel_multiplier=-1).then_inc(ready, 1)
            nc.gpsimd.affine_select(out=t["triB"][:, :], in_=t["ones"][:, :], pattern=[[-1, P]], compare_op=ALU.is_ge,
                                    fill=0.0, base=0, channel_multiplier=1).then_inc(ready, 1)
            nc.gpsimd.affine_select(out=t["ident"][:, :], in_=t["ones"][:, :], pattern=[[-1, P]], compare_op=ALU.is_equal,
                                    fill=0.0, base=0, channel_multiplier=1).then_inc(ready, 1)
            nc.gpsimd.tensor_copy(t["iota"][:, :], t["iota_i"][:, :]).then_inc(ready, 1)
            pool.wait_ge(ready, 6)
            nc.gpsimd.tensor_scalar(t["maskF"][:, :], t["triF"][:, :], 1.0, -NEG, ALU.subtract, ALU.mult).then_inc(ready, 1)
            nc.gpsimd.tensor_scalar(t["maskB"][:, :], t["triB"][:, :], 1.0, -NEG, ALU.subtract, ALU.mult).then_inc(ready, 1)


def modulation(nc, dr, t):
    NCH = 6 * D // 512
    with ExitStack() as ctx:
        sb = lambda n, s, d=F32: ctx.enter_context(nc.sbuf_tensor(n, s, d))
        sem = semaphores(nc, ctx)
        cv = sb("cv", [P, KT, 2])
        sig = sb("cv_sig", [P, KT, 2])
        wm = sb("wm", [P, 4, KT, 512])
        bm = sb("bm", [P, 6, KT])
        raw = sb("mod_raw", [P, 6, KT, 2])
        vt = sb("mod_t", [96, P])
        ps = ctx.enter_context(nc.psum_tensor("mod_ps", [P, 48, 2], F32))
        pt = ctx.enter_context(nc.psum_tensor("mod_pt", [96, P], F32))
        small_in, w_in = sem("mod_small_in"), [sem(f"mod_w{i}") for i in range(4)]
        sig_ready, silu_ready, chunk_done = sem("sig_ready"), sem("silu_ready"), sem("mod_chunk_done")
        vecs_ready, turned, turned_sb, rows_out = sem("vecs_ready"), sem("vecs_turned"), sem("vecs_rows"), sem("rows_out")
        block = ctx.enter_context(nc.Block())

        @block.sync
        def _(sp):
            sp.dma_start(cv[:, :, :], dr["cvT"]).then_inc(small_in, 16)
            sp.dma_start(bm[:, :, :], dr["b_modT"]).then_inc(small_in, 16)
            sp.dma_start(t["gains"][:, :, :], dr["gains"]).then_inc(small_in, 16)
            sp.dma_start(t["rows"][:, :], dr["small_rows"].partition_broadcast(P)).then_inc(small_in, 16)
            for n in range(NCH):
                if n >= 4:
                    sp.wait_ge(chunk_done, n - 3)
                sp.dma_start(wm[:, n % 4], dr["w_mod"][n]).then_inc(w_in[n % 4], 16)
            sp.wait_ge(turned_sb, 1)
            for b in range(BLOCKS):
                c = 0 if b == 0 else 1
                sp.dma_start(dr["mod_rows"][b].rearrange("o (r p) -> (o r) p", p=P),
                             vt[48 * c:48 * c + 48, :]).then_inc(rows_out, 16)
            sp.wait_ge(rows_out, 16 * BLOCKS)

        @block.scalar
        def _(act):
            act.wait_ge(small_in, 64)
            nc.scalar.activation(sig[:, :, :], cv[:, :, :], ACT.Sigmoid).then_inc(sig_ready, 1)
            act.wait_ge(turned, 1)
            nc.scalar.copy(vt[:, :], pt[:, :]).then_inc(turned_sb, 1)

        @block.tensor
        def _(pe):
            pe.wait_ge(silu_ready, 1)
            for n in range(NCH):
                pe.wait_ge(w_in[n % 4], 16 * (n // 4 + 1))
                for m in range(4):
                    for k in range(KT):
                        last = nc.tensor.matmul(ps[:, 4 * n + m, :], wm[:, n % 4, k, m * P:(m + 1) * P], cv[:, k, :],
                                                start=(k == 0), stop=(k == KT - 1))
                last.then_inc(chunk_done, 1)
            pe.wait_ge(vecs_ready, 1)
            nc.tensor.transpose(pt[:, :], t["vecs"][:, :, :, :].rearrange("p c v k -> p (c v k)"),
                                t["ident"][:, :]).then_inc(turned, 1)

        @block.vector
        def _(dve):
            dve.wait_ge(sig_ready, 1)
            nc.vector.tensor_tensor(cv[:, :, :], cv[:, :, :], sig[:, :, :], ALU.mult).then_inc(silu_ready, 1)
            dve.wait_ge(chunk_done, NCH)
            nc.vector.tensor_tensor(raw[:, :, :, :].rearrange("p v k c -> p (v k) c"), ps[:, :, :],
                                    bc_last(bm[:, :, :].rearrange("p v k -> p (v k)"), 2), ALU.add)
            dve.drain()
            g = t["gains"]
            for c in range(2):
                r, o = raw[:, :, :, c], t["vecs"][:, c]
                nc.vector.tensor_copy(o[:, V_SHIFT_A, :], r[:, 0, :])
                nc.vector.scalar_tensor_tensor(o[:, V_SCALE_A, :], r[:, 1, :], 1.0, g[:, 0, :], ALU.add, ALU.mult)
                nc.vector.tensor_tensor(o[:, V_GATE_A, :], r[:, 2, :], g[:, 1, :], ALU.mult)
                nc.vector.tensor_copy(o[:, V_SHIFT_F, :], r[:, 3, :])
                nc.vector.scalar_tensor_tensor(o[:, V_SCALE_F, :], r[:, 4, :], 1.0, g[:, 2, :], ALU.add, ALU.mult)
                last = nc.vector.tensor_tensor(o[:, V_GATE_F, :], r[:, 5, :], g[:, 3, :], ALU.mult)
            dve.drain()
            nc.vector.engine_nop().then_inc(vecs_ready, 1)


def normalise(nc, dr, t, hT):
    with ExitStack() as ctx:
        sb = lambda n, s, d=F32: ctx.enter_context(nc.sbuf_tensor(n, s, d))
        sem = semaphores(nc, ctx)
        x = sb("x", [P, BLOCKS, D])
        sq = sb("x_sq", [P, D])
        ss = sb("x_ss", [P, BLOCKS])
        rstd = sb("x_rstd", [P, BLOCKS])
        ps = [ctx.enter_context(nc.psum_tensor(f"turn{i}", [P, 4, P], F32)) for i in range(4)]
        x_in = [sem(f"x_in{b}") for b in range(BLOCKS)]
        ms_ready, root_ready, scaled, turned, moved = sem("ms_ready"), sem("root_ready"), sem("x_scaled"), sem("x_turned"), sem("h_moved")
        sums_ready = sem("sums_ready")
        block = ctx.enter_context(nc.Block())

        @block.sync
        def _(sp):
            for b in range(BLOCKS):
                sp.dma_start(x[:, b, :], dr["x"][b]).then_inc(x_in[b], 16)

        @block.scalar
        def _(act):
            for b in range(BLOCKS):
                act.wait_ge(x_in[b], 16)
                nc.scalar.activation(sq[:, :], x[:, b, :], ACT.Square, accum_out=ss[:, b:b + 1])
                act.drain()
            nc.scalar.copy(rstd[:, :], ss[:, :]).then_inc(sums_ready, 1)
            act.wait_ge(ms_ready, 1)
            nc.scalar.activation(rstd[:, :], ss[:, :], ACT.Sqrt).then_inc(root_ready, 1)
            for n in range(2 * BLOCKS):
                b, half = n // 2, n % 2
                act.wait_ge(turned, n + 1)
                c = 0 if b == 0 else 1
                for i in range(4):
                    k = 4 * half + i
                    last = nc.scalar.activation(hT[:, k, b * P:(b + 1) * P], ps[n % 4][:, i, :], ACT.Identity,
                                                scale=t["vecs"][:, c, V_SCALE_A, k:k + 1],
                                                bias=t["vecs"][:, c, V_SHIFT_A, k:k + 1])
                last.then_inc(moved, 1)

        @block.vector
        def _(dve):
            dve.wait_ge(sums_ready, 1)
            nc.vector.tensor_scalar(ss[:, :], ss[:, :], 1.0 / D, EPS, ALU.mult, ALU.add).then_inc(ms_ready, 1)
            dve.wait_ge(root_ready, 1)
            nc.vector.reciprocal(ss[:, :], rstd[:, :])
            dve.drain()
            for b in range(BLOCKS):
                nc.vector.tensor_scalar(x[:, b, :], x[:, b, :], ss[:, b:b + 1], None, ALU.mult).then_inc(scaled, 1)

        @block.tensor
        def _(pe):
            for n in range(2 * BLOCKS):
                b, half = n // 2, n % 2
                pe.wait_ge(scaled, b + 1)
                if n >= 4:
                    pe.wait_ge(moved, n - 3)
                for i in range(4):
                    k = 4 * half + i
                    last = nc.tensor.transpose(ps[n % 4][:, i, :], x[:, b, k * P:(k + 1) * P], t["ident"][:, :])
                last.then_inc(turned, 1)


def project(nc, dr, t, hT):
    T_CH, X_CH, Q_CH = COLS_T // 512, 4, 4
    with ExitStack() as ctx:
        sb = lambda n, s, d=F32: ctx.enter_context(nc.sbuf_tensor(n, s, d))
        sem = semaphores(nc, ctx)
        w = sb("w_chunk", [P, 2, KT, 512])
        ws = sb("w_small", [P, KT, 48])
        out = sb("chunk_out", [P, 2, BLOCKS, 512])
        cw = sb("conv_par", [P, 4, 16])
        cc = sb("conv_cur", [P, 4, 8])
        acc = sb("conv_acc", [P, 2, TOK])
        big = sb("tile_out", [P, 2, 4, TOK])
        pst = [ctx.enter_context(nc.psum_tensor(f"pj{i}", [P, 1024], F32)) for i in range(4)]
        banks = [pst[i // 2][:, (i % 2) * 512:(i % 2) * 512 + 512] for i in range(5)]
        w_in = [sem("w_in0"), sem("w_in1")]
        par_in, small_mm, small_moved = sem("par_in"), sem("small_mm"), sem("small_moved")
        t_mm, x_mm, q_mm = sem("t_mm"), sem("x_mm"), sem("q_mm")
        t_bank_free, x_tile_free, q_tile_free, acc_free = sem("t_bank_free"), sem("x_tile_free"), sem("q_tile_free"), sem("acc_free")
        acc_ready, x_act, par_ready = sem("acc_ready"), sem("x_act"), sem("par_ready")
        t_out, x_out, q_out = [[sem(f"{n}_out{j}") for j in range(2)] for n in "txq"]
        block = ctx.enter_context(nc.Block())

        def w_src(c):
            return dr["w_big"][bass.ds(c, 1)].rearrange("o p k n -> p (o k) n")

        @block.sync
        def _(sp):
            sp.dma_start(ws[:, :, :], dr["w_small"]).then_inc(par_in, 16)
            sp.dma_start(cw[:, :, :], dr["convT"]).then_inc(par_in, 16)
            for j in range(2):
                sp.dma_start(w[:, j], dr["w_big"][j]).then_inc(w_in[j], 16)
            with sp.Fori(0, T_CH // 2) as i:
                for j in range(2):
                    sp.wait_ge(t_mm, i * (2 * BLOCKS) + (j + 1) * BLOCKS)
                    sp.dma_start(w[:, j], w_src(i * 2 + (j + 2))).then_inc(w_in[j], 16)
            with sp.Fori(0, X_CH // 2) as i:
                for j in range(2):
                    sp.wait_ge(x_mm, i * 8 + 4 * (j + 1))
                    sp.dma_start(w[:, j], w_src(i * 2 + (j + 2 + T_CH))).then_inc(w_in[j], 16)
            for j in range(2):
                sp.wait_ge(q_mm, 4 * (j + 1))
                sp.dma_start(w[:, j], dr["w_big"][T_CH + X_CH + 2 + j]).then_inc(w_in[j], 16)

        @block.gpsimd
        def _(pool):
            with pool.Fori(0, T_CH // 2) as i:
                for j in range(2):
                    pool.wait_ge(t_bank_free, i * (2 * BLOCKS) + (5 + (j + 1) * BLOCKS))
                    pool.wait_ge(small_moved, 1)
                    pool.dma_start(dr["proj"].rearrange("b p n -> p b n")[:, :, bass.ds((i * 2 + j) * 512, 512)],
                                   out[:, j]).then_inc(t_out[j], 16)
            with pool.Fori(0, X_CH // 2) as i:
                for j in range(2):
                    pool.wait_ge(x_act, i * 8 + 4 * (j + 1))
                    pool.wait_ge(small_moved, 1)
                    pool.dma_start(dr["xbcT"].rearrange("m p t -> p m t")[:, bass.ds(i * 8 + 4 * j, 4)], big[:, j]).then_inc(x_out[j], 16)
            with pool.Fori(0, Q_CH // 2) as i:
                for j in range(2):
                    pool.wait_ge(q_tile_free, i * 8 + (4 + 4 * (j + 1)))
                    pool.wait_ge(small_moved, 1)
                    pool.dma_start(dr["qkT"].rearrange("m p t -> p m t")[:, bass.ds(i * 8 + 4 * j, 4)], big[:, j]).then_inc(q_out[j], 16)
            for j in range(2):
                pool.wait_ge(t_out[j], 16 * (T_CH // 2))
                pool.wait_ge(x_out[j], 16 * (X_CH // 2))
                pool.wait_ge(q_out[j], 16 * (Q_CH // 2))

        @block.tensor
        def _(pe):
            pe.wait_ge(par_in, 32)
            for b in range(BLOCKS):
                for k in range(KT):
                    last = nc.tensor.matmul(banks[0][:, b * 48:(b + 1) * 48], hT[:, k, b * P:(b + 1) * P], ws[:, k, :],
                                            start=(k == 0), stop=(k == KT - 1))
            last.then_inc(small_mm, 1)
            pe.wait_ge(small_moved, 1)
            with pe.Fori(0, T_CH // 2) as i:
                for j in range(2):
                    pe.wait_ge(w_in[j], i * 16 + 16)
                    for b in range(BLOCKS):
                        pe.wait_ge(t_bank_free, i * (2 * BLOCKS) + (j * BLOCKS + b + 1))
                        for k in range(KT):
                            last = nc.tensor.matmul(banks[b], hT[:, k, b * P:(b + 1) * P], w[:, j, k, :],
                                                    start=(k == 0), stop=(k == KT - 1))
                        last.then_inc(t_mm, 1)
            pe.wait_ge(t_bank_free, 5 + T_CH * BLOCKS)

            def channel_tiles(i, done_pairs, tile_free, done):
                for j in range(2):
                    pe.wait_ge(w_in[j], i * 16 + 16 * (done_pairs + 1))
                    for m in range(4):
                        pe.wait_ge(tile_free, i * 8 + (4 * j + m + 1))
                        for k in range(KT):
                            nc.tensor.matmul(pst[m][:, 0:LAT], w[:, j, k, m * P:(m + 1) * P], hT[:, k, P:TOK],
                                             start=(k == 0), stop=(k == KT - 1))
                        for k in range(KT):
                            last = nc.tensor.matmul(pst[m][:, LAT:TOK], w[:, j, k, m * P:(m + 1) * P], hT[:, k, 0:P],
                                                    start=(k == 0), stop=(k == KT - 1))
                        last.then_inc(done, 1)

            with pe.Fori(0, X_CH // 2) as i:
                channel_tiles(i, T_CH // 2, x_tile_free, x_mm)
            pe.wait_ge(x_tile_free, 4 + 4 * X_CH)
            with pe.Fori(0, Q_CH // 2) as i:
                channel_tiles(i, (T_CH + X_CH) // 2, q_tile_free, q_mm)

        @block.scalar
        def _(act):
            act.sem_inc(t_bank_free, 5)
            act.sem_inc(q_tile_free, 4)
            act.wait_ge(small_mm, 1)
            nc.scalar.copy(t["small"][:, :, :].rearrange("p b n -> p (b n)"), banks[0][:, 0:48 * BLOCKS]).then_inc(small_moved, 1)
            with act.Fori(0, T_CH // 2) as i:
                for j in range(2):
                    act.wait_ge(t_out[j], i * 16)
                    for b in range(BLOCKS):
                        act.wait_ge(t_mm, i * (2 * BLOCKS) + (j * BLOCKS + b + 1))
                        nc.scalar.copy(out[:, j, b, :], banks[b]).then_inc(t_bank_free, 1)
            with act.Fori(0, X_CH // 2) as i:
                for j in range(2):
                    act.wait_ge(x_out[j], i * 16)
                    for m in range(4):
                        act.wait_ge(acc_ready, i * 8 + (4 * j + m + 1))
                        nc.scalar.activation(big[:, j, m, P:TOK], acc[:, m % 2, 0:LAT], ACT.Silu)
                        nc.scalar.activation(big[:, j, m, 0:P], acc[:, m % 2, LAT:TOK], ACT.Silu).then_inc(x_act, 1)
            for j in range(2):
                act.wait_ge(x_out[j], 16 * (X_CH // 2))
            with act.Fori(0, Q_CH // 2) as i:
                for j in range(2):
                    act.wait_ge(q_out[j], i * 16)
                    for m in range(4):
                        act.wait_ge(q_mm, i * 8 + (4 * j + m + 1))
                        nc.scalar.copy(big[:, j, m, P:TOK], pst[m][:, 0:LAT])
                        nc.scalar.copy(big[:, j, m, 0:P], pst[m][:, LAT:TOK]).then_inc(q_tile_free, 1)

        @block.vector
        def _(dve):
            dve.sem_inc(x_tile_free, 4)
            dve.wait_ge(par_in, 32)
            with dve.Fori(0, X_CH // 2) as i:
                nc.vector.tensor_copy(cc[:, :, :], cw[:, :, bass.ds(i * 8, 8)])
                dve.drain()
                for n in range(8):
                    m = n % 4
                    dve.wait_ge(x_mm, i * 8 + (n + 1))
                    if n >= 2:
                        dve.wait_ge(x_act, i * 8 + (n - 1))
                    else:
                        dve.wait_ge(x_act, i * 8)
                    lat = acc[:, n % 2, 0:LAT]
                    pro = acc[:, n % 2, LAT:TOK]
                    nc.vector.tensor_scalar(acc[:, n % 2, :], pst[m][:, 0:TOK], cc[:, 1, n:n + 1], cc[:, 3, n:n + 1],
                                            ALU.mult, ALU.add)
                    dve.drain()
                    grid = lat.rearrange("p (r g) -> p r g", g=GRID_W)
                    u = pst[m][:, 0:LAT].rearrange("p (r g) -> p r g", g=GRID_W)
                    nc.vector.scalar_tensor_tensor(grid[:, :, 1:], u[:, :, 0:GRID_W - 1], cc[:, 0, n:n + 1],
                                                   grid[:, :, 1:], ALU.mult, ALU.add)
                    nc.vector.scalar_tensor_tensor(pro[:, 1:], pst[m][:, LAT:TOK - 1], cc[:, 0, n:n + 1],
                                                   pro[:, 1:], ALU.mult, ALU.add)
                    dve.drain()
                    nc.vector.scalar_tensor_tensor(grid[:, :, 0:GRID_W - 1], u[:, :, 1:], cc[:, 2, n:n + 1],
                                                   grid[:, :, 0:GRID_W - 1], ALU.mult, ALU.add)
                    nc.vector.scalar_tensor_tensor(pro[:, 0:P - 1], pst[m][:, LAT + 1:TOK], cc[:, 2, n:n + 1],
                                                   pro[:, 0:P - 1], ALU.mult, ALU.add).then_inc(acc_ready, 1)
                    dve.wait_ge(acc_ready, i * 8 + (n + 1))
                    dve.sem_inc(x_tile_free, 1)


def gates(nc, dr, t):
    NS = 2 * HS
    NM = 2 * HM
    with ExitStack() as ctx:
        sb = lambda n, s, d=F32: ctx.enter_context(nc.sbuf_tensor(n, s, d))
        sem = semaphores(nc, ctx)
        W = NS + NM
        raw = sb("gt_raw", [P, BLOCKS, W])
        nabs = sb("gt_nabs", [P, BLOCKS, W])
        y = sb("gt_y", [P, BLOCKS, W])
        u = sb("gt_u", [P, BLOCKS, W])
        lnu = sb("gt_ln", [P, BLOCKS, W])
        a = sb("gt_a", [P, NS])
        fb = sb("gt_fb", [P, NM])
        tmp = sb("gt_tmp", [P, BLOCKS, NS])
        tm2 = sb("gt_tm2", [P, BLOCKS, NS])
        ps = ctx.enter_context(nc.psum_tensor("gt_ps", [P, BLOCKS, NS], F32))
        pt = ctx.enter_context(nc.psum_tensor("gt_pt", [P, BLOCKS, NS], F32))
        pm = ctx.enter_context(nc.psum_tensor("gt_pm", [P, 2, BLOCKS, NM], F32))
        args_ready, exps_ready, ones_added, logs_ready, steps_ready, sums_ready, lists_ready, done = (
            sem("gt_args"), sem("gt_exps"), sem("gt_ones"), sem("gt_logs"), sem("gt_steps"), sem("gt_sums"), sem("gt_lists"), sem("gt_done"))
        block = ctx.enter_context(nc.Block())
        G, sm, rows = t["gates"], t["small"], t["rows"]

        def per_block(ap):
            return ap.unsqueeze(1).to_broadcast([P, BLOCKS, ap.shape[1]])

        @block.vector
        def _(dve):
            nc.vector.tensor_tensor(raw[:, :, 0:NS], sm[:, :, 0:NS], per_block(rows[:, R_DTB:R_DTB + NS]), ALU.add)
            nc.vector.tensor_scalar(fb[:, :], rows[:, R_FB:R_FB + NM], -1.0, None, ALU.mult)
            dve.drain()
            nc.vector.scalar_tensor_tensor(raw[:, :, NS:W], sm[:, :, NS + NM:NS + 2 * NM], -1.0, per_block(fb[:, :]),
                                           ALU.mult, ALU.add)
            nc.vector.tensor_tensor(G[:, :, G_LI:G_LI + NM], sm[:, :, NS:NS + NM], per_block(rows[:, R_IB:R_IB + NM]), ALU.add)
            dve.drain()
            nc.vector.tensor_scalar(u[:, :, :], raw[:, :, :], -1.0, None, ALU.mult)
            dve.drain()
            nc.vector.tensor_tensor(nabs[:, :, :], u[:, :, :], raw[:, :, :], ALU.min).then_inc(args_ready, 1)
            dve.wait_ge(exps_ready, 1)
            nc.vector.tensor_scalar(u[:, :, :], y[:, :, :], 1.0, None, ALU.add).then_inc(ones_added, 1)
            dve.wait_ge(ones_added, 1)
            nc.vector.tensor_scalar(nabs[:, :, :], u[:, :, :], 1.0, None, ALU.subtract)
            dve.drain()
            nc.vector.tensor_tensor(nabs[:, :, :], y[:, :, :], nabs[:, :, :], ALU.subtract)
            dve.drain()
            dve.wait_ge(logs_ready, 1)
            nc.vector.reciprocal(y[:, :, :], u[:, :, :])
            dve.drain()
            nc.vector.tensor_tensor(nabs[:, :, :], nabs[:, :, :], y[:, :, :], ALU.mult)
            dve.drain()
            nc.vector.tensor_tensor(nabs[:, :, :], nabs[:, :, :], lnu[:, :, :], ALU.add)
            dve.drain()
            nc.vector.scalar_tensor_tensor(nabs[:, :, :], raw[:, :, :], 0.0, nabs[:, :, :], ALU.max, ALU.add)
            dve.drain()
            nc.vector.tensor_copy(G[:, :, G_DT:G_DT + NS], nabs[:, :, 0:NS])
            nc.vector.tensor_scalar(G[:, :, G_LF:G_LF + NM], nabs[:, :, NS:W], -1.0, None, ALU.mult)
            nc.vector.scalar_tensor_tensor(G[:, :, G_DA:G_DA + NS], nabs[:, :, 0:NS], -1.0, per_block(a[:, :]),
                                           ALU.mult, ALU.mult)
            dve.drain()
            dve.sem_inc(steps_ready, 1)
            dve.wait_ge(sums_ready, 1)
            nc.vector.tensor_copy(tmp[:, :, :], ps[:, :, :])
            nc.vector.tensor_scalar(G[:, :, G_NACS:G_NACS + NS], ps[:, :, :], -1.0, None, ALU.mult)
            nc.vector.tensor_copy(G[:, :, G_BC:G_BC + NM], pm[:, 0])
            nc.vector.tensor_copy(G[:, :, G_TOT:G_TOT + NM], pm[:, 1])
            dve.drain()
            nc.vector.tensor_tensor(tm2[:, :, :], pt[:, :, :], tmp[:, :, :], ALU.subtract)
            nc.vector.tensor_tensor(G[:, :, G_E:G_E + NM], G[:, :, G_LI:G_LI + NM], G[:, :, G_BC:G_BC + NM], ALU.subtract)
            dve.drain()
            dve.sem_inc(lists_ready, 1)
            dve.wait_ge(done, 1)
            nc.vector.tensor_tensor(G[:, :, G_WD:G_WD + NS], G[:, :, G_WD:G_WD + NS], G[:, :, G_DT:G_DT + NS], ALU.mult)

        @block.scalar
        def _(act):
            nc.scalar.activation(a[:, :], rows[:, R_ALOG:R_ALOG + NS], ACT.Exp)
            act.wait_ge(args_ready, 1)
            nc.scalar.activation(y[:, :, :], nabs[:, :, :], ACT.Exp).then_inc(exps_ready, 1)
            act.wait_ge(ones_added, 1)
            nc.scalar.activation(lnu[:, :, :], u[:, :, :], ACT.Ln).then_inc(logs_ready, 1)
            act.wait_ge(lists_ready, 1)
            nc.scalar.activation(G[:, :, G_EA:G_EA + NS], tmp[:, :, :], ACT.Exp)
            nc.scalar.activation(G[:, :, G_ED:G_ED + NS], pt[:, :, :], ACT.Exp)
            nc.scalar.activation(G[:, :, G_WD:G_WD + NS], tm2[:, :, :], ACT.Exp).then_inc(done, 1)

        @block.tensor
        def _(pe):
            pe.wait_ge(steps_ready, 1)
            for d, tri in enumerate((t["triF"], t["triB"])):
                for b in range(BLOCKS):
                    c = d * HS
                    nc.tensor.matmul(ps[:, b, c:c + HS], tri[:, :], G[:, b, G_DA + c:G_DA + c + HS], start=True, stop=True)
                    m = d * HM
                    nc.tensor.matmul(pm[:, 0, b, m:m + HM], tri[:, :], G[:, b, G_LF + m:G_LF + m + HM], start=True, stop=True)
            for b in range(BLOCKS):
                nc.tensor.matmul(pt[:, b, :], t["ones"][:, :], G[:, b, G_DA:G_DA + NS], start=True, stop=True)
                last = nc.tensor.matmul(pm[:, 1, b, :], t["ones"][:, :], G[:, b, G_LF:G_LF + NM], start=True, stop=True)
            last.then_inc(sums_ready, 1)


def scan(nc, dr, t, kind):
    full = kind != "back"
    dirs = (0, 1) if full else (1,)
    steps = {"prompt": (0, 1), "back": (1,), "sample": (0,)}[kind]
    prior = kind != "prompt"
    N = {"prompt": 1, "back": CHUNKS - 1, "sample": CHUNKS}[kind]
    tri, mask_t, mask = (t["triF"], t["triB"]), (t["maskF"], t["maskB"]), (t["maskB"], t["maskF"])
    with ExitStack() as ctx:
        pre = kind[0] + "_"
        sb = lambda n, s, d=F32: ctx.enter_context(nc.sbuf_tensor(pre + n, s, d))
        sem = semaphores(nc, ctx, pre)

        xbcT, qkT, v, g = sb("xbcT", [P, 16, P]), sb("qkT", [P, 16, P]), sb("v", [P, D]), sb("g", [P, G_N])
        xs, Bt, Kt = sb("xs", [P, D]), sb("Bt", [P, NG, P]), sb("Kt", [P, HM, DM])
        L, W = sb("L", [P, 2, 2, 4, P]), sb("W", [P, 2, 2, 4, P])
        y, yt, xw = sb("y", [P, D]), sb("yt", [P, D]), sb("xw", [P, 2, D])
        H = [sb(f"H{d}", [P, D]) for d in range(2)]
        C = [sb(f"C{d}", [P, HM, 2, CE]) for d in range(2)]
        mp, emax, me, mx, nmx, mn, rs, den, r, rw = [sb(n, [P, 2, HM]) for n in (
            "mp", "emax", "me", "mx", "nmx", "mn", "rs", "den", "r", "rw")]
        args, ex = sb("args", [P, 4, 2, HM]), sb("ex", [P, 4, 2, HM])
        WA, WI, DN, KW = range(4)
        Em, Pc, PcT = sb("Em", [P, 2, HM, P]), sb("Pc", [P, HM, P]), sb("PcT", [P, HM, P])
        hm, Ks = sb("hm", [P, HM, DM]), sb("Ks", [P, 2, HM, DM])
        bank = [ctx.enter_context(nc.psum_tensor(f"{pre}bank{i}", [P, 1024], F32)) for i in range(4)]
        half = [bank[i // 2][:, (i % 2) * 512:(i % 2) * 512 + 512] for i in range(8)]
        loaded, cur_ready, init_ready = sem("loaded"), sem("cur_ready"), sem("init_ready")
        xs_turned, B_turned, xs_ready, B_ready, K_turned, K_ready = (
            sem("xs_turned"), sem("B_turned"), sem("xs_ready"), sem("B_ready"), sem("K_turned"), sem("K_ready"))
        xw_ready, state_mm, H_new = sem("xw_ready"), [sem("state_mm0"), sem("state_mm1")], [sem("H_new0"), sem("H_new1")]
        E_rows, E_used, args_ready, ex_ready, Ks_ready = sem("E_rows"), sem("E_used"), sem("args_ready"), sem("ex_ready"), sem("Ks_ready")
        mstate_mm, C_new = sem("mstate_mm"), sem("C_new")
        chunk_done, stored = sem("chunk_done"), sem("stored")
        sp_passed, dve_passed = sem("sp_passed"), sem("dve_passed")
        if full:
            scores, decay, decays, W_ready, y_mm, y_done = (
                sem("scores"), sem("decay"), sem("decays"), sem("W_ready"), sem("y_mm"), sem("y_done"))
            yoff_mm, yoff_used = [sem("yoff_mm0"), sem("yoff_mm1")], [sem("yoff_used0"), sem("yoff_used1")]
            qk_mm, X_ready, P_done, inter_mm, inter_used, P_turned, PT_ready, hv_mm, hm_done, P_mixed, qn_used = (
                sem("qk_mm"), sem("X_ready"), sem("P_done"), sem("inter_mm"), sem("inter_used"), sem("P_turned"), sem("PT_ready"),
                sem("hv_mm"), sem("hm_done"), sem("P_mixed"), sem("qn_used"))
        block = ctx.enter_context(nc.Block())
        NM = len(steps) * HM
        LOADS = {"prompt": 3, "back": 3, "sample": 6}[kind]
        STORES = {"prompt": 2, "back": 3, "sample": 2}[kind]

        def loop(eng, body):
            if N == 1:
                body(0)
            else:
                with eng.Fori(0, N) as i:
                    body(i)

        def blk(i):
            return {"prompt": i, "back": CHUNKS - i, "sample": i + 1}[kind]

        def at(ap, i):
            return ap[i] if isinstance(i, int) else row(ap[bass.ds(i, 1)])

        @block.sync
        def _(sp):
            if kind == "back":
                sp.dma_start(H[1][:, :], dr["state_ssd"][1]).then_inc(loaded, 16)
                sp.dma_start(C[1][:, :, :, :].rearrange("p h k c -> p (h k c)"), dr["state_c"][1]).then_inc(loaded, 16)
            if kind == "sample":
                sp.dma_start(H[0][:, :], dr["state_ssd"][0]).then_inc(loaded, 16)
                sp.dma_start(C[0][:, :, :, :].rearrange("p h k c -> p (h k c)"), dr["state_c"][0]).then_inc(loaded, 16)
            INIT = 32 if prior else 0

            def body(i):
                col = blk(i) * P if kind == "prompt" else sp.snap(blk(i) * P)
                sp.wait_ge(chunk_done, i)
                sp.sem_inc(sp_passed, 1)
                tok = slice(0, P) if kind == "prompt" else bass.ds(col, P)
                sp.dma_start(xbcT[:, :, :], dr["xbcT"].rearrange("m p t -> p m t")[:, :, tok]).then_inc(loaded, 16)
                sp.dma_start(qkT[:, :, :], dr["qkT"].rearrange("m p t -> p m t")[:, :, tok]).then_inc(loaded, 16)
                sp.dma_start(v[:, :], at(dr["proj"], blk(i))[:, COL_V:COL_V + D]).then_inc(loaded, 16)
                if kind == "sample":
                    sp.dma_start(H[1][:, :], at(dr["back_ssd"], CHUNKS - 1 - i)).then_inc(loaded, 16)
                    sp.dma_start(C[1][:, :, :, :].rearrange("p h k c -> p (h k c)"),
                                 at(dr["back_c"], CHUNKS - 1 - i)).then_inc(loaded, 16)
                    sp.dma_start(mp[:, 1, :], at(dr["back_m"], CHUNKS - 1 - i)).then_inc(loaded, 16)
                if full:
                    sp.wait_ge(y_done, i + 1)
                    sp.sem_inc(sp_passed, 1)
                    sp.dma_start(at(dr["y_ssd"], blk(i)), y[:, :]).then_inc(stored, 16)
                    sp.wait_ge(hm_done, i + 1)
                    sp.sem_inc(sp_passed, 1)
                    sp.dma_start(at(dr["y_mlstm"], blk(i)), hm[:, :, :].rearrange("p h c -> p (h c)")).then_inc(stored, 16)
                    sp.wait_ge(stored, i * (16 * STORES) + 16 * STORES)
                    sp.sem_inc(sp_passed, 1)
                else:
                    sp.wait_ge(chunk_done, i + 1)
                    sp.sem_inc(sp_passed, 1)
                    sp.dma_start(at(dr["back_ssd"], i + 1), H[1][:, :]).then_inc(stored, 16)
                    sp.dma_start(at(dr["back_c"], i + 1), C[1][:, :, :, :].rearrange("p h k c -> p (h k c)")).then_inc(stored, 16)
                    sp.dma_start(at(dr["back_m"], i + 1), mp[:, 1, :]).then_inc(stored, 16)
                    sp.wait_ge(stored, i * (16 * STORES) + (16 * STORES + 48))
                    sp.sem_inc(sp_passed, 1)

            if kind == "back":
                sp.wait_ge(loaded, INIT)
                sp.wait_ge(init_ready, 1)
                sp.dma_start(dr["back_ssd"][0], H[1][:, :]).then_inc(stored, 16)
                sp.dma_start(dr["back_c"][0], C[1][:, :, :, :].rearrange("p h k c -> p (h k c)")).then_inc(stored, 16)
                sp.dma_start(dr["back_m"][0], mp[:, 1, :]).then_inc(stored, 16)
                sp.wait_ge(stored, 48)
            loop(sp, body)
            if kind == "prompt":
                sp.wait_ge(chunk_done, 1)
                for d in range(2):
                    sp.dma_start(dr["out_ssd"][d], H[d][:, :]).then_inc(stored, 16)
                    sp.dma_start(dr["out_c"][d], C[d][:, :, :, :].rearrange("p h k c -> p (h k c)")).then_inc(stored, 16)
                sp.dma_start(dr["out_m"], mp[0:1, :, :].rearrange("p d h -> p (d h)")).then_inc(stored, 16)
                sp.wait_ge(stored, 32 + 80)

        LOAD0 = 32 if prior else 0

        @block.tensor
        def _(pe):
            ident = t["ident"]

            def body(i):
                pe.wait_ge(loaded, i * (16 * LOADS) + (LOAD0 + 16 * LOADS))
                pe.wait_ge(cur_ready, i + 1)
                if prior:
                    pe.wait_ge(init_ready, 1)
                pe.wait_ge(chunk_done, i)
                for k in range(KT):
                    last = nc.tensor.transpose(bank[0][:, k * P:(k + 1) * P], xbcT[:, k, :], ident[:, :])
                last.then_inc(xs_turned, 1)
                for k in range(NG):
                    last = nc.tensor.transpose(half[2][:, k * P:(k + 1) * P], xbcT[:, KT + k, :], ident[:, :])
                last.then_inc(B_turned, 1)
                if full:
                    for q in range(NG):
                        last = nc.tensor.matmul(half[3][:, q * P:(q + 1) * P], xbcT[:, KT + q, :], xbcT[:, KT + NG + q, :],
                                                start=True, stop=True)
                    last.then_inc(scores, 1)

                    def decay_rows(q):
                        if q:
                            pe.wait_ge(decays, i * NG + q)
                        for d in range(2):
                            out = half[4 + d].rearrange("p (h s) -> p h s", h=4)
                            nc.tensor.matmul(out, ident[:, :], mask_t[d][:, :].unsqueeze(1).to_broadcast([P, 4, P]),
                                             start=True, stop=False)
                            for h in range(4):
                                c = d * HS + q * 4 + h
                                last = nc.tensor.matmul(out[:, h, :], g[:, G_NACS + c:G_NACS + c + 1].to_broadcast([P, P]),
                                                        t["nident"][:, :], start=False, stop=(h == 3))
                        last.then_inc(decay, 1)

                    decay_rows(0)
                    pe.wait_ge(xs_ready, i + 1)
                    for q in range(NG):
                        if q + 1 < NG:
                            decay_rows(q + 1)
                        pe.wait_ge(W_ready, i * NG + (q + 1))
                        for h in range(4):
                            c = (q * 4 + h) * PS
                            for d in range(2):
                                last = nc.tensor.matmul(bank[3][:, c:c + PS], W[:, q % 2, d, h, :], xs[:, c:c + PS],
                                                        start=(d == 0), stop=(d == 1))
                        last.then_inc(y_mm, 1)
                    if prior:
                        for d in range(2):
                            for q in range(NG):
                                last = nc.tensor.matmul(bank[d][:, q * 256:(q + 1) * 256], xbcT[:, KT + NG + q, :],
                                                        H[d][:, q * 256:(q + 1) * 256], start=True, stop=True)
                            last.then_inc(yoff_mm[d], 1)
                pe.wait_ge(B_ready, i + 1)
                pe.wait_ge(xw_ready, i + 1)
                for n, d in enumerate(steps):
                    if n == 0 and full:
                        pe.wait_ge(decays, i * NG + NG)
                    if n == 1:
                        pe.wait_ge(xs_ready, i + 1)
                        if full and prior:
                            pe.wait_ge(yoff_used[0], i + 1)
                    to = bank[(2, 0)[n]]
                    for q in range(NG):
                        last = nc.tensor.matmul(to[:, q * 256:(q + 1) * 256], Bt[:, q, :], xw[:, d, q * 256:(q + 1) * 256],
                                                start=True, stop=True)
                    last.then_inc(state_mm[d], 1)
                if full and prior:
                    pe.wait_ge(yoff_used[1], i + 1)
                if full:
                    pe.wait_ge(W_ready, i * NG + NG)
                for k in range(KT):
                    last = nc.tensor.transpose(bank[1][:, k * P:(k + 1) * P], qkT[:, KT + k, :], ident[:, :])
                last.then_inc(K_turned, 1)
                pe.wait_ge(H_new[steps[0]], i + 1)
                for d in dirs:
                    for h in range(HM):
                        c = G_E + d * HM + h
                        last = nc.tensor.matmul(half[4 + d][:, h * P:(h + 1) * P], g[:, c:c + 1].to_broadcast([P, P]), ident[:, :],
                                                start=True, stop=True)
                last.then_inc(E_rows, 1)
                if full:
                    pe.wait_ge(y_done, i + 1)
                    for h in range(HM):
                        for k in range(2):
                            last = nc.tensor.matmul(half[6][:, h * P:(h + 1) * P], qkT[:, 2 * h + k, :], qkT[:, KT + 2 * h + k, :],
                                                    start=(k == 0), stop=(k == 1))
                    last.then_inc(qk_mm, 1)
                    if prior:
                        if len(steps) == 2:
                            pe.wait_ge(H_new[steps[1]], i + 1)
                        pe.wait_ge(K_ready, i + 1)
                        for d in range(2):
                            for h in range(HM):
                                for k in range(2):
                                    nc.tensor.matmul(bank[d][:, h * DM:(h + 1) * DM], qkT[:, 2 * h + k, :], C[d][:, h, k, 0:DM],
                                                     start=(k == 0), stop=(k == 1))
                                for k in range(2):
                                    last = nc.tensor.matmul(half[7][:, d * HM + h:d * HM + h + 1], qkT[:, 2 * h + k, :],
                                                            C[d][:, h, k, DM:CE], start=(k == 0), stop=(k == 1))
                        last.then_inc(inter_mm, 1)
                    pe.wait_ge(P_mixed, i + 1)
                    for h in range(HM):
                        last = nc.tensor.transpose(half[4][:, h * P:(h + 1) * P], Pc[:, h, :], ident[:, :])
                    last.then_inc(P_turned, 1)
                    pe.wait_ge(PT_ready, i + 1)
                    for h in range(HM):
                        last = nc.tensor.matmul(bank[3][:, h * DM:(h + 1) * DM], PcT[:, h, :], v[:, h * DM:(h + 1) * DM],
                                                start=True, stop=True)
                    last.then_inc(hv_mm, 1)
                    if prior:
                        pe.wait_ge(inter_used, i + 1)
                pe.wait_ge(Ks_ready, i + 1)
                if kind == "prompt":
                    pe.wait_ge(H_new[1], i + 1)
                for n in range(NM):
                    d, h = steps[n // HM], n % HM
                    for k in range(2):
                        nc.tensor.matmul(half[5][:, 2 * n + k:2 * n + k + 1], Ks[:, d, h, k * P:(k + 1) * P],
                                         t["ones"][:, 0:1], start=True, stop=True)
                for n in range(NM):
                    d, h = steps[n // HM], n % HM
                    if n >= 4:
                        pe.wait_ge(C_new, i * NM + (n - 3))
                    for k in range(2):
                        last = nc.tensor.matmul(half[n % 4][:, k * DM:(k + 1) * DM], Ks[:, d, h, k * P:(k + 1) * P],
                                                v[:, h * DM:(h + 1) * DM], start=True, stop=True)
                    last.then_inc(mstate_mm, 1)

            loop(pe, body)

        @block.scalar
        def _(act):
            def body(i):
                act.wait_ge(xs_turned, i + 1)
                nc.scalar.copy(xs[:, :], bank[0][:, :]).then_inc(xs_ready, 1)
                act.wait_ge(B_turned, i + 1)
                nc.scalar.copy(Bt[:, :, :].rearrange("p q n -> p (q n)"), half[2]).then_inc(B_ready, 1)
                if full:
                    for q in range(NG):
                        act.wait_ge(decay, i * NG + (q + 1))
                        if q >= 2:
                            act.wait_ge(W_ready, i * NG + (q - 1))
                        for d in range(2):
                            for h in range(4):
                                c = G_NACS + d * HS + q * 4 + h
                                last = nc.scalar.activation(L[:, q % 2, d, h, :], half[4 + d][:, h * P:(h + 1) * P], ACT.Exp,
                                                            bias=g[:, c:c + 1])
                        last.then_inc(decays, 1)
                act.wait_ge(K_turned, i + 1)
                nc.scalar.copy(Kt[:, :, :].rearrange("p h c -> p (h c)"), bank[1][:, :]).then_inc(K_ready, 1)
                act.wait_ge(args_ready, i + 1)
                nc.scalar.activation(ex[:, :, :, :], args[:, :, :, :], ACT.Exp).then_inc(ex_ready, 1)
                if full:
                    for d in range(2):
                        for h in range(HM):
                            last = nc.scalar.activation(Em[:, d, h, :], Em[:, d, h, :], ACT.Exp, bias=nmx[:, d, h:h + 1])
                    last.then_inc(X_ready, 1)
                    act.wait_ge(P_turned, i + 1)
                    nc.scalar.copy(PcT[:, :, :].rearrange("p h s -> p (h s)"), half[4]).then_inc(PT_ready, 1)

            loop(act, body)

        @block.vector
        def _(dve):
            if kind == "back":
                nc.vector.tensor_copy(mp[:, 1, :], t["rows"][:, R_M0 + HM:R_M0 + 2 * HM])
            elif kind == "sample":
                nc.vector.tensor_copy(mp[:, 0, :], t["rows"][:, R_M0:R_M0 + HM])
            else:
                nc.vector.memset(mp[:, :, :], 0.0)
            nc.vector.memset(args[:, :, :, :], 0.0)
            dve.drain()
            dve.sem_inc(init_ready, 1)
            sd = slice(dirs[0], dirs[-1] + 1)

            def heads(ap):
                return ap.rearrange("p (h c) -> p h c", c=PS)

            def body(i):
                b = i if kind == "prompt" else dve.snap(blk(i))
                dve.wait_ge(loaded, i * (16 * LOADS) + (LOAD0 + 16 * LOADS))
                if kind == "back":
                    dve.wait_ge(stored, i * (16 * STORES) + 48)
                else:
                    dve.wait_ge(stored, i * (16 * STORES))
                dve.sem_inc(dve_passed, 1)
                G = t["gates"]
                nc.vector.tensor_copy(g[:, :], G[:, 0, :] if kind == "prompt" else G[:, bass.ds(b, 1), :].rearrange(
                    "p o n -> p (o n)"))
                dve.drain()
                dve.sem_inc(cur_ready, 1)
                dve.wait_ge(xs_ready, i + 1)
                for d in steps:
                    c = G_WD + d * HS
                    nc.vector.tensor_tensor(heads(xw[:, d, :]), heads(xs[:, :]), bc_last(g[:, c:c + HS], PS), ALU.mult)
                dve.drain()
                dve.sem_inc(xw_ready, 1)
                if full:
                    for q in range(NG):
                        dve.wait_ge(decays, i * NG + (q + 1))
                        dve.wait_ge(scores, i + 1)
                        if q >= 2:
                            dve.wait_ge(y_mm, i * NG + (q - 1))
                        for d in range(2):
                            for h in range(4):
                                c = G_DT + d * HS + q * 4 + h
                                last = nc.vector.scalar_tensor_tensor(W[:, q % 2, d, h, :], L[:, q % 2, d, h, :], g[:, c:c + 1],
                                                                      half[3][:, q * P:(q + 1) * P], ALU.mult, ALU.mult)
                        last.then_inc(W_ready, 1)
                    nc.vector.tensor_tensor(heads(yt[:, :]), heads(xs[:, :]), bc_last(t["skip"][:, :], PS), ALU.mult)
                    dve.drain()
                    dve.wait_ge(y_mm, i * NG + NG)
                    nc.vector.tensor_tensor(y[:, :], yt[:, :], bank[3][:, :], ALU.add)
                    if prior:
                        for d in range(2):
                            dve.drain()
                            dve.wait_ge(yoff_mm[d], i + 1)
                            c = G_EA + d * HS
                            nc.vector.tensor_tensor(heads(yt[:, :]), heads(bank[d][:, :]), bc_last(g[:, c:c + HS], PS),
                                                    ALU.mult).then_inc(yoff_used[d], 1)
                            dve.drain()
                            nc.vector.tensor_tensor(y[:, :], y[:, :], yt[:, :], ALU.add)
                    dve.drain()
                    dve.sem_inc(y_done, 1)
                for n, d in enumerate(steps):
                    c = G_ED + d * HS
                    dve.wait_ge(state_mm[d], i + 1)
                    if prior:
                        nc.vector.tensor_tensor(heads(H[d][:, :]), heads(H[d][:, :]), bc_last(g[:, c:c + HS], PS), ALU.mult)
                        dve.drain()
                        nc.vector.tensor_tensor(H[d][:, :], H[d][:, :], bank[(2, 0)[n]][:, :], ALU.add).then_inc(H_new[d], 1)
                    else:
                        nc.vector.tensor_copy(H[d][:, :], bank[(2, 0)[n]][:, :]).then_inc(H_new[d], 1)
                dve.wait_ge(E_rows, i + 1)
                for d in dirs:
                    E = half[4 + d].rearrange("p (h s) -> p h s", h=HM)
                    nc.vector.tensor_reduce(emax[:, d, :], E, AX, ALU.max)
                    if full:
                        nc.vector.tensor_tensor(Em[:, d, :, :], E, mask[d][:, :].unsqueeze(1).to_broadcast([P, HM, P]), ALU.add)
                        dve.drain()
                        nc.vector.tensor_reduce(me[:, d, :], Em[:, d, :, :], AX, ALU.max)
                dve.drain()
                nc.vector.tensor_tensor(mn[:, sd, :], mp[:, sd, :], emax[:, sd, :], ALU.max)
                if full:
                    nc.vector.tensor_tensor(mx[:, :, :], mp[:, :, :], me[:, :, :], ALU.max)
                dve.drain()
                gd = lambda c: g[:, c:c + 2 * HM].rearrange("p (d h) -> p d h", d=2)[:, sd, :]
                nc.vector.tensor_tensor(args[:, WA, sd, :], mp[:, sd, :], mn[:, sd, :], ALU.subtract)
                nc.vector.tensor_tensor(args[:, KW, sd, :], gd(G_E), mn[:, sd, :], ALU.subtract)
                if full:
                    nc.vector.tensor_scalar(nmx[:, :, :], mx[:, :, :], -1.0, None, ALU.mult)
                    nc.vector.tensor_tensor(args[:, WI, :, :], mp[:, :, :], mx[:, :, :], ALU.subtract)
                    dve.drain()
                    nc.vector.tensor_tensor(args[:, DN, :, :], nmx[:, :, :], gd(G_BC), ALU.subtract)
                dve.drain()
                nc.vector.tensor_tensor(mp[:, sd, :], mn[:, sd, :], gd(G_TOT), ALU.add)
                dve.drain()
                dve.sem_inc(args_ready, 1)
                dve.wait_ge(ex_ready, i + 1)
                dve.wait_ge(K_ready, i + 1)
                for d in steps:
                    nc.vector.scalar_tensor_tensor(Ks[:, d], Kt[:, :, :], DM ** -0.5, bc_last(ex[:, KW, d, :], DM), ALU.mult, ALU.mult)
                dve.drain()
                dve.sem_inc(Ks_ready, 1)
                if full:
                    dve.wait_ge(qk_mm, i + 1)
                    dve.wait_ge(X_ready, i + 1)
                    for d in range(2):
                        for h in range(HM):
                            nc.vector.scalar_tensor_tensor(Em[:, d, h, :], half[6][:, h * P:(h + 1) * P], DM ** -0.5, Em[:, d, h, :],
                                                           ALU.mult, ALU.mult, accum_out=rs[:, d, h:h + 1])
                    dve.drain()
                    if prior:
                        dve.wait_ge(inter_mm, i + 1)
                        nc.vector.tensor_tensor(den[:, :, :], half[7][:, 0:2 * HM].rearrange("p (d h) -> p d h", d=2),
                                                ex[:, WI, :, :], ALU.mult)
                        dve.drain()
                        nc.vector.tensor_tensor(rs[:, :, :], rs[:, :, :], den[:, :, :], ALU.add)
                        dve.drain()
                    nc.vector.scalar_tensor_tensor(den[:, :, :], rs[:, :, :], -1.0, rs[:, :, :], ALU.mult, ALU.max)
                    dve.drain()
                    nc.vector.tensor_tensor(den[:, :, :], den[:, :, :], ex[:, DN, :, :], ALU.max)
                    dve.drain()
                    nc.vector.reciprocal(r[:, :, :], den[:, :, :])
                    dve.drain()
                    nc.vector.tensor_tensor(rw[:, :, :], r[:, :, :], ex[:, WI, :, :], ALU.mult)
                    for h in range(HM):
                        nc.vector.tensor_scalar(Pc[:, h, :], Em[:, 0, h, :], r[:, 0, h:h + 1], None, ALU.mult)
                    dve.drain()
                    for h in range(HM):
                        nc.vector.scalar_tensor_tensor(Pc[:, h, :], Em[:, 1, h, :], r[:, 1, h:h + 1], Pc[:, h, :], ALU.mult, ALU.add)
                    dve.drain()
                    dve.sem_inc(P_mixed, 1)
                    if prior:
                        for h in range(HM):
                            nc.vector.tensor_scalar(hm[:, h, :], bank[0][:, h * DM:(h + 1) * DM], rw[:, 0, h:h + 1], None, ALU.mult)
                        dve.drain()
                        for h in range(HM):
                            nc.vector.scalar_tensor_tensor(hm[:, h, :], bank[1][:, h * DM:(h + 1) * DM], rw[:, 1, h:h + 1],
                                                           hm[:, h, :], ALU.mult, ALU.add)
                        dve.drain()
                        dve.sem_inc(inter_used, 1)
                    dve.wait_ge(hv_mm, i + 1)
                    hv = bank[3][:, :].rearrange("p (h c) -> p h c", c=DM)
                    if prior:
                        nc.vector.tensor_tensor(hm[:, :, :], hm[:, :, :], hv, ALU.add).then_inc(hm_done, 1)
                    else:
                        nc.vector.tensor_copy(hm[:, :, :], hv).then_inc(hm_done, 1)
                for n in range(NM):
                    d, h = steps[n // HM], n % HM
                    dve.wait_ge(mstate_mm, i * NM + (n + 1))
                    new = half[n % 4].rearrange("p (k c) -> p k c", k=2)
                    norm = half[5][:, 2 * n:2 * n + 2].unsqueeze(2)
                    if prior:
                        nc.vector.scalar_tensor_tensor(C[d][:, h, :, 0:DM], C[d][:, h, :, 0:DM], ex[:, WA, d, h:h + 1], new,
                                                       ALU.mult, ALU.add)
                        nc.vector.scalar_tensor_tensor(C[d][:, h, :, DM:CE], C[d][:, h, :, DM:CE], ex[:, WA, d, h:h + 1], norm,
                                                       ALU.mult, ALU.add).then_inc(C_new, 1)
                    else:
                        nc.vector.tensor_copy(C[d][:, h, :, 0:DM], new)
                        nc.vector.tensor_copy(C[d][:, h, :, DM:CE], norm).then_inc(C_new, 1)
                dve.drain()
                dve.sem_inc(chunk_done, 1)

            loop(dve, body)


def skip_sum(nc, t):
    with nc.Block() as block:
        @block.vector
        def _(dve):
            r = t["rows"]
            nc.vector.tensor_tensor(t["skip"][:, :], r[:, R_SKIP:R_SKIP + HS], r[:, R_SKIP + HS:R_SKIP + 2 * HS], ALU.add)
            nc.vector.tensor_scalar(t["nident"][:, :], t["ident"][:, :], -1.0, None, ALU.mult)


def merge(nc, dr, t):
    with ExitStack() as ctx:
        sb = lambda n, s, d=F32: ctx.enter_context(nc.sbuf_tensor("m_" + n, s, d))
        sem = semaphores(nc, ctx, "m_")
        wts = sb("w", [P, 3, KT, D])
        y, z, hm, o, mg, x = sb("y", [P, D]), sb("z", [P, D]), sb("hm", [P, HM, DM]), sb("o", [P, HM, DM]), sb("mg", [P, 2, D]), sb("x", [P, D])
        rows = sb("rows", [P, 3, D])
        sz, sq = sb("sz", [P, D]), sb("sq", [P, D])
        yT, hT, mix = sb("yT", [P, KT, P]), sb("hT", [P, KT, P]), sb("mix", [P, D])
        ss, root, rr = sb("ss", [P, 7]), sb("root", [P, 7]), sb("rr", [P, 7])
        bank = [ctx.enter_context(nc.psum_tensor(f"m_bank{i}", [P, 1024], F32)) for i in range(4)]
        w_in, loaded, sig_ready, y_gated, ss_ready, ms_ready, root_ready, normed = (
            sem("w_in"), sem("loaded"), sem("sig_ready"), sem("y_gated"), sem("ss_ready"), sem("ms_ready"), sem("root_ready"), sem("normed"))
        turned, gained, branch_mm, mixed, mix_turned, mT_ready, out_mm = (
            sem("turned"), sem("gained"), sem("branch_mm"), sem("mixed"), sem("mix_turned"), sem("mT_ready"), sem("out_mm"))
        x1_ready, h2_ready, stored, passed = sem("x1_ready"), sem("h2_ready"), sem("stored"), sem("sp_passed")
        block = ctx.enter_context(nc.Block())
        NL, NR = 7, 3

        @block.sync
        def _(sp):
            for k in range(3):
                sp.dma_start(wts[:, k], dr["w_out3"][k]).then_inc(w_in, 16)
            with sp.Fori(0, BLOCKS) as i:
                b = sp.snap(i + 0)
                sp.wait_ge(stored, i * 32)
                sp.sem_inc(passed, 1)
                pr = row(dr["proj"][bass.ds(b, 1)])
                sp.dma_start(y[:, :], row(dr["y_ssd"][bass.ds(b, 1)])).then_inc(loaded, 16)
                sp.dma_start(z[:, :], pr[:, COL_Z:COL_Z + D]).then_inc(loaded, 16)
                sp.dma_start(hm[:, :, :].rearrange("p h c -> p (h c)"), row(dr["y_mlstm"][bass.ds(b, 1)])).then_inc(loaded, 16)
                sp.dma_start(o[:, :, :].rearrange("p h c -> p (h c)"), pr[:, COL_O:COL_O + D]).then_inc(loaded, 16)
                sp.dma_start(mg[:, :, :].rearrange("p h c -> p (h c)"), pr[:, COL_M:COL_M + 2 * D]).then_inc(loaded, 16)
                sp.dma_start(x[:, :], row(dr["x"][bass.ds(b, 1)])).then_inc(loaded, 16)
                r = row(dr["mod_rows"][bass.ds(b, 1)])[0:1, V_GATE_A * D:(V_SHIFT_F + 1) * D]
                sp.dma_start(rows[:, :, :].rearrange("p v c -> p (v c)"), r.partition_broadcast(P)).then_inc(loaded, 16)
                sp.wait_ge(x1_ready, i + 1)
                sp.sem_inc(passed, 1)
                sp.dma_start(row(dr["x1"][bass.ds(b, 1)]), x[:, :]).then_inc(stored, 16)
                sp.wait_ge(h2_ready, i + 1)
                sp.sem_inc(passed, 1)
                sp.dma_start(row(dr["h2"][bass.ds(b, 1)]), mix[:, :]).then_inc(stored, 16)
            sp.wait_ge(stored, BLOCKS * 32)

        @block.scalar
        def _(act):
            act.wait_ge(w_in, 48)
            with act.Fori(0, BLOCKS) as i:
                act.wait_ge(loaded, i * (16 * NL) + 16 * NL)
                nc.scalar.activation(sz[:, :], z[:, :], ACT.Sigmoid)
                nc.scalar.activation(o[:, :, :], o[:, :, :], ACT.Sigmoid)
                nc.scalar.activation(mg[:, :, :], mg[:, :, :], ACT.Sigmoid).then_inc(sig_ready, 1)
                for h in range(HM):
                    nc.scalar.activation(sq[:, h * DM:(h + 1) * DM], hm[:, h, :], ACT.Square, accum_out=ss[:, 1 + h:2 + h])
                act.drain()
                act.wait_ge(y_gated, i + 1)
                nc.scalar.activation(sq[:, :], y[:, :], ACT.Square, accum_out=ss[:, 0:1])
                act.drain()
                act.sem_inc(ss_ready, 1)
                act.wait_ge(ms_ready, i * NR + 1)
                nc.scalar.activation(root[:, 0:5], ss[:, 0:5], ACT.Sqrt).then_inc(root_ready, 1)
                act.wait_ge(mix_turned, i + 1)
                act.wait_ge(branch_mm, i + 1)
                nc.scalar.copy(yT[:, :, :].rearrange("p k t -> p (k t)"), bank[0][:, :]).then_inc(mT_ready, 1)
                act.wait_ge(out_mm, i + 1)
                nc.scalar.activation(sq[:, :], bank[1][:, :], ACT.Square, accum_out=ss[:, 5:6])
                act.drain()
                act.sem_inc(ss_ready, 1)
                act.wait_ge(ms_ready, i * NR + 2)
                nc.scalar.activation(root[:, 5:6], ss[:, 5:6], ACT.Sqrt).then_inc(root_ready, 1)
                act.wait_ge(x1_ready, i + 1)
                nc.scalar.activation(sq[:, :], x[:, :], ACT.Square, accum_out=ss[:, 6:7])
                act.drain()
                act.sem_inc(ss_ready, 1)
                act.wait_ge(ms_ready, i * NR + 3)
                nc.scalar.activation(root[:, 6:7], ss[:, 6:7], ACT.Sqrt).then_inc(root_ready, 1)

        @block.tensor
        def _(pe):
            pe.wait_ge(w_in, 48)
            with pe.Fori(0, BLOCKS) as i:
                pe.wait_ge(normed, i + 1)
                for k in range(KT):
                    nc.tensor.transpose(bank[0][:, k * P:(k + 1) * P], y[:, k * P:(k + 1) * P], t["ident"][:, :])
                flat = hm[:, :, :].rearrange("p h c -> p (h c)")
                for k in range(KT):
                    last = nc.tensor.transpose(bank[1][:, k * P:(k + 1) * P], flat[:, k * P:(k + 1) * P], t["ident"][:, :])
                last.then_inc(turned, 1)
                pe.wait_ge(gained, i + 1)
                for n, src in enumerate((yT, hT)):
                    for c in range(2):
                        for k in range(KT):
                            last = nc.tensor.matmul(bank[2 + n][:, c * 512:(c + 1) * 512], src[:, k, :],
                                                    wts[:, n, k, c * 512:(c + 1) * 512], start=(k == 0), stop=(k == KT - 1))
                last.then_inc(branch_mm, 1)
                pe.wait_ge(mixed, i + 1)
                for k in range(KT):
                    last = nc.tensor.transpose(bank[0][:, k * P:(k + 1) * P], mix[:, k * P:(k + 1) * P], t["ident"][:, :])
                last.then_inc(mix_turned, 1)
                pe.wait_ge(mT_ready, i + 1)
                for c in range(2):
                    for k in range(KT):
                        last = nc.tensor.matmul(bank[1][:, c * 512:(c + 1) * 512], yT[:, k, :],
                                                wts[:, 2, k, c * 512:(c + 1) * 512], start=(k == 0), stop=(k == KT - 1))
                last.then_inc(out_mm, 1)

        @block.vector
        def _(dve):
            def inverse_root(i, n, a, b, width):
                dve.wait_ge(ss_ready, i * NR + n)
                if n == 1:
                    nc.vector.tensor_scalar(ss[:, 0:1], ss[:, 0:1], 1.0 / D, EPS, ALU.mult, ALU.add)
                    nc.vector.tensor_scalar(ss[:, 1:5], ss[:, 1:5], 1.0 / DM, EPS, ALU.mult, ALU.add)
                else:
                    nc.vector.tensor_scalar(ss[:, a:b], ss[:, a:b], 1.0 / width, EPS, ALU.mult, ALU.add)
                dve.drain()
                dve.sem_inc(ms_ready, 1)
                dve.wait_ge(root_ready, i * NR + n)
                nc.vector.reciprocal(rr[:, a:b], root[:, a:b])
                dve.drain()

            with dve.Fori(0, BLOCKS) as i:
                dve.wait_ge(loaded, i * (16 * NL) + 16 * NL)
                nc.vector.tensor_tensor(y[:, :], y[:, :], z[:, :], ALU.mult)
                dve.drain()
                dve.wait_ge(sig_ready, i + 1)
                nc.vector.tensor_tensor(y[:, :], y[:, :], sz[:, :], ALU.mult).then_inc(y_gated, 1)
                inverse_root(i, 1, 0, 5, D)
                nc.vector.tensor_scalar(y[:, :], y[:, :], rr[:, 0:1], None, ALU.mult)
                for h in range(HM):
                    nc.vector.scalar_tensor_tensor(hm[:, h, :], hm[:, h, :], rr[:, 1 + h:2 + h], o[:, h, :], ALU.mult, ALU.mult)
                dve.drain()
                dve.sem_inc(normed, 1)
                dve.wait_ge(turned, i + 1)
                nc.vector.tensor_tensor(yT[:, :, :], bank[0][:, :].rearrange("p (k t) -> p k t", t=P), bc_last(t["gains"][:, 4, :], P), ALU.mult)
                nc.vector.tensor_tensor(hT[:, :, :], bank[1][:, :].rearrange("p (k t) -> p k t", t=P), bc_last(t["gains"][:, 5, :], P), ALU.mult)
                dve.drain()
                dve.sem_inc(gained, 1)
                dve.wait_ge(branch_mm, i + 1)
                dve.wait_ge(stored, i * 32)
                nc.vector.tensor_tensor(mix[:, :], mg[:, 0, :], bank[2][:, :], ALU.mult)
                nc.vector.tensor_tensor(mg[:, 1, :], mg[:, 1, :], bank[3][:, :], ALU.mult)
                dve.drain()
                nc.vector.tensor_tensor(mix[:, :], mix[:, :], mg[:, 1, :], ALU.add).then_inc(mixed, 1)
                inverse_root(i, 2, 5, 6, D)
                nc.vector.scalar_tensor_tensor(mg[:, 0, :], bank[1][:, :], rr[:, 5:6], rows[:, 0, :], ALU.mult, ALU.mult)
                dve.drain()
                nc.vector.tensor_tensor(x[:, :], x[:, :], mg[:, 0, :], ALU.add).then_inc(x1_ready, 1)
                inverse_root(i, 3, 6, 7, D)
                nc.vector.scalar_tensor_tensor(mix[:, :], x[:, :], rr[:, 6:7], rows[:, 1, :], ALU.mult, ALU.mult)
                dve.drain()
                nc.vector.tensor_tensor(mix[:, :], mix[:, :], rows[:, 2, :], ALU.add).then_inc(h2_ready, 1)


def retrieve(nc, dr, t):
    NT = 2 * HP
    with ExitStack() as ctx:
        sb = lambda n, s, d=F32: ctx.enter_context(nc.sbuf_tensor("r_" + n, s, d))
        sem = semaphores(nc, ctx, "r_")
        wq, keys = sb("wq", [P, KT, NT * P]), sb("keys", [P, 2, P])
        h2, h2T, qT = sb("h2", [P, D]), sb("h2T", [P, KT, P]), sb("qT", [P, 2, P])
        S, S2 = sb("S", [P, NT, P]), sb("S2", [P, NT, P])
        v16, i16, i16f = sb("v16", [P, NT, TOPK]), sb("i16", [P, NT, TOPK], U32), sb("i16f", [P, NT, TOPK])
        cand, cand2 = sb("cand", [P, HP, TOPK, TOPK]), sb("cand2", [P, HP, TOPK, TOPK])
        best, place = sb("best", [P, HP, TOPK]), sb("place", [P, HP, TOPK], U32)
        pick, pickf = sb("pick", [P, 2, SLOTS], U32), sb("pickf", [P, 2, SLOTS])
        hot, num = sb("hot", [P, SLOTS, TOPK]), sb("num", [P, 2, SLOTS])
        arg, total = sb("arg", [P, HP, TOPK]), sb("total", [P, HP])
        bank = [ctx.enter_context(nc.psum_tensor(f"r_bank{i}", [P, 512], F32)) for i in range(8)]
        w_in, loaded, turned, h2T_ready, q_mm, q_moved, s_mm, S_ready, scored, arg_ready, exp_ready, done, passed = (
            sem("w_in"), sem("loaded"), sem("turned"), sem("h2T_ready"), sem("q_mm"), sem("q_moved"), sem("s_mm"), sem("S_ready"),
            sem("scored"), sem("arg_ready"), sem("exp_ready"), sem("done"), sem("passed"))
        block = ctx.enter_context(nc.Block())

        @block.sync
        def _(sp):
            sp.dma_start(wq[:, :, :], dr["w_q"]).then_inc(w_in, 16)
            sp.dma_start(keys[:, :, :], dr["keysT"]).then_inc(w_in, 16)
            with sp.Fori(0, BLOCKS) as i:
                b = sp.snap(i + 0)
                sp.wait_ge(turned, i)
                sp.sem_inc(passed, 1)
                sp.dma_start(h2[:, :], row(dr["h2"][bass.ds(b, 1)])).then_inc(loaded, 16)

        @block.tensor
        def _(pe):
            pe.wait_ge(w_in, 32)
            with pe.Fori(0, BLOCKS) as i:
                pe.wait_ge(loaded, i * 16 + 16)
                pe.wait_ge(S_ready, i)
                for k in range(KT):
                    last = nc.tensor.transpose(bank[k // 4][:, (k % 4) * P:(k % 4 + 1) * P], h2[:, k * P:(k + 1) * P], t["ident"][:, :])
                last.then_inc(turned, 1)
                pe.wait_ge(h2T_ready, i + 1)

                def score(n):
                    pe.wait_ge(q_moved, i * NT + (n + 1))
                    to = bank[4 + n // 4][:, (n % 4) * P:(n % 4 + 1) * P]
                    nc.tensor.matmul(to, qT[:, n % 2, :], keys[:, n % 2, :], start=True, stop=True).then_inc(s_mm, 1)

                for n in range(NT):
                    if n >= 2:
                        pe.wait_ge(q_moved, i * NT + (n - 1))
                    for k in range(KT):
                        last = nc.tensor.matmul(bank[2 + n % 2][:, 0:P], wq[:, k, n * P:(n + 1) * P], h2T[:, k, :],
                                                start=(k == 0), stop=(k == KT - 1))
                    last.then_inc(q_mm, 1)
                    if n:
                        score(n - 1)
                score(NT - 1)

        @block.scalar
        def _(act):
            with act.Fori(0, BLOCKS) as i:
                act.wait_ge(turned, i + 1)
                for c in range(2):
                    last = nc.scalar.copy(h2T[:, 4 * c:4 * c + 4, :].rearrange("p k t -> p (k t)"), bank[c][:, :])
                last.then_inc(h2T_ready, 1)
                for n in range(NT):
                    act.wait_ge(q_mm, i * NT + (n + 1))
                    if n >= 2:
                        act.wait_ge(s_mm, i * NT + (n - 1))
                    nc.scalar.copy(qT[:, n % 2, :], bank[2 + n % 2][:, 0:P]).then_inc(q_moved, 1)
                act.wait_ge(s_mm, i * NT + NT)
                act.wait_ge(scored, i)
                for c in range(4):
                    last = nc.scalar.copy(S[:, 4 * c:4 * c + 4, :].rearrange("p n k -> p (n k)"), bank[4 + c][:, :])
                last.then_inc(S_ready, 1)
                act.wait_ge(arg_ready, i + 1)
                nc.scalar.activation(arg[:, :, :], arg[:, :, :], ACT.Exp).then_inc(exp_ready, 1)

        @block.vector
        def _(dve):
            def best16(values, scratch, v, index, width):
                for n in range(len(values)):
                    nc.vector.max(v[n][:, 0:8], values[n])
                dve.drain()
                for n in range(len(values)):
                    nc.vector.match_replace(scratch[n], v[n][:, 0:8], values[n], -3.0e38)
                dve.drain()
                for n in range(len(values)):
                    nc.vector.max(v[n][:, 8:16], scratch[n])
                    nc.vector.max_index(index[n][:, 0:8], v[n][:, 0:8], values[n])
                dve.drain()
                for n in range(len(values)):
                    nc.vector.max_index(index[n][:, 8:16], v[n][:, 8:16], scratch[n])
                dve.drain()

            flat = lambda ap: ap.rearrange("p a b -> p (a b)")
            with dve.Fori(0, BLOCKS) as i:
                b = dve.snap(i + 0)
                dve.wait_ge(S_ready, i + 1)
                dve.sem_inc(passed, 1)
                best16([S[:, n, :] for n in range(NT)], [S2[:, n, :] for n in range(NT)], [v16[:, n, :] for n in range(NT)],
                       [i16[:, n, :] for n in range(NT)], P)
                dve.sem_inc(scored, 1)
                nc.vector.tensor_copy(i16f[:, :, :], i16[:, :, :])
                for h in range(HP):
                    nc.vector.tensor_tensor(cand[:, h], bc_last(v16[:, 2 * h, :], TOPK),
                                            v16[:, 2 * h + 1, :].unsqueeze(1).to_broadcast([P, TOPK, TOPK]), ALU.add)
                dve.drain()
                best16([flat(cand[:, h]) for h in range(HP)], [flat(cand2[:, h]) for h in range(HP)],
                       [best[:, h, :] for h in range(HP)], [place[:, h, :] for h in range(HP)], TOPK * TOPK)
                nc.vector.tensor_tensor(arg[:, :, :], best[:, :, :], best[:, :, 0:1].to_broadcast([P, HP, TOPK]), ALU.subtract).then_inc(arg_ready, 1)
                nc.vector.tensor_scalar(pick[:, 0, :], flat(place[:, :, :]), 4, None, ALU.logical_shift_right)
                nc.vector.tensor_scalar(pick[:, 1, :], flat(place[:, :, :]), 15, None, ALU.bitwise_and)
                dve.drain()
                nc.vector.tensor_copy(pickf[:, :, :], pick[:, :, :])
                dve.drain()
                for c in range(2):
                    nc.vector.tensor_tensor(hot[:, :, :], bc_last(pickf[:, c, :], TOPK),
                                            t["iota"][:, :].unsqueeze(1).to_broadcast([P, SLOTS, TOPK]), ALU.is_equal)
                    dve.drain()
                    numbers = i16f[:, :, :].rearrange("p (h c) j -> p h c j", c=2)[:, :, c, :]
                    hv = hot[:, :, :].rearrange("p (h k) j -> p h k j", h=HP)
                    nc.vector.tensor_tensor(hv, hv, numbers.unsqueeze(2).to_broadcast([P, HP, TOPK, TOPK]), ALU.mult)
                    dve.drain()
                    nc.vector.tensor_reduce(num[:, c, :], hot[:, :, :], AX, ALU.add)
                    dve.drain()
                nc.vector.scalar_tensor_tensor(num[:, 0, :], num[:, 0, :], float(P), num[:, 1, :], ALU.mult, ALU.add)
                dve.drain()
                nc.vector.tensor_copy(t["idx"][:, bass.ds(b, 1), :].rearrange("p o n -> p (o n)"), num[:, 0, :])
                dve.wait_ge(exp_ready, i + 1)
                nc.vector.tensor_reduce(total[:, :], arg[:, :, :], AX, ALU.add)
                dve.drain()
                nc.vector.reciprocal(total[:, :], total[:, :])
                dve.drain()
                nc.vector.tensor_tensor(t["gate"][:, bass.ds(b, 1), :].rearrange("p o (h k) -> p (o h) k", h=HP), arg[:, :, :],
                                        bc_last(total[:, :], TOPK), ALU.mult)
                dve.drain()


def experts(nc, dr, t):
    HALF, RING = 8, 8
    BODIES = SLOTS // (2 * HALF)
    with ExitStack() as ctx:
        sb = lambda n, s, d=F32: ctx.enter_context(nc.sbuf_tensor("e_" + n, s, d))
        sem = semaphores(nc, ctx, "e_")
        ub, vb = sb("ub", [P, RING, D]), sb("vb", [P, RING, D])
        num = sb("num", [P, 2, HALF], U32)
        xb, x1, row_f, f, sq = sb("xb", [P, D]), sb("x1", [P, D]), sb("row_f", [P, D]), sb("f", [P, D]), sb("sq", [P, D])
        dots, act_v, coef = sb("dots", [P, 2, HALF]), sb("act", [P, 2, HALF]), sb("coef", [P, 2, HALF])
        gcur, diag, zero = sb("gcur", [P, SLOTS]), sb("diag", [P, 2, HALF, P]), sb("zero", [P, P])
        ss, root, rr = sb("ss", [P, 1]), sb("root", [P, 1]), sb("rr", [P, 1])
        acc = ctx.enter_context(nc.psum_tensor("e_acc", [P, D], F32))
        u_in, v_in = [sem(f"u_in{j}") for j in range(RING)], [sem(f"v_in{j}") for j in range(RING)]
        u_free, v_free = sem("u_free"), sem("v_free")
        num_ready, dots_ready, act_ready, coef_ready, diag_ready = sem("num_ready"), sem("dots_ready"), sem("act_ready"), sem("coef_ready"), sem("diag_ready")
        zero_ready, x_in, x1_in, x_used, f_mm, f_out, ms_ready, root_ready, ss_ready, y_ready, y_out = (
            sem("zero_ready"), sem("x_in"), sem("x1_in"), sem("x_used"), sem("f_mm"), sem("f_out"), sem("ms_ready"), sem("root_ready"),
            sem("ss_ready"), sem("y_ready"), sem("y_out"))
        passed, pool_passed = sem("passed"), sem("pool_passed")
        block = ctx.enter_context(nc.Block())

        @block.sync
        def _(sp):
            with sp.Fori(0, BLOCKS) as b:
                c = sp.snap(b + 0)
                sp.wait_ge(x_used, b)
                sp.sem_inc(passed, 1)
                sp.dma_start(xb[:, :], row(dr["h2"][bass.ds(c, 1)])).then_inc(x_in, 16)
                sp.wait_ge(y_out, b * 16)
                sp.sem_inc(passed, 1)
                sp.dma_start(x1[:, :], row(dr["x1"][bass.ds(c, 1)])).then_inc(x1_in, 16)
                r = row(dr["mod_rows"][bass.ds(c, 1)])[0:1, V_GATE_F * D:(V_GATE_F + 1) * D]
                sp.dma_start(row_f[:, :], r.partition_broadcast(P)).then_inc(x1_in, 16)
                sp.wait_ge(y_ready, b + 1)
                sp.sem_inc(passed, 1)
                sp.dma_start(row(dr["out_y"][bass.ds(c, 1)]), x1[:, :]).then_inc(y_out, 16)
            sp.wait_ge(y_out, 16 * BLOCKS)

        @block.gpsimd
        def _(pool):
            with pool.Fori(0, BLOCKS * BODIES) as i:
                for half in range(2):
                    s = i * (2 * HALF) + half * HALF
                    pool.wait_ge(v_free, s)
                    pool.wait_ge(u_free, s)
                    pool.sem_inc(pool_passed, 1)
                    nc.gpsimd.tensor_copy(num[:, half, :], t["idx"][:, :, :].rearrange("p b n -> p (b n)")[:, bass.ds(s, HALF)]).then_inc(num_ready, 1)
                    pool.wait_ge(num_ready, i * 2 + (half + 1))
                    for j in range(HALF):
                        pool.wait_ge(u_free, s + (j + 1))
                        pool.sem_inc(pool_passed, 1)
                        nc.gpsimd.indirect_dma_start(ub[:, j, :], None, dr["peer_u"], bass.IndirectOffsetOnAxis(num[:, half, j:j + 1], 0)).then_inc(u_in[j], 16)
                        pool.wait_ge(v_free, s + (j + 1))
                        pool.sem_inc(pool_passed, 1)
                        nc.gpsimd.indirect_dma_start(vb[:, j, :], None, dr["peer_v"], bass.IndirectOffsetOnAxis(num[:, half, j:j + 1], 0)).then_inc(v_in[j], 16)

        @block.vector
        def _(dve):
            dve.sem_inc(u_free, RING)
            nc.vector.memset(zero[:, :], 0.0).then_inc(zero_ready, 1)
            with dve.Fori(0, BLOCKS) as b:
                c = dve.snap(b + 0)
                dve.wait_ge(x_in, b * 16 + 16)
                dve.sem_inc(passed, 1)
                nc.vector.tensor_copy(gcur[:, :], t["gate"][:, bass.ds(c, 1), :].rearrange("p o n -> p (o n)"))
                dve.drain()
                with dve.Fori(0, BODIES) as k:
                    for half in range(2):
                        seen = (b * BODIES + k) * 2 + half
                        for q in range(2):
                            for j in range(4 * q, 4 * q + 4):
                                dve.wait_ge(u_in[j], seen * 16 + 16)
                                nc.vector.tensor_tensor_reduce(ub[:, j, :], ub[:, j, :], xb[:, :], 1.0, 0.0, ALU.mult, ALU.add,
                                                               dots[:, half, j:j + 1]).then_inc(u_free, 1)
                            dve.drain()
                            dve.sem_inc(dots_ready, 1)
                            dve.wait_ge(act_ready, seen * 2 + (q + 1))
                            dve.wait_ge(diag_ready, seen * 2 + q)
                            dve.sem_inc(passed, 1)
                            w = slice(4 * q, 4 * q + 4)
                            nc.vector.tensor_tensor(coef[:, half, w], act_v[:, half, w],
                                                    gcur[:, bass.ds(k * (2 * HALF) + (half * HALF + 4 * q), 4)], ALU.mult).then_inc(coef_ready, 1)
                dve.drain()
                dve.sem_inc(x_used, 1)
                dve.wait_ge(ss_ready, b + 1)
                nc.vector.tensor_scalar(ss[:, :], ss[:, :], 1.0 / D, EPS, ALU.mult, ALU.add).then_inc(ms_ready, 1)
                dve.wait_ge(root_ready, b + 1)
                nc.vector.reciprocal(rr[:, :], root[:, :])
                dve.drain()
                dve.wait_ge(x1_in, b * 32 + 32)
                nc.vector.scalar_tensor_tensor(f[:, :], f[:, :], rr[:, 0:1], row_f[:, :], ALU.mult, ALU.mult)
                dve.drain()
                nc.vector.tensor_tensor(x1[:, :], x1[:, :], f[:, :], ALU.add)
                dve.drain()
                dve.sem_inc(y_ready, 1)

        @block.scalar
        def _(act):
            with act.Fori(0, BLOCKS) as b:
                with act.Fori(0, BODIES) as k:
                    for half in range(2):
                        seen = (b * BODIES + k) * 2 + half
                        for q in range(2):
                            w = slice(4 * q, 4 * q + 4)
                            act.wait_ge(dots_ready, seen * 2 + (q + 1))
                            nc.scalar.activation(act_v[:, half, w], dots[:, half, w], ACT.Gelu).then_inc(act_ready, 1)
                            act.wait_ge(coef_ready, seen * 2 + (q + 1))
                            act.wait_ge(v_free, seen * 8)
                            for j in range(4 * q, 4 * q + 4):
                                last = nc.scalar.mul(diag[:, half, j, :], t["ident"][:, :], coef[:, half, j:j + 1])
                            last.then_inc(diag_ready, 1)
                act.wait_ge(f_mm, b + 1)
                act.wait_ge(y_ready, b)
                nc.scalar.copy(f[:, :], acc[:, :]).then_inc(f_out, 1)
                act.wait_ge(f_out, b + 1)
                nc.scalar.activation(sq[:, :], f[:, :], ACT.Square, accum_out=ss[:, :])
                act.drain()
                act.sem_inc(ss_ready, 1)
                act.wait_ge(ms_ready, b + 1)
                nc.scalar.activation(root[:, :], ss[:, :], ACT.Sqrt).then_inc(root_ready, 1)

        @block.tensor
        def _(pe):
            pe.sem_inc(v_free, RING)
            pe.wait_ge(zero_ready, 1)
            z512 = zero[:, :].unsqueeze(1).to_broadcast([P, 4, P])
            with pe.Fori(0, BLOCKS) as b:
                pe.wait_ge(f_out, b)
                for c in range(2):
                    nc.tensor.matmul(acc[:, c * 512:(c + 1) * 512], zero[:, :], z512, start=True, stop=False)
                with pe.Fori(0, BODIES) as k:
                    for half in range(2):
                        seen = (b * BODIES + k) * 2 + half
                        for j in range(HALF):
                            if j % 4 == 0:
                                pe.wait_ge(diag_ready, seen * 2 + (j // 4 + 1))
                            pe.wait_ge(v_in[j], seen * 16 + 16)
                            for c in range(2):
                                last = nc.tensor.matmul(acc[:, c * 512:(c + 1) * 512], diag[:, half, j, :],
                                                        vb[:, j, c * 512:(c + 1) * 512], start=False, stop=False)
                            last.then_inc(v_free, 1)
                for c in range(2):
                    last = nc.tensor.matmul(acc[:, c * 512:(c + 1) * 512], zero[:, :], z512, start=False, stop=True)
                last.then_inc(f_mm, 1)


def programme(nc, dr):
    with ExitStack() as ctx:
        sb = lambda n, s, d=F32: ctx.enter_context(nc.sbuf_tensor(n, s, d))
        t = {n: sb(n, [P, P]) for n in ("ones", "triF", "triB", "ident", "nident", "maskF", "maskB")}
        t["iota_i"], t["iota"] = sb("iota_i", [P, TOPK], mybir.dt.int32), sb("iota", [P, TOPK])
        t["rows"], t["skip"], t["gains"] = sb("rows", [P, R_N]), sb("skip", [P, HS]), sb("gains", [P, 6, KT])
        t["vecs"] = sb("vecs", [P, 2, 6, KT])
        t["small"], t["gates"] = sb("small", [P, BLOCKS, 48]), sb("gates", [P, BLOCKS, G_N])
        t["idx"], t["gate"] = sb("idx", [P, BLOCKS, SLOTS], U32), sb("gate", [P, BLOCKS, SLOTS])
        constants(nc, t)
        modulation(nc, dr, t)
        skip_sum(nc, t)
        with nc.sbuf_tensor("hT", [P, KT, TOK], F32) as hT:
            normalise(nc, dr, t, hT)
            project(nc, dr, t, hT)
        gates(nc, dr, t)
        scan(nc, dr, t, "prompt")
        scan(nc, dr, t, "back")
        scan(nc, dr, t, "sample")
        merge(nc, dr, t)
        retrieve(nc, dr, t)
        experts(nc, dr, t)


def cat(*a, axis=-1):
    import numpy as np
    return np.concatenate(a, axis=axis)


def tiles(w, n=512):
    import numpy as np
    rows, columns = w.shape
    return np.ascontiguousarray(w.reshape(rows // P, P, columns // n, n).transpose(2, 1, 0, 3))


def cols(v):
    import numpy as np
    v = v.reshape(*v.shape[:-1], v.shape[-1] // P, P)
    return np.ascontiguousarray(np.moveaxis(v, -1, 0))


def layout(i):
    import numpy as np
    w = i["w_in"][0]
    z, xbc, dt, q, k, v, o, g, m = np.split(w, np.cumsum([1024, 2048, 32, 1024, 1024, 1024, 1024, 16]), axis=1)
    g = g.reshape(1024, 2, 2, 4).transpose(0, 2, 1, 3).reshape(1024, 16)
    out = {}
    out["x"] = cat(i["x_prompt"].reshape(1, 128, 1024), i["x_sample"].reshape(4, 128, 1024), axis=0)
    out["cvT"] = np.ascontiguousarray(np.moveaxis(cols(cat(i["c_ctx"][None], i["c"], axis=0)), 1, 2))
    out["w_mod"] = tiles(i["w_mod"][0])
    out["b_modT"] = cols(i["b_mod"][0].reshape(6, 1024))
    out["gains"] = cols(np.stack([i[n][0] for n in ("g_mix_pre", "g_mix_post", "g_ffn_pre", "g_ffn_post", "ssd_norm_g", "mlstm_norm_g")]))
    out["small_rows"] = cat(*[i[n].reshape(1, -1) for n in ("ssd_a_log", "ssd_dt_bias", "ssd_d", "mlstm_i_bias", "mlstm_f_bias", "state_mlstm_m")])
    out["w_big"] = tiles(cat(z, v, o, m, xbc, q, k))
    out["w_small"] = tiles(cat(dt, g), 48)[0]
    out["convT"] = cols(cat(i["conv_w"][0], i["conv_b"], axis=0))
    out["w_out3"] = np.stack([tiles(i[n][0], 1024)[0] for n in ("w_ssd_out", "w_mlstm_out", "w_out")])
    out["w_q"] = tiles(i["peer_w_q"][0], 2048)[0]
    out["keysT"] = np.ascontiguousarray(np.stack([i["peer_keys1"][0].T, i["peer_keys2"][0].T], axis=1))
    out["peer_u"], out["peer_v"] = i["peer_u"][0], i["peer_v"][0]
    out["state_ssd"] = np.ascontiguousarray(i["state_ssd"].reshape(2, 1024, 128).transpose(0, 2, 1))
    c = cat(i["state_mlstm_c"].reshape(2, 4, 2, 128, 256), i["state_mlstm_n"].reshape(2, 4, 2, 128, 1))
    out["state_c"] = np.ascontiguousarray(c.transpose(0, 3, 1, 2, 4)).reshape(2, 128, 8 * 257)
    return out


SCRATCH = {
    "mod_rows": (BLOCKS, 1, 6 * D), "proj": (BLOCKS, P, COLS_T), "xbcT": (16, P, TOK), "qkT": (16, P, TOK),
    "back_ssd": (CHUNKS, P, D), "back_c": (CHUNKS, P, HM * 2 * CE), "back_m": (CHUNKS, P, HM),
    "y_ssd": (BLOCKS, P, D), "y_mlstm": (BLOCKS, P, D), "x1": (BLOCKS, P, D), "h2": (BLOCKS, P, D),
}
OUTPUTS = {"out_y": (BLOCKS, P, D), "out_ssd": (2, P, D), "out_c": (2, P, HM * 2 * CE), "out_m": (1, 2 * HM)}


def kernel(**inputs):
    import numpy as np
    import concourse.bacc as bacc
    from concourse.bass_utils import run_bass_kernel_spmd

    nc = bacc.Bacc("TRN2", target_bir_lowering=False, num_devices=1)
    arrays, dr = {}, {}
    for name, a in layout({k: np.asarray(v) for k, v in inputs.items()}).items():
        arrays["in_" + name] = np.ascontiguousarray(a)
        dr[name] = nc.dram_tensor("in_" + name, a.shape, F32, kind="ExternalInput").ap()
    for name, shape in SCRATCH.items():
        dr[name] = nc.dram_tensor("scratch_" + name, shape, F32, kind="Internal").ap()
    for name, shape in OUTPUTS.items():
        dr[name] = nc.dram_tensor(name, shape, F32, kind="ExternalOutput").ap()
    programme(nc, dr)
    got = run_bass_kernel_spmd(nc, [arrays], core_ids=[0]).results[0]
    y = got["out_y"]
    ssd = got["out_ssd"].transpose(0, 2, 1).reshape(1, 1, 2, HS, PS, P)
    c = got["out_c"].reshape(2, P, HM, 2, CE).transpose(0, 2, 3, 1, 4).reshape(1, 1, 2, HM, DM, CE)
    return (y[0:1].reshape(1, P, D), y[1:].reshape(1, LAT, D), np.ascontiguousarray(ssd), np.ascontiguousarray(c[..., :DM]),
            np.ascontiguousarray(c[..., DM]), got["out_m"].reshape(1, 1, 2, HM))
```

```python
from contextlib import ExitStack

import concourse.bass as bass
from concourse import mybir

P = 128
D = 1024
KT = D // P
BLOCKS = 5
CHUNKS = BLOCKS - 1
TOK = BLOCKS * P
LAT = CHUNKS * P
GRID_W = 64
EPS = 1e-6
HS, PS, NG = 16, 64, 4
HM, DM = 4, 256
CE = DM + 1
HP, TOPK = 8, 16
SLOTS = HP * TOPK
NEG = -1.0e30

ALU = mybir.AluOpType
ACT = mybir.ActivationFunctionType
AX = mybir.AxisListType.X
F32 = mybir.dt.float32
U32 = mybir.dt.uint32

COL_Z, COL_V, COL_O, COL_M, COLS_T = 0, D, 2 * D, 3 * D, 5 * D
G_DA, G_LI, G_NACS, G_EA, G_WD, G_ED, G_E, G_DT, G_BC, G_TOT, G_LF = 0, 32, 40, 72, 104, 136, 168, 176, 208, 216, 224
G_N = 232
R_ALOG, R_DTB, R_SKIP, R_IB, R_FB, R_M0 = 0, 32, 64, 96, 104, 112
R_N = 120
V_SCALE_A, V_SHIFT_A, V_GATE_A, V_SCALE_F, V_SHIFT_F, V_GATE_F = range(6)


def bc_last(ap, n):
    shape = list(ap.shape) + [n]
    return ap.unsqueeze(len(ap.shape)).to_broadcast(shape)


def semaphores(nc, ctx, prefix=""):
    taken = []

    def sem(name):
        taken.append(nc.alloc_semaphore(prefix + name))
        return taken[-1]

    def give_back():
        nc.clear_and_free_semaphores(taken)
        nc.all_engine_barrier()

    ctx.callback(give_back)
    return sem


def row(ap):
    return ap.rearrange("o p f -> p (o f)")


def constants(nc, t):
    with ExitStack() as ctx:
        ready = semaphores(nc, ctx)("const_step")
        block = ctx.enter_context(nc.Block())

        @block.gpsimd
        def _(pool):
            nc.gpsimd.memset(t["ones"][:, :], 1.0).then_inc(ready, 1)
            nc.gpsimd.iota(t["iota_i"][:, :], [[1, TOPK]], base=0, channel_multiplier=0).then_inc(ready, 1)
            pool.wait_ge(ready, 2)
            nc.gpsimd.affine_select(out=t["triF"][:, :], in_=t["ones"][:, :], pattern=[[1, P]], compare_op=ALU.is_ge,
                                    fill=0.0, base=0, channel_multiplier=-1).then_inc(ready, 1)
            nc.gpsimd.affine_select(out=t["triB"][:, :], in_=t["ones"][:, :], pattern=[[-1, P]], compare_op=ALU.is_ge,
                                    fill=0.0, base=0, channel_multiplier=1).then_inc(ready, 1)
            nc.gpsimd.affine_select(out=t["ident"][:, :], in_=t["ones"][:, :], pattern=[[-1, P]], compare_op=ALU.is_equal,
                                    fill=0.0, base=0, channel_multiplier=1).then_inc(ready, 1)
            nc.gpsimd.tensor_copy(t["iota"][:, :], t["iota_i"][:, :]).then_inc(ready, 1)
            pool.wait_ge(ready, 6)
            nc.gpsimd.tensor_scalar(t["maskF"][:, :], t["triF"][:, :], 1.0, -NEG, ALU.subtract, ALU.mult).then_inc(ready, 1)
            nc.gpsimd.tensor_scalar(t["maskB"][:, :], t["triB"][:, :], 1.0, -NEG, ALU.subtract, ALU.mult).then_inc(ready, 1)


def modulate_and_normalise(nc, dr, t, hT):
    NCH, RING, FIRST = 6 * D // 512, 4, 4
    with ExitStack() as ctx:
        sb = lambda n, s, d=F32: ctx.enter_context(nc.sbuf_tensor(n, s, d))
        sem = semaphores(nc, ctx)
        cv, sig = sb("cv", [P, KT, 2]), sb("cv_sig", [P, KT, 2])
        wm = sb("wm", [P, RING, KT, 512])
        bias, gain = sb("mod_bias", [2, 6 * D]), sb("mod_gain", [2, 4, D])
        raw, vec = sb("mod_raw", [2, 2, 512]), sb("mod_vec", [2, 6, D])
        cols = sb("mod_cols", [P, 2, KT, 2])
        x, sq = sb("x", [P, BLOCKS, D]), sb("x_sq", [P, D])
        ss, root, rstd = sb("x_ss", [P, BLOCKS]), sb("x_root", [P, BLOCKS]), sb("x_rstd", [P, BLOCKS])
        row_ps = [ctx.enter_context(nc.psum_tensor(f"mod_ps{i}", [2, 512], F32)) for i in range(2)]
        col_ps = ctx.enter_context(nc.psum_tensor("mod_cols_ps", [P, 2, KT, 2], F32))
        ps = [ctx.enter_context(nc.psum_tensor(f"turn{i}", [P, 4, P], F32)) for i in range(4)]
        small_in, w_in, x_in = sem("small_in"), [sem(f"mod_w{i}") for i in range(RING)], [sem(f"x_in{b}") for b in range(BLOCKS)]
        sig_ready, silu_ready, chunk_mm, chunk_out, vec_ready = sem("sig_ready"), sem("silu_ready"), sem("chunk_mm"), sem("chunk_out"), sem("vec_ready")
        cols_turned, later_in, rows_out = sem("cols_turned"), sem("later_in"), sem("rows_out")
        sums_ready, ms_ready, root_ready, scaled, turned, moved = (
            sem("sums_ready"), sem("ms_ready"), sem("root_ready"), sem("x_scaled"), sem("x_turned"), sem("h_moved"))
        block = ctx.enter_context(nc.Block())

        @block.sync
        def _(sp):
            sp.dma_start(cv[:, :, :], dr["cvT"]).then_inc(small_in, 16)
            sp.dma_start(bias[:, :], dr["b_mod"].partition_broadcast(2)).then_inc(small_in, 16)
            sp.dma_start(gain[:, :, :].rearrange("p g n -> p (g n)"), dr["gain_rows"].partition_broadcast(2)).then_inc(small_in, 16)
            for n in range(2):
                sp.dma_start(wm[:, n], dr["w_mod"][n]).then_inc(w_in[n], 16)
            for b in range(BLOCKS):
                sp.dma_start(x[:, b, :], dr["x"][b]).then_inc(x_in[b], 16)
            sp.dma_start(t["gains"][:, :, :], dr["gains"]).then_inc(later_in, 16)
            sp.dma_start(t["rows"][:, :], dr["small_rows"].partition_broadcast(P)).then_inc(later_in, 16)
            for n in range(2, NCH):
                if n >= RING:
                    sp.wait_ge(chunk_mm, n - RING + 1)
                sp.dma_start(wm[:, n % RING], dr["w_mod"][n]).then_inc(w_in[n % RING], 16)
            sp.wait_ge(vec_ready, NCH)
            for b in range(BLOCKS):
                c = 0 if b == 0 else 1
                sp.dma_start(dr["mod_rows"][b], vec[c:c + 1, :, :].rearrange("p v n -> p (v n)")).then_inc(rows_out, 16)
            sp.wait_ge(rows_out, 16 * BLOCKS)
            sp.wait_ge(later_in, 32)

        @block.scalar
        def _(act):
            act.wait_ge(small_in, 48)
            nc.scalar.activation(sig[:, :, :], cv[:, :, :], ACT.Sigmoid).then_inc(sig_ready, 1)
            for b in range(BLOCKS):
                act.wait_ge(x_in[b], 16)
                nc.scalar.activation(sq[:, :], x[:, b, :], ACT.Square, accum_out=ss[:, b:b + 1])
                act.drain()
            act.sem_inc(sums_ready, 1)
            act.wait_ge(ms_ready, 1)
            nc.scalar.activation(root[:, :], ss[:, :], ACT.Sqrt).then_inc(root_ready, 1)
            act.wait_ge(cols_turned, 1)
            nc.scalar.copy(cols[:, :, :, :], col_ps[:, :, :, :])
            act.drain()
            for n in range(2 * BLOCKS):
                b, half = n // 2, n % 2
                act.wait_ge(turned, n + 1)
                c = 0 if b == 0 else 1
                for i in range(4):
                    k = 4 * half + i
                    last = nc.scalar.activation(hT[:, k, b * P:(b + 1) * P], ps[n % 4][:, i, :], ACT.Identity,
                                                scale=cols[:, V_SCALE_A, k, c:c + 1], bias=cols[:, V_SHIFT_A, k, c:c + 1])
                last.then_inc(moved, 1)

        @block.tensor
        def _(pe):
            def chunk(n):
                pe.wait_ge(w_in[n % RING], 16 * (n // RING + 1))
                if n >= 2:
                    pe.wait_ge(chunk_out, n - 1)
                for k in range(KT):
                    last = nc.tensor.matmul(row_ps[n % 2][:, :], cv[:, k, :], wm[:, n % RING, k, :], start=(k == 0), stop=(k == KT - 1))
                last.then_inc(chunk_mm, 1)

            pe.wait_ge(silu_ready, 1)
            for n in range(FIRST):
                chunk(n)
            pe.wait_ge(vec_ready, FIRST)
            for v in (V_SCALE_A, V_SHIFT_A):
                for k in range(KT):
                    last = nc.tensor.transpose(col_ps[:, v, k, :], vec[:, v, k * P:(k + 1) * P], t["ident"][0:2, 0:2])
            last.then_inc(cols_turned, 1)
            for n in range(2 * BLOCKS):
                b, half = n // 2, n % 2
                pe.wait_ge(scaled, b + 1)
                if n >= 4:
                    pe.wait_ge(moved, n - 3)
                for i in range(4):
                    k = 4 * half + i
                    last = nc.tensor.transpose(ps[n % 4][:, i, :], x[:, b, k * P:(k + 1) * P], t["ident"][:, :])
                last.then_inc(turned, 1)
            for n in range(FIRST, NCH):
                chunk(n)

        @block.vector
        def _(dve):
            dve.wait_ge(sig_ready, 1)
            nc.vector.tensor_tensor(cv[:, :, :], cv[:, :, :], sig[:, :, :], ALU.mult).then_inc(silu_ready, 1)

            def vector(n):
                v, w = n // 2, slice((n % 2) * 512, (n % 2) * 512 + 512)
                to, plus, gn = ((V_SHIFT_A, 0.0, None), (V_SCALE_A, 1.0, 0), (V_GATE_A, 0.0, 1),
                                (V_SHIFT_F, 0.0, None), (V_SCALE_F, 1.0, 2), (V_GATE_F, 0.0, 3))[v]
                dve.wait_ge(chunk_mm, n + 1)
                nc.vector.tensor_tensor(raw[:, n % 2, :], row_ps[n % 2][:, :], bias[:, n * 512:(n + 1) * 512], ALU.add).then_inc(chunk_out, 1)
                dve.drain()
                if gn is None:
                    nc.vector.tensor_copy(vec[:, to, w], raw[:, n % 2, :]).then_inc(vec_ready, 1)
                else:
                    nc.vector.scalar_tensor_tensor(vec[:, to, w], raw[:, n % 2, :], plus, gain[:, gn, w], ALU.add, ALU.mult).then_inc(vec_ready, 1)

            for n in range(FIRST):
                vector(n)
            dve.wait_ge(sums_ready, 1)
            nc.vector.tensor_scalar(ss[:, :], ss[:, :], 1.0 / D, EPS, ALU.mult, ALU.add).then_inc(ms_ready, 1)
            dve.wait_ge(root_ready, 1)
            nc.vector.reciprocal(rstd[:, :], root[:, :])
            dve.drain()
            for b in range(BLOCKS):
                nc.vector.tensor_scalar(x[:, b, :], x[:, b, :], rstd[:, b:b + 1], None, ALU.mult).then_inc(scaled, 1)
            for n in range(FIRST, NCH):
                vector(n)


def project(nc, dr, t, hT):
    T_CH, X_CH, Q_CH = COLS_T // 512, 4, 4
    with ExitStack() as ctx:
        sb = lambda n, s, d=F32: ctx.enter_context(nc.sbuf_tensor(n, s, d))
        sem = semaphores(nc, ctx)
        w = sb("w_chunk", [P, 2, KT, 512])
        ws = sb("w_small", [P, KT, 48])
        out = sb("chunk_out", [P, 2, BLOCKS, 512])
        cw = sb("conv_par", [P, 4, 16])
        cc = sb("conv_cur", [P, 4, 8])
        acc = sb("conv_acc", [P, 2, TOK])
        big = sb("tile_out", [P, 2, 4, TOK])
        pst = [ctx.enter_context(nc.psum_tensor(f"pj{i}", [P, 1024], F32)) for i in range(4)]
        banks = [pst[i // 2][:, (i % 2) * 512:(i % 2) * 512 + 512] for i in range(5)]
        w_in = [sem("w_in0"), sem("w_in1")]
        par_in, small_mm, small_moved = sem("par_in"), sem("small_mm"), sem("small_moved")
        t_mm, x_mm, q_mm = sem("t_mm"), sem("x_mm"), sem("q_mm")
        t_bank_free, x_tile_free, q_tile_free = sem("t_bank_free"), sem("x_tile_free"), sem("q_tile_free")
        acc_ready, x_act = sem("acc_ready"), sem("x_act")
        t_free, x_free, q_free = sem("t_out_free"), sem("x_out_free"), sem("q_out_free")
        t_out, x_out, q_out = [[sem(f"{n}_out{j}") for j in range(2)] for n in "txq"]
        block = ctx.enter_context(nc.Block())

        def w_src(c):
            return dr["w_big"][bass.ds(c, 1)].rearrange("o p k n -> p (o k) n")

        @block.sync
        def _(sp):
            sp.dma_start(ws[:, :, :], dr["w_small"]).then_inc(par_in, 16)
            sp.dma_start(cw[:, :, :], dr["convT"]).then_inc(par_in, 16)
            for j in range(2):
                sp.dma_start(w[:, j], dr["w_big"][j]).then_inc(w_in[j], 16)
            with sp.Fori(0, T_CH // 2) as i:
                for j in range(2):
                    sp.wait_ge(t_mm, i * (2 * BLOCKS) + (j + 1) * BLOCKS)
                    sp.dma_start(w[:, j], w_src(i * 2 + (j + 2))).then_inc(w_in[j], 16)
            with sp.Fori(0, X_CH // 2) as i:
                for j in range(2):
                    sp.wait_ge(x_mm, i * 8 + 4 * (j + 1))
                    sp.dma_start(w[:, j], w_src(i * 2 + (j + 2 + T_CH))).then_inc(w_in[j], 16)
            for j in range(2):
                sp.wait_ge(q_mm, 4 * (j + 1))
                sp.dma_start(w[:, j], dr["w_big"][T_CH + X_CH + 2 + j]).then_inc(w_in[j], 16)

        @block.gpsimd
        def _(pool):
            with pool.Fori(0, T_CH // 2) as i:
                for j in range(2):
                    pool.wait_ge(t_bank_free, i * (2 * BLOCKS) + (5 + (j + 1) * BLOCKS))
                    pool.wait_ge(small_moved, 1)
                    pool.dma_start(dr["proj"].rearrange("b p n -> p b n")[:, :, bass.ds((i * 2 + j) * 512, 512)],
                                   out[:, j]).then_inc(t_out[j], 16)
                    pool.wait_ge(t_out[j], i * 16 + 16)
                    pool.sem_inc(t_free, 1)
            with pool.Fori(0, X_CH // 2) as i:
                for j in range(2):
                    pool.wait_ge(x_act, i * 8 + (2 + 4 * (j + 1)))
                    pool.wait_ge(small_moved, 1)
                    pool.dma_start(dr["xbcT"].rearrange("m p t -> p m t")[:, bass.ds(i * 8 + 4 * j, 4)], big[:, j]).then_inc(x_out[j], 16)
                    pool.wait_ge(x_out[j], i * 16 + 16)
                    pool.sem_inc(x_free, 1)
            with pool.Fori(0, Q_CH // 2) as i:
                for j in range(2):
                    pool.wait_ge(q_tile_free, i * 8 + (4 + 4 * (j + 1)))
                    pool.wait_ge(small_moved, 1)
                    pool.dma_start(dr["qkT"].rearrange("m p t -> p m t")[:, bass.ds(i * 8 + 4 * j, 4)], big[:, j]).then_inc(q_out[j], 16)
                    pool.wait_ge(q_out[j], i * 16 + 16)
                    pool.sem_inc(q_free, 1)

        @block.tensor
        def _(pe):
            pe.wait_ge(par_in, 32)
            for b in range(BLOCKS):
                for k in range(KT):
                    last = nc.tensor.matmul(banks[0][:, b * 48:(b + 1) * 48], hT[:, k, b * P:(b + 1) * P], ws[:, k, :],
                                            start=(k == 0), stop=(k == KT - 1))
            last.then_inc(small_mm, 1)
            pe.wait_ge(small_moved, 1)
            with pe.Fori(0, T_CH // 2) as i:
                for j in range(2):
                    pe.wait_ge(w_in[j], i * 16 + 16)
                    for b in range(BLOCKS):
                        pe.wait_ge(t_bank_free, i * (2 * BLOCKS) + (j * BLOCKS + b + 1))
                        for k in range(KT):
                            last = nc.tensor.matmul(banks[b], hT[:, k, b * P:(b + 1) * P], w[:, j, k, :],
                                                    start=(k == 0), stop=(k == KT - 1))
                        last.then_inc(t_mm, 1)
            pe.wait_ge(t_bank_free, 5 + T_CH * BLOCKS)

            def channel_tiles(i, done_pairs, tile_free, done):
                for j in range(2):
                    pe.wait_ge(w_in[j], i * 16 + 16 * (done_pairs + 1))
                    for m in range(4):
                        pe.wait_ge(tile_free, i * 8 + (4 * j + m + 1))
                        for k in range(KT):
                            nc.tensor.matmul(pst[m][:, 0:LAT], w[:, j, k, m * P:(m + 1) * P], hT[:, k, P:TOK],
                                             start=(k == 0), stop=(k == KT - 1))
                        for k in range(KT):
                            last = nc.tensor.matmul(pst[m][:, LAT:TOK], w[:, j, k, m * P:(m + 1) * P], hT[:, k, 0:P],
                                                    start=(k == 0), stop=(k == KT - 1))
                        last.then_inc(done, 1)

            with pe.Fori(0, X_CH // 2) as i:
                channel_tiles(i, T_CH // 2, x_tile_free, x_mm)
            pe.wait_ge(x_tile_free, 4 + 4 * X_CH)
            with pe.Fori(0, Q_CH // 2) as i:
                channel_tiles(i, (T_CH + X_CH) // 2, q_tile_free, q_mm)

        @block.scalar
        def _(act):
            act.sem_inc(t_bank_free, 5)
            act.sem_inc(q_tile_free, 4)
            for free in (t_free, x_free, q_free):
                act.sem_inc(free, 2)
            act.wait_ge(small_mm, 1)
            nc.scalar.copy(t["small"][:, :, :].rearrange("p b n -> p (b n)"), banks[0][:, 0:48 * BLOCKS]).then_inc(small_moved, 1)
            with act.Fori(0, T_CH // 2) as i:
                for j in range(2):
                    act.wait_ge(t_free, i * 2 + (j + 1))
                    for b in range(BLOCKS):
                        act.wait_ge(t_mm, i * (2 * BLOCKS) + (j * BLOCKS + b + 1))
                        nc.scalar.copy(out[:, j, b, :], banks[b]).then_inc(t_bank_free, 1)
            with act.Fori(0, X_CH // 2) as i:
                for j in range(2):
                    act.wait_ge(x_free, i * 2 + (j + 1))
                    for m in range(4):
                        act.wait_ge(acc_ready, i * 8 + (4 * j + m + 1))
                        nc.scalar.activation(big[:, j, m, P:TOK], acc[:, m % 2, 0:LAT], ACT.Silu)
                        nc.scalar.activation(big[:, j, m, 0:P], acc[:, m % 2, LAT:TOK], ACT.Silu).then_inc(x_act, 1)
            act.wait_ge(x_free, X_CH + 2)
            with act.Fori(0, Q_CH // 2) as i:
                for j in range(2):
                    act.wait_ge(q_free, i * 2 + (j + 1))
                    for m in range(4):
                        act.wait_ge(q_mm, i * 8 + (4 * j + m + 1))
                        nc.scalar.copy(big[:, j, m, P:TOK], pst[m][:, 0:LAT])
                        nc.scalar.copy(big[:, j, m, 0:P], pst[m][:, LAT:TOK]).then_inc(q_tile_free, 1)

        @block.vector
        def _(dve):
            dve.sem_inc(x_tile_free, 4)
            dve.sem_inc(x_act, 2)
            dve.wait_ge(par_in, 32)
            with dve.Fori(0, X_CH // 2) as i:
                nc.vector.tensor_copy(cc[:, :, :], cw[:, :, bass.ds(i * 8, 8)])
                dve.drain()
                for n in range(8):
                    m = n % 4
                    dve.wait_ge(x_mm, i * 8 + (n + 1))
                    dve.wait_ge(x_act, i * 8 + (n + 1))
                    lat = acc[:, n % 2, 0:LAT]
                    pro = acc[:, n % 2, LAT:TOK]
                    nc.vector.tensor_scalar(acc[:, n % 2, :], pst[m][:, 0:TOK], cc[:, 1, n:n + 1], cc[:, 3, n:n + 1],
                                            ALU.mult, ALU.add)
                    dve.drain()
                    grid = lat.rearrange("p (r g) -> p r g", g=GRID_W)
                    u = pst[m][:, 0:LAT].rearrange("p (r g) -> p r g", g=GRID_W)
                    nc.vector.scalar_tensor_tensor(grid[:, :, 1:], u[:, :, 0:GRID_W - 1], cc[:, 0, n:n + 1],
                                                   grid[:, :, 1:], ALU.mult, ALU.add)
                    nc.vector.scalar_tensor_tensor(pro[:, 1:], pst[m][:, LAT:TOK - 1], cc[:, 0, n:n + 1],
                                                   pro[:, 1:], ALU.mult, ALU.add)
                    dve.drain()
                    nc.vector.scalar_tensor_tensor(grid[:, :, 0:GRID_W - 1], u[:, :, 1:], cc[:, 2, n:n + 1],
                                                   grid[:, :, 0:GRID_W - 1], ALU.mult, ALU.add)
                    nc.vector.scalar_tensor_tensor(pro[:, 0:P - 1], pst[m][:, LAT + 1:TOK], cc[:, 2, n:n + 1],
                                                   pro[:, 0:P - 1], ALU.mult, ALU.add).then_inc(acc_ready, 1)
                    dve.wait_ge(acc_ready, i * 8 + (n + 1))
                    dve.sem_inc(x_tile_free, 1)


def gates(nc, dr, t):
    NS = 2 * HS
    NM = 2 * HM
    with ExitStack() as ctx:
        sb = lambda n, s, d=F32: ctx.enter_context(nc.sbuf_tensor(n, s, d))
        sem = semaphores(nc, ctx)
        W = NS + NM
        raw = sb("gt_raw", [P, BLOCKS, W])
        nabs = sb("gt_nabs", [P, BLOCKS, W])
        y = sb("gt_y", [P, BLOCKS, W])
        u = sb("gt_u", [P, BLOCKS, W])
        lnu = sb("gt_ln", [P, BLOCKS, W])
        a = sb("gt_a", [P, NS])
        fb = sb("gt_fb", [P, NM])
        tmp = sb("gt_tmp", [P, BLOCKS, NS])
        tm2 = sb("gt_tm2", [P, BLOCKS, NS])
        ps = ctx.enter_context(nc.psum_tensor("gt_ps", [P, BLOCKS, NS], F32))
        pt = ctx.enter_context(nc.psum_tensor("gt_pt", [P, BLOCKS, NS], F32))
        pm = ctx.enter_context(nc.psum_tensor("gt_pm", [P, 2, BLOCKS, NM], F32))
        args_ready, exps_ready, ones_added, logs_ready, steps_ready, sums_ready, lists_ready, done = (
            sem("gt_args"), sem("gt_exps"), sem("gt_ones"), sem("gt_logs"), sem("gt_steps"), sem("gt_sums"), sem("gt_lists"), sem("gt_done"))
        block = ctx.enter_context(nc.Block())
        G, sm, rows = t["gates"], t["small"], t["rows"]

        def per_block(ap):
            return ap.unsqueeze(1).to_broadcast([P, BLOCKS, ap.shape[1]])

        @block.vector
        def _(dve):
            nc.vector.tensor_tensor(raw[:, :, 0:NS], sm[:, :, 0:NS], per_block(rows[:, R_DTB:R_DTB + NS]), ALU.add)
            nc.vector.tensor_scalar(fb[:, :], rows[:, R_FB:R_FB + NM], -1.0, None, ALU.mult)
            dve.drain()
            nc.vector.scalar_tensor_tensor(raw[:, :, NS:W], sm[:, :, NS + NM:NS + 2 * NM], -1.0, per_block(fb[:, :]),
                                           ALU.mult, ALU.add)
            nc.vector.tensor_tensor(G[:, :, G_LI:G_LI + NM], sm[:, :, NS:NS + NM], per_block(rows[:, R_IB:R_IB + NM]), ALU.add)
            dve.drain()
            nc.vector.tensor_scalar(u[:, :, :], raw[:, :, :], -1.0, None, ALU.mult)
            dve.drain()
            nc.vector.tensor_tensor(nabs[:, :, :], u[:, :, :], raw[:, :, :], ALU.min).then_inc(args_ready, 1)
            dve.wait_ge(exps_ready, 1)
            nc.vector.tensor_scalar(u[:, :, :], y[:, :, :], 1.0, None, ALU.add).then_inc(ones_added, 1)
            dve.wait_ge(ones_added, 1)
            nc.vector.tensor_scalar(nabs[:, :, :], u[:, :, :], 1.0, None, ALU.subtract)
            dve.drain()
            nc.vector.tensor_tensor(nabs[:, :, :], y[:, :, :], nabs[:, :, :], ALU.subtract)
            dve.drain()
            dve.wait_ge(logs_ready, 1)
            nc.vector.reciprocal(y[:, :, :], u[:, :, :])
            dve.drain()
            nc.vector.tensor_tensor(nabs[:, :, :], nabs[:, :, :], y[:, :, :], ALU.mult)
            dve.drain()
            nc.vector.tensor_tensor(nabs[:, :, :], nabs[:, :, :], lnu[:, :, :], ALU.add)
            dve.drain()
            nc.vector.scalar_tensor_tensor(nabs[:, :, :], raw[:, :, :], 0.0, nabs[:, :, :], ALU.max, ALU.add)
            dve.drain()
            nc.vector.tensor_copy(G[:, :, G_DT:G_DT + NS], nabs[:, :, 0:NS])
            nc.vector.tensor_scalar(G[:, :, G_LF:G_LF + NM], nabs[:, :, NS:W], -1.0, None, ALU.mult)
            nc.vector.scalar_tensor_tensor(G[:, :, G_DA:G_DA + NS], nabs[:, :, 0:NS], -1.0, per_block(a[:, :]),
                                           ALU.mult, ALU.mult)
            dve.drain()
            dve.sem_inc(steps_ready, 1)
            dve.wait_ge(sums_ready, 1)
            nc.vector.tensor_copy(tmp[:, :, :], ps[:, :, :])
            nc.vector.tensor_scalar(G[:, :, G_NACS:G_NACS + NS], ps[:, :, :], -1.0, None, ALU.mult)
            nc.vector.tensor_copy(G[:, :, G_BC:G_BC + NM], pm[:, 0])
            nc.vector.tensor_copy(G[:, :, G_TOT:G_TOT + NM], pm[:, 1])
            dve.drain()
            nc.vector.tensor_tensor(tm2[:, :, :], pt[:, :, :], tmp[:, :, :], ALU.subtract)
            nc.vector.tensor_tensor(G[:, :, G_E:G_E + NM], G[:, :, G_LI:G_LI + NM], G[:, :, G_BC:G_BC + NM], ALU.subtract)
            dve.drain()
            dve.sem_inc(lists_ready, 1)
            dve.wait_ge(done, 1)
            nc.vector.tensor_tensor(G[:, :, G_WD:G_WD + NS], G[:, :, G_WD:G_WD + NS], G[:, :, G_DT:G_DT + NS], ALU.mult)

        @block.scalar
        def _(act):
            nc.scalar.activation(a[:, :], rows[:, R_ALOG:R_ALOG + NS], ACT.Exp)
            act.wait_ge(args_ready, 1)
            nc.scalar.activation(y[:, :, :], nabs[:, :, :], ACT.Exp).then_inc(exps_ready, 1)
            act.wait_ge(ones_added, 1)
            nc.scalar.activation(lnu[:, :, :], u[:, :, :], ACT.Ln).then_inc(logs_ready, 1)
            act.wait_ge(lists_ready, 1)
            nc.scalar.activation(G[:, :, G_EA:G_EA + NS], tmp[:, :, :], ACT.Exp)
            nc.scalar.activation(G[:, :, G_ED:G_ED + NS], pt[:, :, :], ACT.Exp)
            nc.scalar.activation(G[:, :, G_WD:G_WD + NS], tm2[:, :, :], ACT.Exp).then_inc(done, 1)

        @block.tensor
        def _(pe):
            pe.wait_ge(steps_ready, 1)
            for d, tri in enumerate((t["triF"], t["triB"])):
                for b in range(BLOCKS):
                    c = d * HS
                    nc.tensor.matmul(ps[:, b, c:c + HS], tri[:, :], G[:, b, G_DA + c:G_DA + c + HS], start=True, stop=True)
                    m = d * HM
                    nc.tensor.matmul(pm[:, 0, b, m:m + HM], tri[:, :], G[:, b, G_LF + m:G_LF + m + HM], start=True, stop=True)
            for b in range(BLOCKS):
                nc.tensor.matmul(pt[:, b, :], t["ones"][:, :], G[:, b, G_DA:G_DA + NS], start=True, stop=True)
                last = nc.tensor.matmul(pm[:, 1, b, :], t["ones"][:, :], G[:, b, G_LF:G_LF + NM], start=True, stop=True)
            last.then_inc(sums_ready, 1)


def scan(nc, dr, t, kind):
    full = kind != "back"
    dirs = (0, 1) if full else (1,)
    steps = {"prompt": (0, 1), "back": (1,), "sample": (0,)}[kind]
    prior = kind != "prompt"
    N = {"prompt": 1, "back": CHUNKS - 1, "sample": CHUNKS}[kind]
    tri, mask_t, mask = (t["triF"], t["triB"]), (t["maskF"], t["maskB"]), (t["maskB"], t["maskF"])
    with ExitStack() as ctx:
        pre = kind[0] + "_"
        sb = lambda n, s, d=F32: ctx.enter_context(nc.sbuf_tensor(pre + n, s, d))
        sem = semaphores(nc, ctx, pre)

        xbcT, qkT, v, g = sb("xbcT", [P, 16, P]), sb("qkT", [P, 16, P]), sb("v", [P, D]), sb("g", [P, G_N])
        xs, Bt, Kt = sb("xs", [P, D]), sb("Bt", [P, NG, P]), sb("Kt", [P, HM, DM])
        L, W = sb("L", [P, 2, 2, 4, P]), sb("W", [P, 2, 2, 4, P])
        y, yt, xw = sb("y", [P, D]), sb("yt", [P, D]), sb("xw", [P, 2, D])
        H = [sb(f"H{d}", [P, D]) for d in range(2)]
        C = [sb(f"C{d}", [P, HM, 2, CE]) for d in range(2)]
        mp, emax, me, mx, nmx, mn, rs, den, r, rw = [sb(n, [P, 2, HM]) for n in (
            "mp", "emax", "me", "mx", "nmx", "mn", "rs", "den", "r", "rw")]
        args, ex = sb("args", [P, 4, 2, HM]), sb("ex", [P, 4, 2, HM])
        WA, WI, DN, KW = range(4)
        Em, Pc, PcT = sb("Em", [P, 2, HM, P]), sb("Pc", [P, HM, P]), sb("PcT", [P, HM, P])
        hm, Ks = sb("hm", [P, HM, DM]), sb("Ks", [P, 2, HM, DM])
        bank = [ctx.enter_context(nc.psum_tensor(f"{pre}bank{i}", [P, 1024], F32)) for i in range(4)]
        half = [bank[i // 2][:, (i % 2) * 512:(i % 2) * 512 + 512] for i in range(8)]
        x_in, qk_in, v_in, cur_ready, init_ready = sem("x_in"), sem("qk_in"), sem("v_in"), sem("cur_ready"), sem("init_ready")
        xs_turned, B_turned, xs_ready, B_ready, K_turned, K_ready = (
            sem("xs_turned"), sem("B_turned"), sem("xs_ready"), sem("B_ready"), sem("K_turned"), sem("K_ready"))
        xw_ready, state_mm, H_new = sem("xw_ready"), [sem("state_mm0"), sem("state_mm1")], [sem("H_new0"), sem("H_new1")]
        E_rows, E_used, args_ready, ex_ready, Ks_ready = sem("E_rows"), sem("E_used"), sem("args_ready"), sem("ex_ready"), sem("Ks_ready")
        mstate_mm, C_new = sem("mstate_mm"), sem("C_new")
        chunk_done = sem("chunk_done")
        if prior:
            state_in = sem("state_in")
        if kind == "sample":
            H_in, C_in, m_in = sem("H_in"), sem("C_in"), sem("m_in")
        if kind == "back":
            stored = sem("stored")
        if kind == "prompt":
            state_out = sem("state_out")
        sp_passed, dve_passed = sem("sp_passed"), sem("dve_passed")
        if full:
            y_out, hm_out = sem("y_out"), sem("hm_out")
            scores, decay, decays, W_ready, y_mm, y_done = (
                sem("scores"), sem("decay"), sem("decays"), sem("W_ready"), sem("y_mm"), sem("y_done"))
            yoff_mm, yoff_used = [sem("yoff_mm0"), sem("yoff_mm1")], [sem("yoff_used0"), sem("yoff_used1")]
            qk_mm, X_ready, P_done, inter_mm, inter_used, P_turned, PT_ready, hv_mm, hm_done, P_mixed, qn_used = (
                sem("qk_mm"), sem("X_ready"), sem("P_done"), sem("inter_mm"), sem("inter_used"), sem("P_turned"), sem("PT_ready"),
                sem("hv_mm"), sem("hm_done"), sem("P_mixed"), sem("qn_used"))
        block = ctx.enter_context(nc.Block())
        NM = len(steps) * HM
        def loop(eng, body):
            if N == 1:
                body(0)
            else:
                with eng.Fori(0, N) as i:
                    body(i)

        def blk(i):
            return {"prompt": i, "back": CHUNKS - i, "sample": i + 1}[kind]

        def at(ap, i):
            return ap[i] if isinstance(i, int) else row(ap[bass.ds(i, 1)])

        flat_c = lambda d: C[d][:, :, :, :].rearrange("p h k c -> p (h k c)")

        @block.sync
        def _(sp):
            def tok(i):
                return slice(0, P) if kind == "prompt" else slice(blk(i) * P, blk(i) * P + P) if isinstance(i, int) else bass.ds(blk(i) * P, P)

            def load_x(i):
                sp.dma_start(xbcT[:, :, :], dr["xbcT"].rearrange("m p t -> p m t")[:, :, tok(i)]).then_inc(x_in, 16)
                if kind == "sample":
                    sp.dma_start(H[1][:, :], at(dr["back_ssd"], CHUNKS - 1 - i)).then_inc(H_in, 16)

            def load_m(i):
                if kind == "sample":
                    sp.dma_start(mp[:, 1, :], at(dr["back_m"], CHUNKS - 1 - i)).then_inc(m_in, 16)

            def load_qk(i):
                sp.dma_start(qkT[:, :, :], dr["qkT"].rearrange("m p t -> p m t")[:, :, tok(i)]).then_inc(qk_in, 16)
                if kind == "sample":
                    sp.dma_start(flat_c(1), at(dr["back_c"], CHUNKS - 1 - i)).then_inc(C_in, 16)

            def load_v(i):
                sp.dma_start(v[:, :], at(dr["proj"], blk(i))[:, COL_V:COL_V + D]).then_inc(v_in, 16)

            load_x(0)
            if prior:
                d = steps[0]
                sp.dma_start(H[d][:, :], dr["state_ssd"][d]).then_inc(state_in, 16)
                sp.dma_start(flat_c(d), dr["state_c"][d]).then_inc(state_in, 16)
            load_m(0)
            load_qk(0)
            load_v(0)

            def store_state(i):
                sp.dma_start(at(dr["back_ssd"], i), H[1][:, :]).then_inc(stored, 16)
                sp.dma_start(at(dr["back_c"], i), flat_c(1)).then_inc(stored, 16)
                sp.dma_start(at(dr["back_m"], i), mp[:, 1, :]).then_inc(stored, 16)

            def body(i, more):
                if more:
                    sp.wait_ge(yoff_mm[1] if full else B_turned, i + 1)
                    sp.sem_inc(sp_passed, 1)
                    load_x(i + 1)
                if full:
                    sp.wait_ge(y_done, i + 1)
                    sp.sem_inc(sp_passed, 1)
                    sp.dma_start(at(dr["y_ssd"], blk(i)), y[:, :]).then_inc(y_out, 16)
                if more:
                    if kind == "sample":
                        sp.wait_ge(args_ready, i + 1)
                        sp.sem_inc(sp_passed, 1)
                        load_m(i + 1)
                    sp.wait_ge(inter_mm if full else K_turned, i + 1)
                    sp.sem_inc(sp_passed, 1)
                    load_qk(i + 1)
                if full:
                    sp.wait_ge(hm_done, i + 1)
                    sp.sem_inc(sp_passed, 1)
                    sp.dma_start(at(dr["y_mlstm"], blk(i)), hm[:, :, :].rearrange("p h c -> p (h c)")).then_inc(hm_out, 16)
                if more:
                    sp.wait_ge(mstate_mm, i * NM + NM)
                    sp.sem_inc(sp_passed, 1)
                    load_v(i + 1)
                if kind == "back":
                    sp.wait_ge(chunk_done, i + 2)
                    sp.sem_inc(sp_passed, 1)
                    store_state(i + 1)

            if kind == "back":
                sp.wait_ge(state_in, 32)
                sp.wait_ge(init_ready, 1)
                store_state(0)
            if N > 1:
                with sp.Fori(0, N - 1) as i:
                    body(i, True)
            body(N - 1, False)
            if kind == "prompt":
                sp.wait_ge(chunk_done, 2)
                for d in range(2):
                    sp.dma_start(dr["out_ssd"][d], H[d][:, :]).then_inc(state_out, 16)
                    sp.dma_start(dr["out_c"][d], flat_c(d)).then_inc(state_out, 16)
                sp.dma_start(dr["out_m"], mp[0:1, :, :].rearrange("p d h -> p (d h)")).then_inc(state_out, 16)
                sp.wait_ge(state_out, 80)
            if kind == "back":
                sp.wait_ge(stored, 48 * (N + 1))
            if full:
                sp.wait_ge(y_out, 16 * (N + 1))
                sp.wait_ge(hm_out, 16 * (N + 1))

        @block.tensor
        def _(pe):
            ident = t["ident"]

            def body(i):
                pe.wait_ge(x_in, i * 16 + 16)
                pe.wait_ge(cur_ready, i + 1)
                pe.wait_ge(chunk_done, i + 1)
                for k in range(KT):
                    last = nc.tensor.transpose(bank[0][:, k * P:(k + 1) * P], xbcT[:, k, :], ident[:, :])
                last.then_inc(xs_turned, 1)
                for k in range(NG):
                    last = nc.tensor.transpose(half[2][:, k * P:(k + 1) * P], xbcT[:, KT + k, :], ident[:, :])
                last.then_inc(B_turned, 1)
                if full:
                    for q in range(NG):
                        last = nc.tensor.matmul(half[3][:, q * P:(q + 1) * P], xbcT[:, KT + q, :], xbcT[:, KT + NG + q, :],
                                                start=True, stop=True)
                    last.then_inc(scores, 1)

                    def decay_rows(q):
                        if q:
                            pe.wait_ge(decays, i * NG + q)
                        for d in range(2):
                            out = half[4 + d].rearrange("p (h s) -> p h s", h=4)
                            nc.tensor.matmul(out, ident[:, :], mask_t[d][:, :].unsqueeze(1).to_broadcast([P, 4, P]),
                                             start=True, stop=False)
                            for h in range(4):
                                c = d * HS + q * 4 + h
                                last = nc.tensor.matmul(out[:, h, :], g[:, G_NACS + c:G_NACS + c + 1].to_broadcast([P, P]),
                                                        t["nident"][:, :], start=False, stop=(h == 3))
                        last.then_inc(decay, 1)

                    decay_rows(0)
                    pe.wait_ge(xs_ready, i + 1)
                    for q in range(NG):
                        if q + 1 < NG:
                            decay_rows(q + 1)
                        pe.wait_ge(W_ready, i * NG + (q + 1))
                        for h in range(4):
                            c = (q * 4 + h) * PS
                            for d in range(2):
                                last = nc.tensor.matmul(bank[3][:, c:c + PS], W[:, q % 2, d, h, :], xs[:, c:c + PS],
                                                        start=(d == 0), stop=(d == 1))
                        last.then_inc(y_mm, 1)
                    if prior:
                        pe.wait_ge(state_in, 32)
                        pe.wait_ge(H_in, i * 16 + 16)
                        for d in range(2):
                            for q in range(NG):
                                last = nc.tensor.matmul(bank[d][:, q * 256:(q + 1) * 256], xbcT[:, KT + NG + q, :],
                                                        H[d][:, q * 256:(q + 1) * 256], start=True, stop=True)
                            last.then_inc(yoff_mm[d], 1)
                pe.wait_ge(B_ready, i + 1)
                pe.wait_ge(xw_ready, i + 1)
                for n, d in enumerate(steps):
                    if n == 0 and full:
                        pe.wait_ge(decays, i * NG + NG)
                    if n == 1:
                        pe.wait_ge(xs_ready, i + 1)
                        if full and prior:
                            pe.wait_ge(yoff_used[0], i + 1)
                    to = bank[(2, 0)[n]]
                    for q in range(NG):
                        last = nc.tensor.matmul(to[:, q * 256:(q + 1) * 256], Bt[:, q, :], xw[:, d, q * 256:(q + 1) * 256],
                                                start=True, stop=True)
                    last.then_inc(state_mm[d], 1)
                if full and prior:
                    pe.wait_ge(yoff_used[1], i + 1)
                if full:
                    pe.wait_ge(W_ready, i * NG + NG)
                pe.wait_ge(qk_in, i * 16 + 16)
                for k in range(KT):
                    last = nc.tensor.transpose(bank[1][:, k * P:(k + 1) * P], qkT[:, KT + k, :], ident[:, :])
                last.then_inc(K_turned, 1)
                pe.wait_ge(H_new[steps[0]], i + 1)
                for d in dirs:
                    for h in range(HM):
                        c = G_E + d * HM + h
                        last = nc.tensor.matmul(half[4 + d][:, h * P:(h + 1) * P], g[:, c:c + 1].to_broadcast([P, P]), ident[:, :],
                                                start=True, stop=True)
                last.then_inc(E_rows, 1)
                if full:
                    pe.wait_ge(y_done, i + 1)
                    for h in range(HM):
                        for k in range(2):
                            last = nc.tensor.matmul(half[6][:, h * P:(h + 1) * P], qkT[:, 2 * h + k, :], qkT[:, KT + 2 * h + k, :],
                                                    start=(k == 0), stop=(k == 1))
                    last.then_inc(qk_mm, 1)
                    if prior:
                        if len(steps) == 2:
                            pe.wait_ge(H_new[steps[1]], i + 1)
                        pe.wait_ge(K_ready, i + 1)
                        pe.wait_ge(C_in, i * 16 + 16)
                        for d in range(2):
                            for h in range(HM):
                                for k in range(2):
                                    nc.tensor.matmul(bank[d][:, h * DM:(h + 1) * DM], qkT[:, 2 * h + k, :], C[d][:, h, k, 0:DM],
                                                     start=(k == 0), stop=(k == 1))
                                for k in range(2):
                                    last = nc.tensor.matmul(half[7][:, d * HM + h:d * HM + h + 1], qkT[:, 2 * h + k, :],
                                                            C[d][:, h, k, DM:CE], start=(k == 0), stop=(k == 1))
                        last.then_inc(inter_mm, 1)
                    pe.wait_ge(P_mixed, i + 1)
                    for h in range(HM):
                        last = nc.tensor.transpose(half[4][:, h * P:(h + 1) * P], Pc[:, h, :], ident[:, :])
                    last.then_inc(P_turned, 1)
                    pe.wait_ge(PT_ready, i + 1)
                    pe.wait_ge(v_in, i * 16 + 16)
                    for h in range(HM):
                        last = nc.tensor.matmul(bank[3][:, h * DM:(h + 1) * DM], PcT[:, h, :], v[:, h * DM:(h + 1) * DM],
                                                start=True, stop=True)
                    last.then_inc(hv_mm, 1)
                    if prior:
                        pe.wait_ge(inter_used, i + 1)
                pe.wait_ge(Ks_ready, i + 1)
                if not full:
                    pe.wait_ge(v_in, i * 16 + 16)
                if kind == "prompt":
                    pe.wait_ge(H_new[1], i + 1)
                for n in range(NM):
                    d, h = steps[n // HM], n % HM
                    for k in range(2):
                        nc.tensor.matmul(half[5][:, 2 * n + k:2 * n + k + 1], Ks[:, d, h, k * P:(k + 1) * P],
                                         t["ones"][:, 0:1], start=True, stop=True)
                for n in range(NM):
                    d, h = steps[n // HM], n % HM
                    if n >= 4:
                        pe.wait_ge(C_new, i * NM + (n - 3))
                    for k in range(2):
                        last = nc.tensor.matmul(half[n % 4][:, k * DM:(k + 1) * DM], Ks[:, d, h, k * P:(k + 1) * P],
                                                v[:, h * DM:(h + 1) * DM], start=True, stop=True)
                    last.then_inc(mstate_mm, 1)

            loop(pe, body)

        @block.scalar
        def _(act):
            def body(i):
                act.wait_ge(xs_turned, i + 1)
                nc.scalar.copy(xs[:, :], bank[0][:, :]).then_inc(xs_ready, 1)
                act.wait_ge(B_turned, i + 1)
                nc.scalar.copy(Bt[:, :, :].rearrange("p q n -> p (q n)"), half[2]).then_inc(B_ready, 1)
                if full:
                    for q in range(NG):
                        act.wait_ge(decay, i * NG + (q + 1))
                        if q >= 2:
                            act.wait_ge(W_ready, i * NG + (q - 1))
                        for d in range(2):
                            for h in range(4):
                                c = G_NACS + d * HS + q * 4 + h
                                last = nc.scalar.activation(L[:, q % 2, d, h, :], half[4 + d][:, h * P:(h + 1) * P], ACT.Exp,
                                                            bias=g[:, c:c + 1])
                        last.then_inc(decays, 1)
                act.wait_ge(K_turned, i + 1)
                nc.scalar.copy(Kt[:, :, :].rearrange("p h c -> p (h c)"), bank[1][:, :]).then_inc(K_ready, 1)
                act.wait_ge(args_ready, i + 1)
                nc.scalar.activation(ex[:, :, :, :], args[:, :, :, :], ACT.Exp).then_inc(ex_ready, 1)
                if full:
                    for d in range(2):
                        for h in range(HM):
                            last = nc.scalar.activation(Em[:, d, h, :], Em[:, d, h, :], ACT.Exp, bias=nmx[:, d, h:h + 1])
                    last.then_inc(X_ready, 1)
                    act.wait_ge(P_turned, i + 1)
                    nc.scalar.copy(PcT[:, :, :].rearrange("p h s -> p (h s)"), half[4]).then_inc(PT_ready, 1)

            loop(act, body)

        @block.vector
        def _(dve):
            if kind == "back":
                nc.vector.tensor_copy(mp[:, 1, :], t["rows"][:, R_M0 + HM:R_M0 + 2 * HM])
            elif kind == "sample":
                nc.vector.tensor_copy(mp[:, 0, :], t["rows"][:, R_M0:R_M0 + HM])
            else:
                nc.vector.memset(mp[:, :, :], 0.0)
            nc.vector.memset(args[:, :, :, :], 0.0)
            dve.drain()
            dve.sem_inc(init_ready, 1)
            dve.sem_inc(chunk_done, 1)
            if full:
                dve.sem_inc(y_out, 16)
                dve.sem_inc(hm_out, 16)
            sd = slice(dirs[0], dirs[-1] + 1)

            def heads(ap):
                return ap.rearrange("p (h c) -> p h c", c=PS)

            def body(i):
                b = i if kind == "prompt" else dve.snap(blk(i))
                G = t["gates"]
                nc.vector.tensor_copy(g[:, :], G[:, 0, :] if kind == "prompt" else G[:, bass.ds(b, 1), :].rearrange(
                    "p o n -> p (o n)"))
                dve.drain()
                dve.sem_inc(cur_ready, 1)
                dve.wait_ge(xs_ready, i + 1)
                for d in steps:
                    c = G_WD + d * HS
                    nc.vector.tensor_tensor(heads(xw[:, d, :]), heads(xs[:, :]), bc_last(g[:, c:c + HS], PS), ALU.mult)
                dve.drain()
                dve.sem_inc(xw_ready, 1)
                if full:
                    for q in range(NG):
                        dve.wait_ge(decays, i * NG + (q + 1))
                        dve.wait_ge(scores, i + 1)
                        if q >= 2:
                            dve.wait_ge(y_mm, i * NG + (q - 1))
                        for d in range(2):
                            for h in range(4):
                                c = G_DT + d * HS + q * 4 + h
                                last = nc.vector.scalar_tensor_tensor(W[:, q % 2, d, h, :], L[:, q % 2, d, h, :], g[:, c:c + 1],
                                                                      half[3][:, q * P:(q + 1) * P], ALU.mult, ALU.mult)
                        last.then_inc(W_ready, 1)
                    nc.vector.tensor_tensor(heads(yt[:, :]), heads(xs[:, :]), bc_last(t["skip"][:, :], PS), ALU.mult)
                    dve.drain()
                    dve.wait_ge(y_mm, i * NG + NG)
                    dve.wait_ge(y_out, i * 16 + 16)
                    nc.vector.tensor_tensor(y[:, :], yt[:, :], bank[3][:, :], ALU.add)
                    if prior:
                        for d in range(2):
                            dve.drain()
                            dve.wait_ge(yoff_mm[d], i + 1)
                            c = G_EA + d * HS
                            nc.vector.tensor_tensor(heads(yt[:, :]), heads(bank[d][:, :]), bc_last(g[:, c:c + HS], PS),
                                                    ALU.mult).then_inc(yoff_used[d], 1)
                            dve.drain()
                            nc.vector.tensor_tensor(y[:, :], y[:, :], yt[:, :], ALU.add)
                    dve.drain()
                    dve.sem_inc(y_done, 1)
                if prior:
                    dve.wait_ge(state_in, 32)
                if kind == "back":
                    dve.wait_ge(stored, i * 48 + 48)
                for n, d in enumerate(steps):
                    c = G_ED + d * HS
                    dve.wait_ge(state_mm[d], i + 1)
                    if prior:
                        nc.vector.tensor_tensor(heads(H[d][:, :]), heads(H[d][:, :]), bc_last(g[:, c:c + HS], PS), ALU.mult)
                        dve.drain()
                        nc.vector.tensor_tensor(H[d][:, :], H[d][:, :], bank[(2, 0)[n]][:, :], ALU.add).then_inc(H_new[d], 1)
                    else:
                        nc.vector.tensor_copy(H[d][:, :], bank[(2, 0)[n]][:, :]).then_inc(H_new[d], 1)
                dve.wait_ge(E_rows, i + 1)
                if kind == "sample":
                    dve.wait_ge(m_in, i * 16 + 16)
                for d in dirs:
                    E = half[4 + d].rearrange("p (h s) -> p h s", h=HM)
                    nc.vector.tensor_reduce(emax[:, d, :], E, AX, ALU.max)
                    if full:
                        nc.vector.tensor_tensor(Em[:, d, :, :], E, mask[d][:, :].unsqueeze(1).to_broadcast([P, HM, P]), ALU.add)
                        dve.drain()
                        nc.vector.tensor_reduce(me[:, d, :], Em[:, d, :, :], AX, ALU.max)
                dve.drain()
                nc.vector.tensor_tensor(mn[:, sd, :], mp[:, sd, :], emax[:, sd, :], ALU.max)
                if full:
                    nc.vector.tensor_tensor(mx[:, :, :], mp[:, :, :], me[:, :, :], ALU.max)
                dve.drain()
                gd = lambda c: g[:, c:c + 2 * HM].rearrange("p (d h) -> p d h", d=2)[:, sd, :]
                nc.vector.tensor_tensor(args[:, WA, sd, :], mp[:, sd, :], mn[:, sd, :], ALU.subtract)
                nc.vector.tensor_tensor(args[:, KW, sd, :], gd(G_E), mn[:, sd, :], ALU.subtract)
                if full:
                    nc.vector.tensor_scalar(nmx[:, :, :], mx[:, :, :], -1.0, None, ALU.mult)
                    nc.vector.tensor_tensor(args[:, WI, :, :], mp[:, :, :], mx[:, :, :], ALU.subtract)
                    dve.drain()
                    nc.vector.tensor_tensor(args[:, DN, :, :], nmx[:, :, :], gd(G_BC), ALU.subtract)
                dve.drain()
                nc.vector.tensor_tensor(mp[:, sd, :], mn[:, sd, :], gd(G_TOT), ALU.add)
                dve.drain()
                dve.sem_inc(args_ready, 1)
                dve.wait_ge(ex_ready, i + 1)
                dve.wait_ge(K_ready, i + 1)
                for d in steps:
                    nc.vector.scalar_tensor_tensor(Ks[:, d], Kt[:, :, :], DM ** -0.5, bc_last(ex[:, KW, d, :], DM), ALU.mult, ALU.mult)
                dve.drain()
                dve.sem_inc(Ks_ready, 1)
                if full:
                    dve.wait_ge(qk_mm, i + 1)
                    dve.wait_ge(X_ready, i + 1)
                    for d in range(2):
                        for h in range(HM):
                            nc.vector.scalar_tensor_tensor(Em[:, d, h, :], half[6][:, h * P:(h + 1) * P], DM ** -0.5, Em[:, d, h, :],
                                                           ALU.mult, ALU.mult, accum_out=rs[:, d, h:h + 1])
                    dve.drain()
                    if prior:
                        dve.wait_ge(inter_mm, i + 1)
                        nc.vector.tensor_tensor(den[:, :, :], half[7][:, 0:2 * HM].rearrange("p (d h) -> p d h", d=2),
                                                ex[:, WI, :, :], ALU.mult)
                        dve.drain()
                        nc.vector.tensor_tensor(rs[:, :, :], rs[:, :, :], den[:, :, :], ALU.add)
                        dve.drain()
                    nc.vector.scalar_tensor_tensor(den[:, :, :], rs[:, :, :], -1.0, rs[:, :, :], ALU.mult, ALU.max)
                    dve.drain()
                    nc.vector.tensor_tensor(den[:, :, :], den[:, :, :], ex[:, DN, :, :], ALU.max)
                    dve.drain()
                    nc.vector.reciprocal(r[:, :, :], den[:, :, :])
                    dve.drain()
                    nc.vector.tensor_tensor(rw[:, :, :], r[:, :, :], ex[:, WI, :, :], ALU.mult)
                    for h in range(HM):
                        nc.vector.tensor_scalar(Pc[:, h, :], Em[:, 0, h, :], r[:, 0, h:h + 1], None, ALU.mult)
                    dve.drain()
                    for h in range(HM):
                        nc.vector.scalar_tensor_tensor(Pc[:, h, :], Em[:, 1, h, :], r[:, 1, h:h + 1], Pc[:, h, :], ALU.mult, ALU.add)
                    dve.drain()
                    dve.sem_inc(P_mixed, 1)
                    dve.wait_ge(hm_out, i * 16 + 16)
                    if prior:
                        for h in range(HM):
                            nc.vector.tensor_scalar(hm[:, h, :], bank[0][:, h * DM:(h + 1) * DM], rw[:, 0, h:h + 1], None, ALU.mult)
                        dve.drain()
                        for h in range(HM):
                            nc.vector.scalar_tensor_tensor(hm[:, h, :], bank[1][:, h * DM:(h + 1) * DM], rw[:, 1, h:h + 1],
                                                           hm[:, h, :], ALU.mult, ALU.add)
                        dve.drain()
                        dve.sem_inc(inter_used, 1)
                    dve.wait_ge(hv_mm, i + 1)
                    hv = bank[3][:, :].rearrange("p (h c) -> p h c", c=DM)
                    if prior:
                        nc.vector.tensor_tensor(hm[:, :, :], hm[:, :, :], hv, ALU.add).then_inc(hm_done, 1)
                    else:
                        nc.vector.tensor_copy(hm[:, :, :], hv).then_inc(hm_done, 1)
                for n in range(NM):
                    d, h = steps[n // HM], n % HM
                    dve.wait_ge(mstate_mm, i * NM + (n + 1))
                    new = half[n % 4].rearrange("p (k c) -> p k c", k=2)
                    norm = half[5][:, 2 * n:2 * n + 2].unsqueeze(2)
                    if prior:
                        nc.vector.scalar_tensor_tensor(C[d][:, h, :, 0:DM], C[d][:, h, :, 0:DM], ex[:, WA, d, h:h + 1], new,
                                                       ALU.mult, ALU.add)
                        nc.vector.scalar_tensor_tensor(C[d][:, h, :, DM:CE], C[d][:, h, :, DM:CE], ex[:, WA, d, h:h + 1], norm,
                                                       ALU.mult, ALU.add).then_inc(C_new, 1)
                    else:
                        nc.vector.tensor_copy(C[d][:, h, :, 0:DM], new)
                        nc.vector.tensor_copy(C[d][:, h, :, DM:CE], norm).then_inc(C_new, 1)
                dve.drain()
                dve.sem_inc(chunk_done, 1)

            loop(dve, body)


def skip_sum(nc, t):
    with nc.Block() as block:
        @block.vector
        def _(dve):
            r = t["rows"]
            nc.vector.tensor_tensor(t["skip"][:, :], r[:, R_SKIP:R_SKIP + HS], r[:, R_SKIP + HS:R_SKIP + 2 * HS], ALU.add)
            nc.vector.tensor_scalar(t["nident"][:, :], t["ident"][:, :], -1.0, None, ALU.mult)


def merge(nc, dr, t):
    with ExitStack() as ctx:
        sb = lambda n, s, d=F32: ctx.enter_context(nc.sbuf_tensor("m_" + n, s, d))
        sem = semaphores(nc, ctx, "m_")
        wts = sb("w", [P, 3, KT, D])
        y, z, hm, o = sb("y", [P, D]), sb("z", [P, D]), sb("hm", [P, HM, DM]), sb("o", [P, HM, DM])
        sz, yn, hn = sb("sz", [P, D]), sb("yn", [P, D]), sb("hn", [P, HM, DM])
        yT, hT = sb("yT", [P, KT, P]), sb("hT", [P, KT, P])
        mg, x = sb("mg", [P, 2, D]), sb("x", [P, D])
        rows = sb("rows", [P, 3, D])
        mix, mixT, gated, h2 = sb("mix", [P, D]), sb("mixT", [P, KT, P]), sb("gated", [P, D]), sb("h2", [P, D])
        sq = sb("sq", [P, D])
        ss, root, rr = sb("ss", [P, 7]), sb("root", [P, 7]), sb("rr", [P, 7])
        bank = [ctx.enter_context(nc.psum_tensor(f"m_bank{i}", [P, 1024], F32)) for i in range(4)]
        w_in = [sem(f"w_in{k}") for k in range(3)]
        head_in = sem("head_in")
        branches_in, gates_in, x_in = sem("branches_in"), sem("gates_in"), sem("x_in")
        branch_sig, gate_sig, y_gated, branch_sums, branch_ms, branch_root, normed, turned, gained = (
            sem("branch_sig"), sem("gate_sig"), sem("y_gated"), sem("branch_sums"), sem("branch_ms"), sem("branch_root"),
            sem("normed"), sem("turned"), sem("gained"))
        branch_mm, mixed, mix_turned, mixT_ready, out_mm = sem("branch_mm"), sem("mixed"), sem("mix_turned"), sem("mixT_ready"), sem("out_mm")
        out_sums, out_ms, out_root, x1_ready, x1_sums, x1_ms, x1_root, h2_ready = (
            sem("out_sums"), sem("out_ms"), sem("out_root"), sem("x1_ready"), sem("x1_sums"), sem("x1_ms"), sem("x1_root"), sem("h2_ready"))
        x1_out, h2_out, sp_passed = sem("x1_out"), sem("h2_out"), sem("sp_passed")
        out_free = sem("out_free")
        block = ctx.enter_context(nc.Block())
        flat = lambda ap: ap.rearrange("p h c -> p (h c)")

        def turns(eng, ahead, turn):
            ahead(0)
            with eng.Fori(0, BLOCKS - 1) as i:
                turn(i, True)
            turn(BLOCKS - 1, False)

        @block.sync
        def _(sp):
            def of(ap, b):
                return ap[b] if isinstance(b, int) else row(ap[bass.ds(b, 1)])

            def load_branches(b):
                pr = of(dr["proj"], b)
                sp.dma_start(y[:, :], of(dr["y_ssd"], b)).then_inc(branches_in, 16)
                sp.dma_start(z[:, :], pr[:, COL_Z:COL_Z + D]).then_inc(branches_in, 16)
                sp.dma_start(flat(hm[:, :, :]), of(dr["y_mlstm"], b)).then_inc(branches_in, 16)
                sp.dma_start(flat(o[:, :, :]), pr[:, COL_O:COL_O + D]).then_inc(branches_in, 16)

            def load_gates(b):
                sp.dma_start(flat(mg[:, :, :]), of(dr["proj"], b)[:, COL_M:COL_M + 2 * D]).then_inc(gates_in, 16)

            def load_x(b):
                sp.dma_start(x[:, :], of(dr["x"], b)).then_inc(x_in, 16)
                r = of(dr["mod_rows"], b)[0:1, V_GATE_A * D:(V_SHIFT_F + 1) * D]
                sp.dma_start(flat(rows[:, :, :]), r.partition_broadcast(P)).then_inc(x_in, 16)

            def turn(b, two_more, one_more):
                if two_more:
                    sp.wait_ge(normed, b + 2)
                    sp.sem_inc(sp_passed, 1)
                    load_branches(b + 2)
                if one_more:
                    sp.wait_ge(mixed, b + 1)
                    sp.sem_inc(sp_passed, 1)
                    load_gates(b + 1)
                sp.wait_ge(x1_ready, b + 1)
                sp.sem_inc(sp_passed, 1)
                sp.dma_start(of(dr["x1"], b), x[:, :]).then_inc(x1_out, 16)
                sp.wait_ge(h2_ready, b + 1)
                sp.sem_inc(sp_passed, 1)
                sp.dma_start(of(dr["h2"], b), h2[:, :]).then_inc(h2_out, 16)
                sp.wait_ge(x1_out, b * 16 + 16)
                sp.sem_inc(sp_passed, 1)
                if one_more:
                    load_x(b + 1)

            load_branches(0)
            sp.dma_start(wts[:, 0], dr["w_out3"][0]).then_inc(w_in[0], 16)
            load_gates(0)
            sp.wait_ge(normed, 1)
            load_branches(1)
            sp.dma_start(wts[:, 1], dr["w_out3"][1]).then_inc(w_in[1], 16)
            sp.dma_start(wts[:, 2], dr["w_out3"][2]).then_inc(w_in[2], 16)
            load_x(0)
            sp.dma_start(t["w_head"][:, :, :], dr["w_q"][:, :, (HP - 1) * 2 * P:HP * 2 * P]).then_inc(head_in, 16)
            sp.dma_start(t["keys"][:, :, :], dr["keysT"]).then_inc(head_in, 16)
            with sp.Fori(0, BLOCKS - 2) as i:
                turn(sp.snap(i + 0), True, True)
            turn(BLOCKS - 2, False, True)
            turn(BLOCKS - 1, False, False)
            sp.wait_ge(h2_out, BLOCKS * 16 + 16)
            sp.wait_ge(head_in, 32)

        @block.scalar
        def _(act):
            def ahead(b):
                act.wait_ge(branches_in, b * 64 + 64)
                nc.scalar.activation(sz[:, :], z[:, :], ACT.Sigmoid)
                nc.scalar.activation(o[:, :, :], o[:, :, :], ACT.Sigmoid).then_inc(branch_sig, 1)
                for h in range(HM):
                    nc.scalar.activation(sq[:, h * DM:(h + 1) * DM], hm[:, h, :], ACT.Square, accum_out=ss[:, 1 + h:2 + h])
                act.drain()
                act.wait_ge(y_gated, b + 1)
                nc.scalar.activation(sq[:, :], yn[:, :], ACT.Square, accum_out=ss[:, 0:1])
                act.drain()
                act.sem_inc(branch_sums, 1)
                act.wait_ge(branch_ms, b + 1)
                nc.scalar.activation(root[:, 0:5], ss[:, 0:5], ACT.Sqrt).then_inc(branch_root, 1)

            def turn(b, more):
                act.wait_ge(gates_in, b * 16 + 16)
                nc.scalar.activation(mg[:, :, :], mg[:, :, :], ACT.Sigmoid).then_inc(gate_sig, 1)
                if more:
                    ahead(b + 1)
                act.wait_ge(mix_turned, b + 1)
                nc.scalar.copy(flat(mixT[:, :, :]), bank[2][:, :]).then_inc(mixT_ready, 1)
                act.wait_ge(out_mm, b + 1)
                nc.scalar.activation(sq[:, :], bank[3][:, :], ACT.Square, accum_out=ss[:, 5:6])
                act.drain()
                act.sem_inc(out_sums, 1)
                act.wait_ge(out_ms, b + 1)
                nc.scalar.activation(root[:, 5:6], ss[:, 5:6], ACT.Sqrt).then_inc(out_root, 1)
                act.wait_ge(x1_ready, b + 1)
                nc.scalar.activation(sq[:, :], x[:, :], ACT.Square, accum_out=ss[:, 6:7])
                act.drain()
                act.sem_inc(x1_sums, 1)
                act.wait_ge(x1_ms, b + 1)
                nc.scalar.activation(root[:, 6:7], ss[:, 6:7], ACT.Sqrt).then_inc(x1_root, 1)

            turns(act, ahead, turn)

        @block.tensor
        def _(pe):
            def ahead(b):
                pe.wait_ge(normed, b + 1)
                for k in range(KT):
                    nc.tensor.transpose(bank[0][:, k * P:(k + 1) * P], yn[:, k * P:(k + 1) * P], t["ident"][:, :])
                for k in range(KT):
                    last = nc.tensor.transpose(bank[1][:, k * P:(k + 1) * P], flat(hn[:, :, :])[:, k * P:(k + 1) * P], t["ident"][:, :])
                last.then_inc(turned, 1)

            def product(to, src, n):
                for c in range(2):
                    for k in range(KT):
                        last = nc.tensor.matmul(to[:, c * 512:(c + 1) * 512], src[:, k, :],
                                                wts[:, n, k, c * 512:(c + 1) * 512], start=(k == 0), stop=(k == KT - 1))
                return last

            def turn(b, more):
                pe.wait_ge(gained, b + 1)
                pe.wait_ge(w_in[0], 16)
                product(bank[2], yT, 0)
                pe.wait_ge(out_free, b + 1)
                pe.wait_ge(w_in[1], 16)
                product(bank[3], hT, 1).then_inc(branch_mm, 1)
                if more:
                    ahead(b + 1)
                pe.wait_ge(mixed, b + 1)
                for k in range(KT):
                    last = nc.tensor.transpose(bank[2][:, k * P:(k + 1) * P], mix[:, k * P:(k + 1) * P], t["ident"][:, :])
                last.then_inc(mix_turned, 1)
                pe.wait_ge(mixT_ready, b + 1)
                pe.wait_ge(w_in[2], 16)
                product(bank[3], mixT, 2).then_inc(out_mm, 1)

            turns(pe, ahead, turn)

        @block.vector
        def _(dve):
            dve.sem_inc(out_free, 1)
            dve.sem_inc(h2_out, 16)

            def ahead(b):
                dve.wait_ge(branches_in, b * 64 + 64)
                nc.vector.tensor_tensor(yn[:, :], y[:, :], z[:, :], ALU.mult)
                dve.drain()
                dve.wait_ge(branch_sig, b + 1)
                nc.vector.tensor_tensor(yn[:, :], yn[:, :], sz[:, :], ALU.mult).then_inc(y_gated, 1)
                dve.wait_ge(branch_sums, b + 1)
                nc.vector.tensor_scalar(ss[:, 0:1], ss[:, 0:1], 1.0 / D, EPS, ALU.mult, ALU.add)
                nc.vector.tensor_scalar(ss[:, 1:5], ss[:, 1:5], 1.0 / DM, EPS, ALU.mult, ALU.add)
                dve.drain()
                dve.sem_inc(branch_ms, 1)
                dve.wait_ge(branch_root, b + 1)
                nc.vector.reciprocal(rr[:, 0:5], root[:, 0:5])
                dve.drain()
                nc.vector.tensor_scalar(yn[:, :], yn[:, :], rr[:, 0:1], None, ALU.mult)
                for h in range(HM):
                    nc.vector.scalar_tensor_tensor(hn[:, h, :], hm[:, h, :], rr[:, 1 + h:2 + h], o[:, h, :], ALU.mult, ALU.mult)
                dve.drain()
                dve.sem_inc(normed, 1)

            def gain(b):
                dve.wait_ge(turned, b + 1)
                nc.vector.tensor_tensor(yT[:, :, :], bank[0][:, :].rearrange("p (k t) -> p k t", t=P), bc_last(t["gains"][:, 4, :], P), ALU.mult)
                nc.vector.tensor_tensor(hT[:, :, :], bank[1][:, :].rearrange("p (k t) -> p k t", t=P), bc_last(t["gains"][:, 5, :], P), ALU.mult)
                dve.drain()
                dve.sem_inc(gained, 1)

            def inverse_root(b, n, sums, ms, roots):
                dve.wait_ge(sums, b + 1)
                nc.vector.tensor_scalar(ss[:, n:n + 1], ss[:, n:n + 1], 1.0 / D, EPS, ALU.mult, ALU.add).then_inc(ms, 1)
                dve.wait_ge(roots, b + 1)
                nc.vector.reciprocal(rr[:, n:n + 1], root[:, n:n + 1])
                dve.drain()

            def turn(b, more):
                if more:
                    ahead(b + 1)
                dve.wait_ge(gate_sig, b + 1)
                dve.wait_ge(branch_mm, b + 1)
                nc.vector.tensor_tensor(mix[:, :], mg[:, 0, :], bank[2][:, :], ALU.mult)
                nc.vector.tensor_tensor(gated[:, :], mg[:, 1, :], bank[3][:, :], ALU.mult)
                dve.drain()
                nc.vector.tensor_tensor(mix[:, :], mix[:, :], gated[:, :], ALU.add)
                dve.drain()
                dve.sem_inc(mixed, 1)
                if more:
                    gain(b + 1)
                inverse_root(b, 5, out_sums, out_ms, out_root)
                dve.wait_ge(x_in, b * 32 + 32)
                nc.vector.scalar_tensor_tensor(gated[:, :], bank[3][:, :], rr[:, 5:6], rows[:, 0, :], ALU.mult, ALU.mult)
                dve.drain()
                dve.sem_inc(out_free, 1)
                nc.vector.tensor_tensor(x[:, :], x[:, :], gated[:, :], ALU.add).then_inc(x1_ready, 1)
                inverse_root(b, 6, x1_sums, x1_ms, x1_root)
                dve.wait_ge(h2_out, b * 16 + 16)
                nc.vector.scalar_tensor_tensor(h2[:, :], x[:, :], rr[:, 6:7], rows[:, 1, :], ALU.mult, ALU.mult)
                dve.drain()
                nc.vector.tensor_tensor(h2[:, :], h2[:, :], rows[:, 2, :], ALU.add).then_inc(h2_ready, 1)

            ahead(0)
            gain(0)
            with dve.Fori(0, BLOCKS - 1) as i:
                turn(i, True)
            turn(BLOCKS - 1, False)


def channel_mixer(nc, dr, t):
    HALF, RING, AHEAD = 8, 8, 2
    GROUP = 2
    GH = HALF // GROUP
    with ExitStack() as ctx:
        sb = lambda n, s, d=F32: ctx.enter_context(nc.sbuf_tensor("e_" + n, s, d))
        sem = semaphores(nc, ctx, "e_")
        wq, keys, w_head = sb("wq", [P, KT, 2 * HP * P]), t["keys"], t["w_head"]
        h2, h2T, qT = sb("h2", [P, D]), sb("h2T", [P, KT, P]), sb("qT", [P, 2, P])
        S, S2 = sb("S", [P, 2, P]), sb("S2", [P, 2, P])
        v16, i16, i16f = sb("v16", [P, 2, TOPK]), sb("i16", [P, 2, TOPK], U32), sb("i16f", [P, 2, TOPK])
        cand, cand2 = sb("cand", [P, TOPK, TOPK]), sb("cand2", [P, TOPK, TOPK])
        best, place = sb("best", [P, TOPK]), sb("place", [P, TOPK], U32)
        pick, pickf = sb("pick", [P, 2, TOPK], U32), sb("pickf", [P, 2, TOPK])
        hot, number = sb("hot", [P, 2, TOPK, TOPK]), sb("number", [P, 2, TOPK])
        arg, expo, total = sb("arg", [P, TOPK]), sb("expo", [P, TOPK]), sb("total", [P, 2])
        expert = sb("expert", [P, RING, 2 * D])
        num = sb("num", [P, 2, HALF], U32)
        x_next, xb, x1, row_f, f = sb("x_next", [P, D]), sb("xb", [P, D]), sb("x1", [P, D]), sb("row_f", [P, D]), sb("f", [P, D])
        dots, act_v, coef = sb("dots", [P, 2, HALF]), sb("act", [P, 2, HALF]), sb("coef", [P, 2, HALF])
        diag, zero = sb("diag", [P, HALF, P]), sb("zero", [P, P])
        ss, root, rr = sb("ss", [P, 1]), sb("root", [P, 1]), sb("rr", [P, 1])
        acc = ctx.enter_context(nc.psum_tensor("e_acc", [P, D], F32))
        sq = ctx.enter_context(nc.psum_tensor("e_sq", [P, D], F32))
        qb = [ctx.enter_context(nc.psum_tensor(f"e_q{i}", [P, 512], F32)) for i in range(2)]
        turn = ctx.enter_context(nc.psum_tensor("e_turn", [P, D], F32))
        w_in = sem("w_in")
        h2_in, turned, h2T_ready = sem("h2_in"), sem("turned"), sem("h2T_ready")
        w_copied, q_mm, q_moved, s_mm, S_moved, scored = sem("w_copied"), sem("q_mm"), sem("q_moved"), sem("s_mm"), sem("S_moved"), sem("scored")
        arg_ready, exp_ready, chosen = sem("arg_ready"), sem("exp_ready"), sem("chosen")
        in_slot = [sem(f"in_slot{j}") for j in range(RING)]
        slot_free = sem("slot_free")
        dots_ready, act_ready, coef_ready, diag_ready = sem("dots_ready"), sem("act_ready"), sem("coef_ready"), sem("diag_ready")
        num_ready, zero_ready = sem("num_ready"), sem("zero_ready")
        x_copied, x1_in, x_ready, f_mm, f_out, acc_free, f_free, ms_ready, root_ready, ss_ready, y_ready, y_out = (
            sem("x_copied"), sem("x1_in"), sem("x_ready"), sem("f_mm"), sem("f_out"), sem("acc_free"), sem("f_free"), sem("ms_ready"),
            sem("root_ready"), sem("ss_ready"), sem("y_ready"), sem("y_out"))
        passed, pe_passed, pool_passed, sp_passed = sem("passed"), sem("pe_passed"), sem("pool_passed"), sem("sp_passed")
        block = ctx.enter_context(nc.Block())

        def schedule(eng, prepare, begin, body, end):
            prepare(0)
            with eng.Fori(0, AHEAD) as k:
                body(None, (k, 0))
            with eng.Fori(0, BLOCKS - 1) as b:
                begin(b)
                with eng.Fori(0, HP - AHEAD) as k:
                    body((k, b), (k + AHEAD, b))
                prepare(b + 1)
                with eng.Fori(0, AHEAD) as k:
                    body((k + (HP - AHEAD), b), (k, b + 1))
                end(b)
            b = BLOCKS - 1
            begin(b)
            with eng.Fori(0, HP - AHEAD) as k:
                body((k, b), (k + AHEAD, b))
            with eng.Fori(0, AHEAD) as k:
                body((k + (HP - AHEAD), b), None)
            end(b)

        def of(ap, b):
            return ap[b] if isinstance(b, int) else row(ap[bass.ds(b, 1)])

        @block.sync
        def _(sp):
            sp.dma_start(h2[:, :], dr["h2"][0]).then_inc(h2_in, 16)
            sp.dma_start(wq[:, :, :], dr["w_q"]).then_inc(w_in, 16)

            sp.wait_ge(x_copied, 1)
            sp.dma_start(h2[:, :], dr["h2"][1]).then_inc(h2_in, 16)

            def run(b, more):
                if more:
                    sp.wait_ge(x_copied, b + 2)
                    sp.sem_inc(sp_passed, 1)
                    sp.dma_start(h2[:, :], of(dr["h2"], b + 2)).then_inc(h2_in, 16)
                sp.dma_start(x1[:, :], of(dr["x1"], b)).then_inc(x1_in, 16)
                r = of(dr["mod_rows"], b)[0:1, V_GATE_F * D:(V_GATE_F + 1) * D]
                sp.dma_start(row_f[:, :], r.partition_broadcast(P)).then_inc(x1_in, 16)
                sp.wait_ge(y_ready, b + 1)
                sp.sem_inc(sp_passed, 1)
                sp.dma_start(of(dr["out_y"], b), x1[:, :]).then_inc(y_out, 16)
                sp.wait_ge(y_out, b * 16 + 16)
                sp.sem_inc(sp_passed, 1)

            with sp.Fori(0, BLOCKS - 2) as b:
                run(b, True)
            run(BLOCKS - 2, False)
            run(BLOCKS - 1, False)

        @block.gpsimd
        def _(pool):
            with pool.Fori(0, BLOCKS) as b:
                with pool.Fori(0, HP) as k:
                    pool.wait_ge(chosen, b * HP + k + 1)
                    for half in range(2):
                        s = (b * HP + k) * (2 * HALF) + half * HALF
                        pool.wait_ge(slot_free, s + 1)
                        pool.sem_inc(pool_passed, 1)
                        nc.gpsimd.tensor_copy(num[:, half, :], t["idx"][:, :, :].rearrange("p b n -> p (b n)")[:, bass.ds(s, HALF)]).then_inc(num_ready, 1)
                        pool.wait_ge(num_ready, (b * HP + k) * 2 + (half + 1))
                        for j in range(HALF):
                            pool.wait_ge(slot_free, s + (j + 1))
                            pool.sem_inc(pool_passed, 1)
                            nc.gpsimd.indirect_dma_start(expert[:, j, :], None, dr["peer_uv"], bass.IndirectOffsetOnAxis(num[:, half, j:j + 1], 0)).then_inc(in_slot[j], 16)

        @block.vector
        def _(dve):
            dve.sem_inc(f_free, 1)
            dve.sem_inc(scored, 1)
            nc.vector.memset(zero[:, :], 0.0).then_inc(zero_ready, 1)

            def group_dots(k, b, half, q):
                seen = (b * HP + k) * 2 + half
                for j in range(GROUP * q, GROUP * (q + 1)):
                    dve.wait_ge(in_slot[j], seen * 16 + 16)
                    nc.vector.tensor_tensor_reduce(expert[:, j, 0:D], expert[:, j, 0:D], xb[:, :], 1.0, 0.0, ALU.mult, ALU.add,
                                                   dots[:, half, j:j + 1])
                dve.drain()
                dve.sem_inc(dots_ready, 1)

            def group_gates(k, b, half, q):
                seen = (b * HP + k) * 2 + half
                dve.wait_ge(act_ready, seen * GH + (q + 1))
                dve.sem_inc(passed, 1)
                w = slice(GROUP * q, GROUP * (q + 1))
                gates = t["gate"][:, :, :].rearrange("p b n -> p (b n)")
                nc.vector.tensor_tensor(coef[:, half, w], act_v[:, half, w],
                                        gates[:, bass.ds(seen * HALF + GROUP * q, GROUP)], ALU.mult).then_inc(coef_ready, 1)

            def best16(values, scratch, v, index):
                n = len(values)
                for a in range(n):
                    nc.vector.max(v[a][:, 0:8], values[a])
                dve.drain()
                for a in range(n):
                    nc.vector.match_replace(scratch[a], v[a][:, 0:8], values[a], -3.0e38)
                dve.drain()
                for a in range(n):
                    nc.vector.max(v[a][:, 8:16], scratch[a])
                    nc.vector.max_index(index[a][:, 0:8], v[a][:, 0:8], values[a])
                dve.drain()
                for a in range(n):
                    nc.vector.max_index(index[a][:, 8:16], v[a][:, 8:16], scratch[a])
                dve.drain()

            flat = lambda ap: ap.rearrange("p a b -> p (a b)")

            def keys_of_head(k, c):
                turn_no = c * HP + k
                dve.wait_ge(S_moved, turn_no + 1)
                dve.sem_inc(passed, 1)
                best16([S[:, n, :] for n in range(2)], [S2[:, n, :] for n in range(2)], [v16[:, n, :] for n in range(2)],
                       [i16[:, n, :] for n in range(2)])
                dve.sem_inc(scored, 1)
                nc.vector.tensor_copy(i16f[:, :, :], i16[:, :, :])
                nc.vector.tensor_tensor(cand[:, :, :], bc_last(v16[:, 0, :], TOPK),
                                        v16[:, 1, :].unsqueeze(1).to_broadcast([P, TOPK, TOPK]), ALU.add)
                dve.drain()

            def sums_of_head(k, c):
                best16([flat(cand[:, :, :])], [flat(cand2[:, :, :])], [best[:, :]], [place[:, :]])
                nc.vector.tensor_scalar(arg[:, :], best[:, :], best[:, 0:1], None, ALU.subtract).then_inc(arg_ready, 1)

            def experts_of_head(k, c):
                turn_no = c * HP + k
                nc.vector.tensor_scalar(pick[:, 0, :], place[:, :], 4, None, ALU.logical_shift_right)
                nc.vector.tensor_scalar(pick[:, 1, :], place[:, :], 15, None, ALU.bitwise_and)
                dve.drain()
                nc.vector.tensor_copy(pickf[:, :, :], pick[:, :, :])
                dve.drain()
                nc.vector.tensor_tensor(hot[:, :, :, :].rearrange("p c k j -> p (c k) j"), bc_last(flat(pickf[:, :, :]), TOPK),
                                        t["iota"][:, :].unsqueeze(1).to_broadcast([P, 2 * TOPK, TOPK]), ALU.is_equal)
                dve.drain()
                nc.vector.tensor_tensor(hot[:, :, :, :], hot[:, :, :, :], i16f[:, :, :].unsqueeze(2).to_broadcast([P, 2, TOPK, TOPK]), ALU.mult)
                dve.drain()
                nc.vector.tensor_reduce(number[:, :, :], hot[:, :, :, :], AX, ALU.add)
                dve.drain()
                dve.wait_ge(exp_ready, turn_no + 1)
                nc.vector.scalar_tensor_tensor(number[:, 0, :], number[:, 0, :], float(P), number[:, 1, :], ALU.mult, ALU.add)
                nc.vector.tensor_reduce(total[:, 0:1], expo[:, :], AX, ALU.add)
                dve.drain()
                nc.vector.reciprocal(total[:, 1:2], total[:, 0:1])
                at = bass.ds(turn_no * TOPK, TOPK)
                nc.vector.tensor_copy(flat(t["idx"][:, :, :])[:, at], number[:, 0, :])
                dve.drain()
                nc.vector.tensor_scalar(flat(t["gate"][:, :, :])[:, at], expo[:, :], total[:, 1:2], None, ALU.mult)
                dve.drain()
                dve.sem_inc(chosen, 1)

            def prepare(c):
                dve.wait_ge(turned, c + 1)
                nc.vector.tensor_copy(x_next[:, :], h2[:, :]).then_inc(x_copied, 1)

            def begin(b):
                dve.drain()
                nc.vector.tensor_copy(xb[:, :], x_next[:, :])
                dve.drain()

            def body(run, choose):
                for n in range(2 * GH):
                    half, q, step = n // GH, n % GH, {2 * GH - 3: keys_of_head, 2 * GH - 1: sums_of_head}.get(n)
                    if run:
                        group_dots(*run, half, q)
                        group_gates(*run, half, q)
                    if choose and step:
                        step(*choose)
                if choose:
                    experts_of_head(*choose)

            def end(b):
                dve.wait_ge(ss_ready, b + 1)
                nc.vector.tensor_scalar(ss[:, :], ss[:, :], 1.0 / D, EPS, ALU.mult, ALU.add).then_inc(ms_ready, 1)
                dve.wait_ge(root_ready, b + 1)
                nc.vector.reciprocal(rr[:, :], root[:, :])
                dve.drain()
                dve.wait_ge(x1_in, b * 32 + 32)
                nc.vector.scalar_tensor_tensor(f[:, :], f[:, :], rr[:, 0:1], row_f[:, :], ALU.mult, ALU.mult)
                dve.drain()
                nc.vector.tensor_tensor(x1[:, :], x1[:, :], f[:, :], ALU.add)
                dve.drain()
                dve.sem_inc(y_ready, 1)
                dve.sem_inc(f_free, 1)

            schedule(dve, prepare, begin, body, end)

        @block.scalar
        def _(act):
            act.sem_inc(acc_free, 1)
            act.sem_inc(w_copied, 1)

            def prepare(c):
                act.wait_ge(turned, c + 1)
                nc.scalar.copy(h2T[:, :, :].rearrange("p k t -> p (k t)"), turn[:, :]).then_inc(h2T_ready, 1)

            def head_weights(k):
                act.wait_ge(w_in, 16)
                nc.scalar.copy(w_head[:, :, :], wq[:, :, bass.ds(k * (2 * P), 2 * P)]).then_inc(w_copied, 1)

            def queries(k, c):
                j = c * HP + k
                act.wait_ge(q_mm, j + 1)
                for n in range(2):
                    last = nc.scalar.copy(qT[:, n, :], qb[n][:, 0:P])
                last.then_inc(q_moved, 1)

            def scores(k, c):
                j = c * HP + k
                act.wait_ge(s_mm, j + 1)
                act.wait_ge(scored, j + 1)
                nc.scalar.copy(S[:, :, :].rearrange("p n k -> p (n k)"), turn[:, 0:2 * P]).then_inc(S_moved, 1)

            def exponentials(k, c):
                j = c * HP + k
                act.wait_ge(arg_ready, j + 1)
                nc.scalar.activation(expo[:, :], arg[:, :], ACT.Exp).then_inc(exp_ready, 1)

            def gelus(k, b, half, q):
                seen = (b * HP + k) * 2 + half
                w = slice(GROUP * q, GROUP * (q + 1))
                act.wait_ge(dots_ready, seen * GH + (q + 1))
                nc.scalar.activation(act_v[:, half, w], dots[:, half, w], ACT.Gelu).then_inc(act_ready, 1)

            def diagonals(k, b, half, q):
                seen = (b * HP + k) * 2 + half
                act.wait_ge(coef_ready, seen * GH + (q + 1))
                act.wait_ge(slot_free, seen * HALF + GROUP * (q + 1))
                for j in range(GROUP):
                    at = GROUP * q + j
                    last = nc.scalar.mul(diag[:, at, :], t["ident"][:, :], coef[:, half, at:at + 1])
                last.then_inc(diag_ready, 1)

            def retrieval(k, c):
                queries(k, c)
                head_weights(k)
                scores(k, c)

            def first_retrieval(k, c):
                queries(k, c)
                scores(k, c)
                head_weights(k)

            def body(run, choose):
                for n in range(2 * GH):
                    half, q, step = n // GH, n % GH, {GH // 2 - 1: retrieval if run else first_retrieval, 2 * GH - 1: exponentials}.get(n)
                    if run:
                        gelus(*run, half, q)
                        diagonals(*run, half, q)
                    if choose and step:
                        step(*choose)

            def end(b):
                act.wait_ge(f_mm, b + 1)
                act.wait_ge(f_free, b + 1)
                nc.scalar.copy(f[:, :], acc[:, :])
                act.drain()
                act.sem_inc(acc_free, 1)
                nc.scalar.activation(sq[:, :], f[:, :], ACT.Square, accum_out=ss[:, :])
                act.drain()
                act.sem_inc(ss_ready, 1)
                act.wait_ge(ms_ready, b + 1)
                nc.scalar.activation(root[:, :], ss[:, :], ACT.Sqrt).then_inc(root_ready, 1)

            schedule(act, prepare, lambda b: None, body, end)

        @block.tensor
        def _(pe):
            pe.sem_inc(slot_free, RING)
            pe.wait_ge(zero_ready, 1)
            z512 = zero[:, :].unsqueeze(1).to_broadcast([P, 4, P])

            def prepare(c):
                pe.wait_ge(h2_in, c * 16 + 16)
                if not isinstance(c, int):
                    pe.wait_ge(S_moved, c * HP)
                for k in range(KT):
                    last = nc.tensor.transpose(turn[:, k * P:(k + 1) * P], h2[:, k * P:(k + 1) * P], t["ident"][:, :])
                last.then_inc(turned, 1)
                pe.wait_ge(h2T_ready, c + 1)
                pe.sem_inc(pe_passed, 1)

            def begin(b):
                pe.wait_ge(acc_free, b + 1)
                for half in range(2):
                    nc.tensor.matmul(acc[:, half * 512:(half + 1) * 512], zero[:, :], z512, start=True, stop=False)

            def group_products(k, b, half, q):
                seen = (b * HP + k) * 2 + half
                pe.wait_ge(diag_ready, seen * GH + (q + 1))
                for j in range(GROUP * q, GROUP * (q + 1)):
                    pe.wait_ge(in_slot[j], seen * 16 + 16)
                    for c in range(2):
                        last = nc.tensor.matmul(acc[:, c * 512:(c + 1) * 512], diag[:, j, :],
                                                expert[:, j, D + c * 512:D + (c + 1) * 512], start=False, stop=False)
                    last.then_inc(slot_free, 1)

            def retrieval(k, c):
                j = c * HP + k
                pe.wait_ge(w_copied, j + 1)
                for n in range(2):
                    for m in range(KT):
                        last = nc.tensor.matmul(qb[n][:, 0:P], w_head[:, m, n * P:(n + 1) * P], h2T[:, m, :],
                                                start=(m == 0), stop=(m == KT - 1))
                last.then_inc(q_mm, 1)
                pe.wait_ge(q_moved, j + 1)
                for n in range(2):
                    last = nc.tensor.matmul(turn[:, n * P:(n + 1) * P], qT[:, n, :], keys[:, n, :], start=True, stop=True)
                last.then_inc(s_mm, 1)

            def body(run, choose):
                for n in range(2 * GH):
                    if run:
                        group_products(*run, n // GH, n % GH)
                    if choose and n == GH // 2 - 1:
                        retrieval(*choose)

            def end(b):
                for c in range(2):
                    last = nc.tensor.matmul(acc[:, c * 512:(c + 1) * 512], zero[:, :], z512, start=False, stop=True)
                last.then_inc(f_mm, 1)

            schedule(pe, prepare, begin, body, end)


def programme(nc, dr):
    with ExitStack() as ctx:
        sb = lambda n, s, d=F32: ctx.enter_context(nc.sbuf_tensor(n, s, d))
        t = {n: sb(n, [P, P]) for n in ("ones", "triF", "triB", "ident", "nident", "maskF", "maskB")}
        t["iota_i"], t["iota"] = sb("iota_i", [P, TOPK], mybir.dt.int32), sb("iota", [P, TOPK])
        t["rows"], t["skip"], t["gains"] = sb("rows", [P, R_N]), sb("skip", [P, HS]), sb("gains", [P, 6, KT])
        t["small"], t["gates"] = sb("small", [P, BLOCKS, 48]), sb("gates", [P, BLOCKS, G_N])
        t["idx"], t["gate"] = sb("idx", [P, BLOCKS, SLOTS], U32), sb("gate", [P, BLOCKS, SLOTS])
        constants(nc, t)
        with nc.sbuf_tensor("hT", [P, KT, TOK], F32) as hT:
            modulate_and_normalise(nc, dr, t, hT)
            project(nc, dr, t, hT)
        skip_sum(nc, t)
        gates(nc, dr, t)
        scan(nc, dr, t, "prompt")
        scan(nc, dr, t, "back")
        scan(nc, dr, t, "sample")
        t["w_head"], t["keys"] = sb("w_head", [P, KT, 2 * P]), sb("keys", [P, 2, P])
        merge(nc, dr, t)
        channel_mixer(nc, dr, t)


def cat(*a, axis=-1):
    import numpy as np
    return np.concatenate(a, axis=axis)


def tiles(w, n=512):
    import numpy as np
    rows, columns = w.shape
    return np.ascontiguousarray(w.reshape(rows // P, P, columns // n, n).transpose(2, 1, 0, 3))


def cols(v):
    import numpy as np
    v = v.reshape(*v.shape[:-1], v.shape[-1] // P, P)
    return np.ascontiguousarray(np.moveaxis(v, -1, 0))


def layout(i):
    import numpy as np
    w = i["w_in"][0]
    z, xbc, dt, q, k, v, o, g, m = np.split(w, np.cumsum([1024, 2048, 32, 1024, 1024, 1024, 1024, 16]), axis=1)
    g = g.reshape(1024, 2, 2, 4).transpose(0, 2, 1, 3).reshape(1024, 16)
    out = {}
    out["x"] = cat(i["x_prompt"].reshape(1, 128, 1024), i["x_sample"].reshape(4, 128, 1024), axis=0)
    out["cvT"] = np.ascontiguousarray(np.moveaxis(cols(cat(i["c_ctx"][None], i["c"], axis=0)), 1, 2))
    out["w_mod"] = tiles(i["w_mod"][0])
    out["b_mod"] = i["b_mod"]
    out["gain_rows"] = cat(*[i[n] for n in ("g_mix_pre", "g_mix_post", "g_ffn_pre", "g_ffn_post")])
    out["gains"] = cols(np.stack([i[n][0] for n in ("g_mix_pre", "g_mix_post", "g_ffn_pre", "g_ffn_post", "ssd_norm_g", "mlstm_norm_g")]))
    out["small_rows"] = cat(*[i[n].reshape(1, -1) for n in ("ssd_a_log", "ssd_dt_bias", "ssd_d", "mlstm_i_bias", "mlstm_f_bias", "state_mlstm_m")])
    out["w_big"] = tiles(cat(z, v, o, m, xbc, q, k))
    out["w_small"] = tiles(cat(dt, g), 48)[0]
    out["convT"] = cols(cat(i["conv_w"][0], i["conv_b"], axis=0))
    out["w_out3"] = np.stack([tiles(i[n][0], 1024)[0] for n in ("w_ssd_out", "w_mlstm_out", "w_out")])
    out["w_q"] = tiles(cat(i["peer_w_q"][0][:, 256:], i["peer_w_q"][0][:, :256]), 2048)[0]
    out["keysT"] = np.ascontiguousarray(np.stack([i["peer_keys1"][0].T, i["peer_keys2"][0].T], axis=1))
    out["peer_uv"] = cat(i["peer_u"][0], i["peer_v"][0])
    out["state_ssd"] = np.ascontiguousarray(i["state_ssd"].reshape(2, 1024, 128).transpose(0, 2, 1))
    c = cat(i["state_mlstm_c"].reshape(2, 4, 2, 128, 256), i["state_mlstm_n"].reshape(2, 4, 2, 128, 1))
    out["state_c"] = np.ascontiguousarray(c.transpose(0, 3, 1, 2, 4)).reshape(2, 128, 8 * 257)
    return out


SCRATCH = {
    "mod_rows": (BLOCKS, 1, 6 * D), "proj": (BLOCKS, P, COLS_T), "xbcT": (16, P, TOK), "qkT": (16, P, TOK),
    "back_ssd": (CHUNKS, P, D), "back_c": (CHUNKS, P, HM * 2 * CE), "back_m": (CHUNKS, P, HM),
    "y_ssd": (BLOCKS, P, D), "y_mlstm": (BLOCKS, P, D), "x1": (BLOCKS, P, D), "h2": (BLOCKS, P, D),
}
OUTPUTS = {"out_y": (BLOCKS, P, D), "out_ssd": (2, P, D), "out_c": (2, P, HM * 2 * CE), "out_m": (1, 2 * HM)}


def kernel(**inputs):
    import numpy as np
    import concourse.bacc as bacc
    from concourse.bass_utils import run_bass_kernel_spmd

    nc = bacc.Bacc("TRN2", target_bir_lowering=False, num_devices=1)
    arrays, dr = {}, {}
    for name, a in layout({k: np.asarray(v) for k, v in inputs.items()}).items():
        arrays["in_" + name] = np.ascontiguousarray(a)
        dr[name] = nc.dram_tensor("in_" + name, a.shape, F32, kind="ExternalInput").ap()
    for name, shape in SCRATCH.items():
        dr[name] = nc.dram_tensor("scratch_" + name, shape, F32, kind="Internal").ap()
    for name, shape in OUTPUTS.items():
        dr[name] = nc.dram_tensor(name, shape, F32, kind="ExternalOutput").ap()
    programme(nc, dr)
    got = run_bass_kernel_spmd(nc, [arrays], core_ids=[0]).results[0]
    y = got["out_y"]
    ssd = got["out_ssd"].transpose(0, 2, 1).reshape(1, 1, 2, HS, PS, P)
    c = got["out_c"].reshape(2, P, HM, 2, CE).transpose(0, 2, 3, 1, 4).reshape(1, 1, 2, HM, DM, CE)
    return (y[0:1].reshape(1, P, D), y[1:].reshape(1, LAT, D), np.ascontiguousarray(ssd), np.ascontiguousarray(c[..., :DM]),
            np.ascontiguousarray(c[..., DM]), got["out_m"].reshape(1, 1, 2, HM))
```

```python
from contextlib import ExitStack

import concourse.bass as bass
from concourse import mybir

P = 128
D = 1024
KT = D // P
BLOCKS = 5
CHUNKS = BLOCKS - 1
TOK = BLOCKS * P
LAT = CHUNKS * P
GRID_W = 64
EPS = 1e-6
HS, PS, NG = 16, 64, 4
HM, DM = 4, 256
CE = DM + 1
HP, TOPK = 8, 16
SLOTS = HP * TOPK
NEG = -(2.0 ** 100)

ALU = mybir.AluOpType
ACT = mybir.ActivationFunctionType
AX = mybir.AxisListType.X
F32 = mybir.dt.float32
BF16 = mybir.dt.bfloat16
U32 = mybir.dt.uint32

COL_Z, COL_V, COL_O, COL_M, COLS_T = 0, D, 2 * D, 3 * D, 5 * D
G_DA, G_LI, G_NACS, G_EA, G_WD, G_ED, G_E, G_DT, G_BC, G_TOT, G_LF = 0, 32, 40, 72, 104, 136, 168, 176, 208, 216, 224
G_N = 232
R_ALOG, R_DTB, R_SKIP, R_IB, R_FB, R_M0 = 0, 32, 64, 96, 104, 112
R_N = 120
V_SHIFT_A, V_SCALE_A = range(2)
V_GATE_A, V_SHIFT_F, V_SCALE_F, V_GATE_F, V_ROWS = range(5)
MOD_FIRST, MOD_LATER = 2 * D // 512, V_ROWS * D // 512


def bc_last(ap, n):
    shape = list(ap.shape) + [n]
    return ap.unsqueeze(len(ap.shape)).to_broadcast(shape)


def semaphores(nc, ctx, prefix=""):
    taken = []

    def sem(name):
        taken.append(nc.alloc_semaphore(prefix + name))
        return taken[-1]

    def give_back():
        nc.clear_and_free_semaphores(taken)
        nc.all_engine_barrier()

    ctx.callback(give_back)
    return sem


def row(ap):
    return ap.rearrange("o p f -> p (o f)")


CONSTANTS = 11


def constants(nc, t, ready):
    pool = nc.gpsimd
    nc.gpsimd.memset(t["ones"][:, :], 1.0).then_inc(ready, 1)
    nc.gpsimd.iota(t["iota_i"][:, :], [[1, TOPK]], base=0, channel_multiplier=0).then_inc(ready, 1)
    pool.wait_ge(ready, 2)
    nc.gpsimd.affine_select(out=t["triF"][:, :], in_=t["ones"][:, :], pattern=[[1, P]], compare_op=ALU.is_ge,
                            fill=0.0, base=0, channel_multiplier=-1).then_inc(ready, 1)
    nc.gpsimd.affine_select(out=t["triB"][:, :], in_=t["ones"][:, :], pattern=[[-1, P]], compare_op=ALU.is_ge,
                            fill=0.0, base=0, channel_multiplier=1).then_inc(ready, 1)
    nc.gpsimd.affine_select(out=t["ident"][:, :], in_=t["ones"][:, :], pattern=[[-1, P]], compare_op=ALU.is_equal,
                            fill=0.0, base=0, channel_multiplier=1).then_inc(ready, 1)
    nc.gpsimd.tensor_copy(t["iota"][:, :], t["iota_i"][:, :]).then_inc(ready, 1)
    pool.wait_ge(ready, 6)
    nc.gpsimd.tensor_scalar(t["maskF"][:, :], t["triF"][:, :], 1.0, -NEG, ALU.subtract, ALU.mult).then_inc(ready, 1)
    nc.gpsimd.tensor_scalar(t["maskB"][:, :], t["triB"][:, :], 1.0, -NEG, ALU.subtract, ALU.mult).then_inc(ready, 1)
    pool.wait_ge(ready, 8)
    for name in ("ident", "maskF", "maskB"):
        nc.gpsimd.tensor_copy(t[name + "_16"][:, :], t[name][:, :]).then_inc(ready, 1)


def modulate_and_normalise(nc, dr, t, hT):
    with ExitStack() as ctx:
        sb = lambda n, s, d=F32: ctx.enter_context(nc.sbuf_tensor(n, s, d))
        sem = semaphores(nc, ctx)
        cv, sig = t["cv"], sb("cv_sig", [P, KT, 2])
        wm = sb("wm", [P, MOD_FIRST, KT, 512])
        bias, gain = sb("mod_bias", [2, 2 * D]), sb("mod_gain", [2, D])
        raw, vec = sb("mod_raw", [2, 2, 512]), sb("mod_vec", [2, 2, D])
        cols = sb("mod_cols", [P, 2, KT, 2])
        x, sq = sb("x", [P, BLOCKS, D]), sb("x_sq", [P, D])
        ss, root, rstd = sb("x_ss", [P, BLOCKS]), sb("x_root", [P, BLOCKS]), sb("x_rstd", [P, BLOCKS])
        row_ps = [ctx.enter_context(nc.psum_tensor(f"mod_ps{i}", [2, 512], F32)) for i in range(2)]
        col_ps = ctx.enter_context(nc.psum_tensor("mod_cols_ps", [P, 2, KT, 2], F32))
        ps = [ctx.enter_context(nc.psum_tensor(f"turn{i}", [P, 4, P], F32)) for i in range(4)]
        small_in, w_in, x_in = sem("small_in"), [sem(f"mod_w{i}") for i in range(MOD_FIRST)], [sem(f"x_in{b}") for b in range(BLOCKS)]
        sig_ready, silu_ready, chunk_mm, chunk_out, vec_ready = sem("sig_ready"), sem("silu_ready"), sem("chunk_mm"), sem("chunk_out"), sem("vec_ready")
        const_ready = sem("const_ready")
        cols_turned, cols_ready, later_in = sem("cols_turned"), sem("cols_ready"), sem("later_in")
        sums_ready, ms_ready, root_ready, scaled, turned, moved = (
            sem("sums_ready"), sem("ms_ready"), sem("root_ready"), sem("x_scaled"), sem("x_turned"), sem("h_moved"))
        block = ctx.enter_context(nc.Block())

        @block.gpsimd
        def _(pool):
            constants(nc, t, const_ready)

        @block.sync
        def _(sp):
            sp.dma_start(cv[:, :, :], dr["cvT"]).then_inc(small_in, 16)
            sp.dma_start(bias[:, :], dr["b_mod"][:, 0:2 * D].partition_broadcast(2)).then_inc(small_in, 16)
            sp.dma_start(gain[:, :], dr["gain_rows"][:, 0:D].partition_broadcast(2)).then_inc(small_in, 16)
            sp.dma_start(wm[:, 0], dr["w_mod"][0]).then_inc(w_in[0], 16)
            for b in range(BLOCKS):
                sp.dma_start(x[:, b, :], dr["x"][b]).then_inc(x_in[b], 16)
            for n in range(1, MOD_FIRST):
                sp.dma_start(wm[:, n], dr["w_mod"][n]).then_inc(w_in[n], 16)
            sp.dma_start(t["gains"][:, :, :], dr["gains"]).then_inc(later_in, 16)
            sp.dma_start(t["rows"][:, :], dr["small_rows"].partition_broadcast(P)).then_inc(later_in, 16)
            sp.wait_ge(later_in, 32)

        @block.scalar
        def _(act):
            act.wait_ge(small_in, 48)
            nc.scalar.activation(sig[:, :, :], cv[:, :, :], ACT.Sigmoid).then_inc(sig_ready, 1)
            for b in range(BLOCKS):
                act.wait_ge(x_in[b], 16)
                nc.scalar.activation(sq[:, :], x[:, b, :], ACT.Square, accum_out=ss[:, b:b + 1])
                act.drain()
            act.sem_inc(sums_ready, 1)
            act.wait_ge(ms_ready, 1)
            nc.scalar.activation(root[:, :], ss[:, :], ACT.Sqrt).then_inc(root_ready, 1)
            for n in range(2 * BLOCKS):
                b, half = n // 2, n % 2
                act.wait_ge(turned, n + 1)
                nc.scalar.copy(hT[:, 4 * half:4 * half + 4, b * P:(b + 1) * P], ps[n % 4][:, :, :]).then_inc(moved, 1)
            act.wait_ge(cols_turned, 1)
            nc.scalar.copy(cols[:, :, :, :], col_ps[:, :, :, :])
            act.drain()
            act.sem_inc(cols_ready, 1)
            for k in range(KT // 2):
                for c, tokens in enumerate((slice(0, P), slice(P, TOK))):
                    nc.scalar.activation(hT[:, k, tokens], hT[:, k, tokens], ACT.Identity,
                                         scale=cols[:, V_SCALE_A, k, c:c + 1], bias=cols[:, V_SHIFT_A, k, c:c + 1])

        @block.tensor
        def _(pe):
            def chunk(n):
                pe.wait_ge(w_in[n], 16)
                if n >= 2:
                    pe.wait_ge(chunk_out, n - 1)
                for k in range(KT):
                    last = nc.tensor.matmul(row_ps[n % 2][:, :], cv[:, k, :], wm[:, n, k, :], start=(k == 0), stop=(k == KT - 1))
                last.then_inc(chunk_mm, 1)

            pe.wait_ge(silu_ready, 1)
            for n in range(MOD_FIRST // 2):
                chunk(n)
            pe.wait_ge(const_ready, CONSTANTS)
            for n in range(2 * BLOCKS):
                b, half = n // 2, n % 2
                pe.wait_ge(scaled, b + 1)
                if n >= 4:
                    pe.wait_ge(moved, n - 3)
                for i in range(4):
                    k = 4 * half + i
                    last = nc.tensor.transpose(ps[n % 4][:, i, :], x[:, b, k * P:(k + 1) * P], t["ident"][:, :])
                last.then_inc(turned, 1)
            for n in range(MOD_FIRST // 2, MOD_FIRST):
                chunk(n)
            pe.wait_ge(vec_ready, MOD_FIRST)
            for v in (V_SCALE_A, V_SHIFT_A):
                for k in range(KT):
                    last = nc.tensor.transpose(col_ps[:, v, k, :], vec[:, v, k * P:(k + 1) * P], t["ident"][0:2, 0:2])
            last.then_inc(cols_turned, 1)

        @block.vector
        def _(dve):
            dve.wait_ge(sig_ready, 1)
            nc.vector.tensor_tensor(cv[:, :, :], cv[:, :, :], sig[:, :, :], ALU.mult).then_inc(silu_ready, 1)

            def vector(n):
                v, w = n // 2, slice((n % 2) * 512, (n % 2) * 512 + 512)
                dve.wait_ge(chunk_mm, n + 1)
                nc.vector.tensor_tensor(raw[:, n % 2, :], row_ps[n % 2][:, :], bias[:, n * 512:(n + 1) * 512], ALU.add).then_inc(chunk_out, 1)
                dve.drain()
                if v == V_SHIFT_A:
                    nc.vector.tensor_copy(vec[:, v, w], raw[:, n % 2, :]).then_inc(vec_ready, 1)
                else:
                    nc.vector.scalar_tensor_tensor(vec[:, v, w], raw[:, n % 2, :], 1.0, gain[:, w], ALU.add, ALU.mult).then_inc(vec_ready, 1)

            vector(0)
            dve.wait_ge(sums_ready, 1)
            nc.vector.tensor_scalar(ss[:, :], ss[:, :], 1.0 / D, EPS, ALU.mult, ALU.add).then_inc(ms_ready, 1)
            dve.wait_ge(root_ready, 1)
            nc.vector.reciprocal(rstd[:, :], root[:, :])
            dve.drain()
            for b in range(BLOCKS):
                nc.vector.tensor_scalar(x[:, b, :], x[:, b, :], rstd[:, b:b + 1], None, ALU.mult).then_inc(scaled, 1)
            for n in range(1, MOD_FIRST):
                vector(n)
            dve.wait_ge(cols_ready, 1)
            dve.wait_ge(moved, 2 * BLOCKS)
            for k in range(KT // 2, KT):
                for c, tokens in enumerate((slice(0, P), slice(P, TOK))):
                    nc.vector.tensor_scalar(hT[:, k, tokens], hT[:, k, tokens], cols[:, V_SCALE_A, k, c:c + 1],
                                            cols[:, V_SHIFT_A, k, c:c + 1], ALU.mult, ALU.add)


def gate_scalars(nc, t, sb, sem, bank):
    NS, NM = 2 * HS, 2 * HM
    W = NS + NM
    raw, nabs, y, u, lnu = [sb("gt_" + n, [P, BLOCKS, W]) for n in ("raw", "nabs", "y", "u", "lnu")]
    a, fb = sb("gt_a", [P, NS]), sb("gt_fb", [P, NM])
    sums, rest = sb("gt_sums", [P, BLOCKS, NS]), sb("gt_rest", [P, BLOCKS, NS])
    at = lambda start, n: bank[:, start:start + BLOCKS * n].rearrange("p (b n) -> p b n", n=n)
    ps, pt, pm = at(0, NS), at(BLOCKS * NS, NS), (at(2 * BLOCKS * NS, NM), at(2 * BLOCKS * NS + BLOCKS * NM, NM))
    args_ready, exps_ready, ones_added, logs_ready, steps_ready, sums_ready, lists_ready, done = (
        sem("gt_args"), sem("gt_exps"), sem("gt_ones"), sem("gt_logs"), sem("gt_steps"), sem("gt_sums_ready"), sem("gt_lists"), sem("gt_done"))
    G, sm, rows = t["gates"], t["small"], t["rows"]
    dve, act, pe = nc.vector, nc.scalar, nc.tensor

    def per_block(ap):
        return ap.unsqueeze(1).to_broadcast([P, BLOCKS, ap.shape[1]])

    def dve_steps():
        nc.vector.tensor_tensor(raw[:, :, 0:NS], sm[:, :, 0:NS], per_block(rows[:, R_DTB:R_DTB + NS]), ALU.add)
        nc.vector.tensor_scalar(fb[:, :], rows[:, R_FB:R_FB + NM], -1.0, None, ALU.mult)
        dve.drain()
        nc.vector.scalar_tensor_tensor(raw[:, :, NS:W], sm[:, :, NS + NM:NS + 2 * NM], -1.0, per_block(fb[:, :]),
                                       ALU.mult, ALU.add)
        nc.vector.tensor_tensor(G[:, :, G_LI:G_LI + NM], sm[:, :, NS:NS + NM], per_block(rows[:, R_IB:R_IB + NM]), ALU.add)
        dve.drain()
        nc.vector.tensor_scalar(u[:, :, :], raw[:, :, :], -1.0, None, ALU.mult)
        dve.drain()
        nc.vector.tensor_tensor(nabs[:, :, :], u[:, :, :], raw[:, :, :], ALU.min).then_inc(args_ready, 1)
        dve.wait_ge(exps_ready, 1)
        nc.vector.tensor_scalar(u[:, :, :], y[:, :, :], 1.0, None, ALU.add).then_inc(ones_added, 1)
        dve.wait_ge(ones_added, 1)
        nc.vector.tensor_scalar(nabs[:, :, :], u[:, :, :], 1.0, None, ALU.subtract)
        dve.drain()
        nc.vector.tensor_tensor(nabs[:, :, :], y[:, :, :], nabs[:, :, :], ALU.subtract)
        dve.drain()
        dve.wait_ge(logs_ready, 1)
        nc.vector.reciprocal(y[:, :, :], u[:, :, :])
        dve.drain()
        nc.vector.tensor_tensor(nabs[:, :, :], nabs[:, :, :], y[:, :, :], ALU.mult)
        dve.drain()
        nc.vector.tensor_tensor(nabs[:, :, :], nabs[:, :, :], lnu[:, :, :], ALU.add)
        dve.drain()
        nc.vector.scalar_tensor_tensor(nabs[:, :, :], raw[:, :, :], 0.0, nabs[:, :, :], ALU.max, ALU.add)
        dve.drain()
        nc.vector.tensor_copy(G[:, :, G_DT:G_DT + NS], nabs[:, :, 0:NS])
        nc.vector.tensor_scalar(G[:, :, G_LF:G_LF + NM], nabs[:, :, NS:W], -1.0, None, ALU.mult)
        nc.vector.scalar_tensor_tensor(G[:, :, G_DA:G_DA + NS], nabs[:, :, 0:NS], -1.0, per_block(a[:, :]),
                                       ALU.mult, ALU.mult)
        r = t["rows"]
        nc.vector.tensor_tensor(t["skip"][:, :], r[:, R_SKIP:R_SKIP + HS], r[:, R_SKIP + HS:R_SKIP + 2 * HS], ALU.add)
        nc.vector.tensor_scalar(t["nident"][:, :], t["ident"][:, :], -1.0, None, ALU.mult)
        dve.drain()
        dve.sem_inc(steps_ready, 1)

    def act_steps():
        nc.scalar.activation(a[:, :], rows[:, R_ALOG:R_ALOG + NS], ACT.Exp)
        act.wait_ge(args_ready, 1)
        nc.scalar.activation(y[:, :, :], nabs[:, :, :], ACT.Exp).then_inc(exps_ready, 1)
        act.wait_ge(ones_added, 1)
        nc.scalar.activation(lnu[:, :, :], u[:, :, :], ACT.Ln).then_inc(logs_ready, 1)

    def pe_sums():
        pe.wait_ge(steps_ready, 1)
        for d, tri in enumerate((t["triF"], t["triB"])):
            c, m = d * HS, d * HM
            nc.tensor.matmul(ps[:, :, c:c + HS], tri[:, :], G[:, :, G_DA + c:G_DA + c + HS], start=True, stop=True)
            nc.tensor.matmul(pm[0][:, :, m:m + HM], tri[:, :], G[:, :, G_LF + m:G_LF + m + HM], start=True, stop=True)
        nc.tensor.matmul(pt, t["ones"][:, :], G[:, :, G_DA:G_DA + NS], start=True, stop=True)
        last = nc.tensor.matmul(pm[1], t["ones"][:, :], G[:, :, G_LF:G_LF + NM], start=True, stop=True)
        last.then_inc(sums_ready, 1)

    def dve_lists():
        dve.wait_ge(sums_ready, 1)
        nc.vector.tensor_copy(sums[:, :, :], ps)
        nc.vector.tensor_scalar(G[:, :, G_NACS:G_NACS + NS], ps, -1.0, None, ALU.mult)
        nc.vector.tensor_copy(G[:, :, G_BC:G_BC + NM], pm[0])
        nc.vector.tensor_copy(G[:, :, G_TOT:G_TOT + NM], pm[1])
        dve.drain()
        nc.vector.tensor_tensor(rest[:, :, :], pt, sums[:, :, :], ALU.subtract)
        nc.vector.tensor_tensor(G[:, :, G_E:G_E + NM], G[:, :, G_LI:G_LI + NM], G[:, :, G_BC:G_BC + NM], ALU.subtract)
        dve.drain()
        dve.sem_inc(lists_ready, 1)

    def act_exponentials():
        act.wait_ge(lists_ready, 1)
        nc.scalar.activation(G[:, :, G_EA:G_EA + NS], sums[:, :, :], ACT.Exp)
        nc.scalar.activation(G[:, :, G_ED:G_ED + NS], pt, ACT.Exp)
        nc.scalar.activation(G[:, :, G_WD:G_WD + NS], rest[:, :, :], ACT.Exp).then_inc(done, 1)

    def pe_bank_read():
        pe.wait_ge(done, 1)

    def dve_weights():
        dve.wait_ge(done, 1)
        nc.vector.tensor_tensor(G[:, :, G_WD:G_WD + NS], G[:, :, G_WD:G_WD + NS], G[:, :, G_DT:G_DT + NS], ALU.mult)

    return (dve_steps, dve_lists, dve_weights), (act_steps, act_exponentials), (pe_sums, pe_bank_read)


def project(nc, dr, t, hT):
    T_CH, X_CH, Q_CH = COLS_T // 512, 4, 4
    with ExitStack() as ctx:
        sb = lambda n, s, d=F32: ctx.enter_context(nc.sbuf_tensor(n, s, d))
        sem = semaphores(nc, ctx)
        w = sb("w_chunk", [P, 2, KT, 512])
        ws = sb("w_small", [P, KT, 48])
        out = sb("chunk_out", [P, 2, BLOCKS, 512])
        cw = sb("conv_par", [P, 4, 16])
        cc = sb("conv_cur", [P, 4, 8])
        acc = sb("conv_acc", [P, 2, TOK])
        big = sb("tile_out", [P, 2, 4, TOK])
        pst = [ctx.enter_context(nc.psum_tensor(f"pj{i}", [P, 1024], F32)) for i in range(4)]
        banks = [pst[i // 2][:, (i % 2) * 512:(i % 2) * 512 + 512] for i in range(5)]
        w_in = [sem("w_in0"), sem("w_in1")]
        par_in, small_mm, small_moved = sem("par_in"), sem("small_mm"), sem("small_moved")
        t_mm, x_mm, q_mm = sem("t_mm"), sem("x_mm"), sem("q_mm")
        t_bank_free, x_tile_free, q_tile_free = sem("t_bank_free"), sem("x_tile_free"), sem("q_tile_free")
        acc_ready, x_act = sem("acc_ready"), sem("x_act")
        t_free, x_free, q_free = sem("t_out_free"), sem("x_out_free"), sem("q_out_free")
        t_out, x_out, q_out = [[sem(f"{n}_out{j}") for j in range(2)] for n in "txq"]
        (dve_steps, dve_lists, dve_weights), (act_steps, act_exponentials), (pe_sums, pe_bank_read) = gate_scalars(
            nc, t, sb, sem, pst[3][:, 0:512])
        block = ctx.enter_context(nc.Block())

        def w_src(c):
            return dr["w_big"][bass.ds(c, 1)].rearrange("o p k n -> p (o k) n")

        @block.sync
        def _(sp):
            sp.dma_start(ws[:, :, :], dr["w_small"]).then_inc(par_in, 16)
            sp.dma_start(cw[:, :, :], dr["convT"]).then_inc(par_in, 16)
            for j in range(2):
                sp.dma_start(w[:, j], dr["w_big"][j]).then_inc(w_in[j], 16)
            with sp.Fori(0, T_CH // 2) as i:
                for j in range(2):
                    sp.wait_ge(t_mm, i * (2 * BLOCKS) + (j + 1) * BLOCKS)
                    sp.dma_start(w[:, j], w_src(i * 2 + (j + 2))).then_inc(w_in[j], 16)
            with sp.Fori(0, X_CH // 2) as i:
                for j in range(2):
                    sp.wait_ge(x_mm, i * 8 + 4 * (j + 1))
                    sp.dma_start(w[:, j], w_src(i * 2 + (j + 2 + T_CH))).then_inc(w_in[j], 16)
            for j in range(2):
                sp.wait_ge(q_mm, 4 * (j + 1))
                sp.dma_start(w[:, j], dr["w_big"][T_CH + X_CH + 2 + j]).then_inc(w_in[j], 16)

        @block.gpsimd
        def _(pool):
            with pool.Fori(0, T_CH // 2) as i:
                for j in range(2):
                    pool.wait_ge(t_bank_free, i * (2 * BLOCKS) + (5 + (j + 1) * BLOCKS))
                    pool.wait_ge(small_moved, 1)
                    pool.dma_start(dr["proj"].rearrange("b p n -> p b n")[:, :, bass.ds((i * 2 + j) * 512, 512)],
                                   out[:, j]).then_inc(t_out[j], 16)
                    pool.wait_ge(t_out[j], i * 16 + 16)
                    pool.sem_inc(t_free, 1)
            with pool.Fori(0, X_CH // 2) as i:
                for j in range(2):
                    pool.wait_ge(x_act, i * 8 + (2 + 4 * (j + 1)))
                    pool.wait_ge(small_moved, 1)
                    pool.dma_start(dr["xbcT"].rearrange("m p t -> p m t")[:, bass.ds(i * 8 + 4 * j, 4)], big[:, j]).then_inc(x_out[j], 16)
                    pool.wait_ge(x_out[j], i * 16 + 16)
                    pool.sem_inc(x_free, 1)
            with pool.Fori(0, Q_CH // 2) as i:
                for j in range(2):
                    pool.wait_ge(q_tile_free, i * 8 + (4 + 4 * (j + 1)))
                    pool.wait_ge(small_moved, 1)
                    pool.dma_start(dr["qkT"].rearrange("m p t -> p m t")[:, bass.ds(i * 8 + 4 * j, 4)], big[:, j]).then_inc(q_out[j], 16)
                    pool.wait_ge(q_out[j], i * 16 + 16)
                    pool.sem_inc(q_free, 1)

        @block.tensor
        def _(pe):
            pe.wait_ge(par_in, 32)
            for b in range(BLOCKS):
                for k in range(KT):
                    last = nc.tensor.matmul(banks[0][:, b * 48:(b + 1) * 48], hT[:, k, b * P:(b + 1) * P], ws[:, k, :],
                                            start=(k == 0), stop=(k == KT - 1))
            last.then_inc(small_mm, 1)
            pe.wait_ge(small_moved, 1)

            def token_chunks(i):
                for j in range(2):
                    pe.wait_ge(w_in[j], i * 16 + 16)
                    for b in range(BLOCKS):
                        pe.wait_ge(t_bank_free, i * (2 * BLOCKS) + (j * BLOCKS + b + 1))
                        for k in range(KT):
                            last = nc.tensor.matmul(banks[b], hT[:, k, b * P:(b + 1) * P], w[:, j, k, :],
                                                    start=(k == 0), stop=(k == KT - 1))
                        last.then_inc(t_mm, 1)

            with pe.Fori(0, T_CH // 2 - 1) as i:
                token_chunks(i)
            pe_sums()
            token_chunks(T_CH // 2 - 1)
            pe_bank_read()
            pe.wait_ge(t_bank_free, 5 + T_CH * BLOCKS)

            def channel_tiles(i, done_pairs, tile_free, done):
                for j in range(2):
                    pe.wait_ge(w_in[j], i * 16 + 16 * (done_pairs + 1))
                    for m in range(4):
                        pe.wait_ge(tile_free, i * 8 + (4 * j + m + 1))
                        for k in range(KT):
                            nc.tensor.matmul(pst[m][:, 0:LAT], w[:, j, k, m * P:(m + 1) * P], hT[:, k, P:TOK],
                                             start=(k == 0), stop=(k == KT - 1))
                        for k in range(KT):
                            last = nc.tensor.matmul(pst[m][:, LAT:TOK], w[:, j, k, m * P:(m + 1) * P], hT[:, k, 0:P],
                                                    start=(k == 0), stop=(k == KT - 1))
                        last.then_inc(done, 1)

            with pe.Fori(0, X_CH // 2) as i:
                channel_tiles(i, T_CH // 2, x_tile_free, x_mm)
            pe.wait_ge(x_tile_free, 4 + 4 * X_CH)
            with pe.Fori(0, Q_CH // 2) as i:
                channel_tiles(i, (T_CH + X_CH) // 2, q_tile_free, q_mm)

        @block.scalar
        def _(act):
            act.sem_inc(t_bank_free, 5)
            act.sem_inc(q_tile_free, 4)
            for free in (t_free, x_free, q_free):
                act.sem_inc(free, 2)
            act.wait_ge(small_mm, 1)
            nc.scalar.copy(t["small"][:, :, :].rearrange("p b n -> p (b n)"), banks[0][:, 0:48 * BLOCKS]).then_inc(small_moved, 1)
            act_steps()

            def token_results(i):
                for j in range(2):
                    act.wait_ge(t_free, i * 2 + (j + 1))
                    for b in range(BLOCKS):
                        act.wait_ge(t_mm, i * (2 * BLOCKS) + (j * BLOCKS + b + 1))
                        nc.scalar.copy(out[:, j, b, :], banks[b]).then_inc(t_bank_free, 1)

            with act.Fori(0, T_CH // 2 - 1) as i:
                token_results(i)
            act_exponentials()
            token_results(T_CH // 2 - 1)
            with act.Fori(0, X_CH // 2) as i:
                for j in range(2):
                    act.wait_ge(x_free, i * 2 + (j + 1))
                    for m in range(4):
                        act.wait_ge(acc_ready, i * 8 + (4 * j + m + 1))
                        nc.scalar.activation(big[:, j, m, P:TOK], acc[:, m % 2, 0:LAT], ACT.Silu)
                        nc.scalar.activation(big[:, j, m, 0:P], acc[:, m % 2, LAT:TOK], ACT.Silu).then_inc(x_act, 1)
            act.wait_ge(x_free, X_CH + 2)
            with act.Fori(0, Q_CH // 2) as i:
                for j in range(2):
                    act.wait_ge(q_free, i * 2 + (j + 1))
                    for m in range(4):
                        act.wait_ge(q_mm, i * 8 + (4 * j + m + 1))
                        nc.scalar.copy(big[:, j, m, P:TOK], pst[m][:, 0:LAT])
                        nc.scalar.copy(big[:, j, m, 0:P], pst[m][:, LAT:TOK]).then_inc(q_tile_free, 1)

        @block.vector
        def _(dve):
            dve.sem_inc(x_tile_free, 4)
            dve.sem_inc(x_act, 2)
            dve.wait_ge(small_moved, 1)
            dve_steps()
            dve_lists()
            dve_weights()
            dve.wait_ge(par_in, 32)
            with dve.Fori(0, X_CH // 2) as i:
                nc.vector.tensor_copy(cc[:, :, :], cw[:, :, bass.ds(i * 8, 8)])
                dve.drain()
                for n in range(8):
                    m = n % 4
                    dve.wait_ge(x_mm, i * 8 + (n + 1))
                    dve.wait_ge(x_act, i * 8 + (n + 1))
                    lat = acc[:, n % 2, 0:LAT]
                    pro = acc[:, n % 2, LAT:TOK]
                    nc.vector.tensor_scalar(acc[:, n % 2, :], pst[m][:, 0:TOK], cc[:, 1, n:n + 1], cc[:, 3, n:n + 1],
                                            ALU.mult, ALU.add)
                    dve.drain()
                    grid = lat.rearrange("p (r g) -> p r g", g=GRID_W)
                    u = pst[m][:, 0:LAT].rearrange("p (r g) -> p r g", g=GRID_W)
                    nc.vector.scalar_tensor_tensor(grid[:, :, 1:], u[:, :, 0:GRID_W - 1], cc[:, 0, n:n + 1],
                                                   grid[:, :, 1:], ALU.mult, ALU.add)
                    nc.vector.scalar_tensor_tensor(pro[:, 1:], pst[m][:, LAT:TOK - 1], cc[:, 0, n:n + 1],
                                                   pro[:, 1:], ALU.mult, ALU.add)
                    dve.drain()
                    nc.vector.scalar_tensor_tensor(grid[:, :, 0:GRID_W - 1], u[:, :, 1:], cc[:, 2, n:n + 1],
                                                   grid[:, :, 0:GRID_W - 1], ALU.mult, ALU.add)
                    nc.vector.scalar_tensor_tensor(pro[:, 0:P - 1], pst[m][:, LAT + 1:TOK], cc[:, 2, n:n + 1],
                                                   pro[:, 0:P - 1], ALU.mult, ALU.add).then_inc(acc_ready, 1)
                    dve.wait_ge(acc_ready, i * 8 + (n + 1))
                    dve.sem_inc(x_tile_free, 1)


def scan(nc, dr, t, kind):
    full = kind != "back"
    dirs = (0, 1) if full else (1,)
    steps = {"prompt": (0, 1), "back": (1,), "sample": (0,)}[kind]
    prior = kind != "prompt"
    N = {"prompt": 1, "back": CHUNKS - 1, "sample": CHUNKS}[kind]
    mask_t, mask = (t["maskF_16"], t["maskB_16"]), (t["maskB"], t["maskF"])
    with ExitStack() as ctx:
        pre = kind[0] + "_"
        sb = lambda n, s, d=F32: ctx.enter_context(nc.sbuf_tensor(pre + n, s, d))
        sem = semaphores(nc, ctx, pre)

        xbcT, qkT, v, H, C, mp = [t[n] for n in ("scan_xbcT", "scan_qkT", "scan_v", "scan_H", "scan_C", "scan_m")]
        g = sb("g", [P, G_N])
        xs, Bt, Kt = sb("xs", [P, D]), sb("Bt", [P, NG, P]), sb("Kt", [P, HM, DM])
        if full:
            L, W = sb("L", [P, 2, 2, 4, P]), sb("W", [P, 2, 4, P])
        if kind == "back":
            m_bias, m_gain = sb("m_bias", [2, V_ROWS * D]), sb("m_gain", [2, 3, D])
        y, yt, xw = sb("y", [P, D]), sb("yt", [P, D]), sb("xw", [P, 2, D])
        emax, me, mx, nmx, mn, rs, den, r, rw = [sb(n, [P, 2, HM]) for n in (
            "emax", "me", "mx", "nmx", "mn", "rs", "den", "r", "rw")]
        args, ex = sb("args", [P, 4, 2, HM]), sb("ex", [P, 4, 2, HM])
        WA, WI, DN, KW = range(4)
        Em, Pc, PcT = sb("Em", [P, 2, HM, P]), sb("Pc", [P, HM, P]), sb("PcT", [P, HM, P])
        hm, Ks = sb("hm", [P, HM, DM]), sb("Ks", [P, 2, HM, DM])
        bank = [ctx.enter_context(nc.psum_tensor(f"{pre}bank{i}", [P, 1024], F32)) for i in range(4)]
        half = [bank[i // 2][:, (i % 2) * 512:(i % 2) * 512 + 512] for i in range(8)]
        x_in, qk_in, v_in, cur_ready, init_ready = sem("x_in"), sem("qk_in"), sem("v_in"), sem("cur_ready"), sem("init_ready")
        xs_turned, B_turned, xs_ready, B_ready, K_turned, K_ready = (
            sem("xs_turned"), sem("B_turned"), sem("xs_ready"), sem("B_ready"), sem("K_turned"), sem("K_ready"))
        xw_ready, state_mm, H_new = sem("xw_ready"), [sem("state_mm0"), sem("state_mm1")], [sem("H_new0"), sem("H_new1")]
        E_rows, args_ready, ex_ready, Ks_ready = sem("E_rows"), sem("args_ready"), sem("ex_ready"), sem("Ks_ready")
        mstate_mm, C_new = sem("mstate_mm"), sem("C_new")
        chunk_done = sem("chunk_done")
        if prior:
            state_in = sem("state_in")
        m_rows = t["mod_rows"]
        if kind == "sample":
            norms = sb("norms", [P, HM, 2, 2])
            mod_out, norms_ready = sem("mod_out"), sem("norms_ready")
            H_in, C_in, m_in = sem("H_in"), sem("C_in"), sem("m_in")
        if kind == "back":
            stored = sem("stored")
            mod_w, mod_par, mod_mm, pool_passed = [sem("mod_w0"), sem("mod_w1")], sem("mod_par"), sem("mod_mm"), sem("pool_passed")
            mod_bank_free = sem("mod_bank_free")
            mod_w_ready = sem("mod_w_ready")
        if kind == "prompt":
            state_out, mod_w = sem("state_out"), [sem("mod_w0"), sem("mod_w1")]
        sp_passed, dve_passed = sem("sp_passed"), sem("dve_passed")
        if full:
            y_read, norm_mm = sem("y_read"), sem("norm_mm")
            y_out, hm_out = sem("y_out"), sem("hm_out")
            scores, decay, decays, W_ready, y_mm, y_done = (
                sem("scores"), sem("decay"), sem("decays"), sem("W_ready"), sem("y_mm"), sem("y_done"))
            yoff_mm, yoff_used = [sem("yoff_mm0"), sem("yoff_mm1")], [sem("yoff_used0"), sem("yoff_used1")]
            qk_mm, X_ready, inter_mm, inter_used, P_turned, PT_ready, hv_mm, hm_done, P_mixed = (
                sem("qk_mm"), sem("X_ready"), sem("inter_mm"), sem("inter_used"), sem("P_turned"), sem("PT_ready"),
                sem("hv_mm"), sem("hm_done"), sem("P_mixed"))
        block = ctx.enter_context(nc.Block())
        NM = len(steps) * HM
        def loop(eng, body):
            if N == 1:
                body(0)
            else:
                with eng.Fori(0, N) as i:
                    body(i)

        def blk(i):
            return {"prompt": i, "back": CHUNKS - i, "sample": i + 1}[kind]

        def at(ap, i):
            return ap[i] if isinstance(i, int) else row(ap[bass.ds(i, 1)])

        flat_c = lambda d: C[d][:, :, :, :].rearrange("p h k c -> p (h k c)")

        @block.sync
        def _(sp):
            def load_x(b):
                tokens = bass.ds(b * P, P) if not isinstance(b, int) else slice(b * P, b * P + P)
                sp.dma_start(xbcT[:, :, :], dr["xbcT"].rearrange("m p t -> p m t")[:, :, tokens]).then_inc(x_in, 16)

            def load_qk(b):
                tokens = bass.ds(b * P, P) if not isinstance(b, int) else slice(b * P, b * P + P)
                sp.dma_start(qkT[:, :, :], dr["qkT"].rearrange("m p t -> p m t")[:, :, tokens]).then_inc(qk_in, 16)

            def load_v(b):
                sp.dma_start(v[:, :, 0:DM], at(dr["proj"], b)[:, COL_V:COL_V + D].rearrange("p (h c) -> p h c", c=DM)).then_inc(v_in, 16)

            def store_H(i):
                sp.dma_start(at(dr["back_ssd"], i), H[1][:, :]).then_inc(stored, 16)

            def store_C(i):
                sp.dma_start(at(dr["back_c"], i), flat_c(1)).then_inc(stored, 16)
                sp.dma_start(at(dr["back_m"], i), mp[:, 1, :]).then_inc(stored, 16)

            if kind == "prompt":
                load_x(0)
                load_qk(0)
                load_v(0)
            else:
                for loaded in (x_in, qk_in, v_in):
                    sp.sem_inc(loaded, 16)
            if kind == "sample":
                for loaded in (H_in, C_in, m_in):
                    sp.sem_inc(loaded, 16)
            if prior:
                d = steps[0]
                sp.dma_start(H[d][:, :], dr["state_ssd"][d]).then_inc(state_in, 16)
                sp.dma_start(flat_c(d), dr["state_c"][d]).then_inc(state_in, 16)

            def body(i, more):
                follows = more or kind != "sample"
                b = blk(i + 1) if more else {"prompt": CHUNKS, "back": 1}.get(kind)
                if follows:
                    sp.wait_ge({"prompt": scores, "sample": yoff_mm[1]}[kind] if full else B_turned, i + 1)
                    sp.sem_inc(sp_passed, 1)
                    load_x(b)
                if more and kind == "sample":
                    sp.dma_start(H[1][:, :], at(dr["back_ssd"], CHUNKS - 2 - i)).then_inc(H_in, 16)
                if full:
                    sp.wait_ge(y_done, i + 1)
                    sp.sem_inc(sp_passed, 1)
                    sp.dma_start(at(dr["y_ssd"], blk(i)), y[:, :]).then_inc(y_out, 16)
                if more and kind == "sample":
                    sp.wait_ge(args_ready, i + 1)
                    sp.sem_inc(sp_passed, 1)
                    sp.dma_start(mp[:, 1, :], at(dr["back_m"], CHUNKS - 2 - i)).then_inc(m_in, 16)
                if follows:
                    sp.wait_ge({"prompt": qk_mm, "sample": inter_mm}[kind] if full else K_turned, i + 1)
                    sp.sem_inc(sp_passed, 1)
                    load_qk(b)
                if more and kind == "sample":
                    sp.dma_start(flat_c(1), at(dr["back_c"], CHUNKS - 2 - i)).then_inc(C_in, 16)
                if kind == "prompt":
                    for d in range(2):
                        sp.wait_ge(H_new[d], 1)
                        sp.dma_start(dr["out_ssd"][d], H[d][:, :]).then_inc(state_out, 16)
                if full:
                    sp.wait_ge(hm_done, i + 1)
                    sp.sem_inc(sp_passed, 1)
                    sp.dma_start(at(dr["y_mlstm"], blk(i)), hm[:, :, :].rearrange("p h c -> p (h c)")).then_inc(hm_out, 16)
                if more and kind == "back":
                    sp.wait_ge(H_new[1], i + 1)
                    sp.sem_inc(sp_passed, 1)
                    store_H(i + 1)
                if kind == "prompt":
                    sp.wait_ge(C_new, 2 * HM)
                    sp.dma_start(dr["out_c"][0], flat_c(0)).then_inc(state_out, 16)
                if follows:
                    sp.wait_ge(mstate_mm, i * (2 * NM) + 2 * NM)
                    sp.sem_inc(sp_passed, 1)
                    load_v(b)
                if more and kind == "back":
                    sp.wait_ge(chunk_done, i + 2)
                    sp.sem_inc(sp_passed, 1)
                    store_C(i + 1)

            if kind == "back":
                sp.wait_ge(state_in, 32)
                sp.wait_ge(init_ready, 1)
                store_H(0)
                store_C(0)
            if N > 1:
                with sp.Fori(0, N - 1) as i:
                    body(i, True)
            body(N - 1, False)
            if kind == "prompt":
                sp.wait_ge(C_new, 4 * HM)
                sp.dma_start(dr["out_c"][1], flat_c(1)).then_inc(state_out, 16)
                sp.wait_ge(chunk_done, 2)
                sp.dma_start(dr["out_m"], mp[0:1, :, :].rearrange("p d h -> p (d h)")).then_inc(state_out, 16)
                sp.wait_ge(state_out, 80)
            if kind == "back":
                sp.wait_ge(stored, 48 * N)
            if kind != "sample":
                for loaded in (x_in, qk_in, v_in):
                    sp.wait_ge(loaded, 16 * (N + 1))
            if full:
                sp.wait_ge(y_out, 16 * (N + 1))
                sp.wait_ge(hm_out, 16 * (N + 1))

        if kind != "sample":
            wm = t["wm"]
        if kind == "prompt":
            @block.gpsimd
            def _(pool):
                pool.wait_ge(v_in, 16)
                for j in range(2):
                    pool.dma_start(wm[:, j], dr["w_mod"][MOD_FIRST + j]).then_inc(mod_w[j], 16)
                for j in range(2):
                    pool.wait_ge(mod_w[j], 16)

        if kind == "back":
            @block.gpsimd
            def _(pool):
                pool.sem_inc(mod_w_ready, 2)
                pool.wait_ge(v_in, 16)
                pool.dma_start(m_bias[:, :], dr["b_mod"][:, 2 * D:].partition_broadcast(2)).then_inc(mod_par, 16)
                pool.dma_start(m_gain[:, :, :].rearrange("p g n -> p (g n)"), dr["gain_rows"][:, D:].partition_broadcast(2)).then_inc(mod_par, 16)
                with pool.Fori(0, N) as i:
                    for j in range(2):
                        pool.wait_ge(mod_mm, i * 2 + (j + 1))
                        pool.sem_inc(pool_passed, 1)
                        pool.dma_start(wm[:, j], dr["w_mod"][bass.ds(i * 2 + (MOD_FIRST + 2 + j), 1)].rearrange(
                            "o p k n -> p (o k) n")).then_inc(mod_w[j], 16)
                    for j in range(2):
                        pool.wait_ge(mod_w[j], i * 16 + 16)
                        pool.sem_inc(mod_w_ready, 1)

        if kind == "sample":
            @block.gpsimd
            def _(pool):
                for b in range(BLOCKS):
                    c = 0 if b == 0 else 1
                    pool.dma_start(dr["mod_rows"][b], m_rows[c:c + 1, :]).then_inc(mod_out, 16)
                pool.wait_ge(mod_out, 16 * BLOCKS)

        @block.tensor
        def _(pe):
            ident = t["ident"]

            def modulation(i, j):
                pe.wait_ge(mod_w_ready, i * 2 + (j + 1))
                pe.wait_ge(mod_bank_free, i * 2 + (j + 1))
                for k in range(KT):
                    last = nc.tensor.matmul(half[6 + j][0:2, :], t["cv"][:, k, :], wm[:, j, k, :], start=(k == 0), stop=(k == KT - 1))
                last.then_inc(mod_mm, 1)

            def body(i):
                pe.wait_ge(x_in, i * 16 + 16)
                pe.wait_ge(cur_ready, i + 1)
                pe.wait_ge(chunk_done, i + 1)
                for k in range(KT):
                    last = nc.tensor.transpose(bank[0][:, k * P:(k + 1) * P], xbcT[:, k, :], ident[:, :])
                last.then_inc(xs_turned, 1)
                for k in range(NG):
                    last = nc.tensor.transpose(half[2][:, k * P:(k + 1) * P], xbcT[:, KT + k, :], ident[:, :])
                last.then_inc(B_turned, 1)
                if full:
                    for q in range(NG):
                        last = nc.tensor.matmul(half[3][:, q * P:(q + 1) * P], xbcT[:, KT + q, :], xbcT[:, KT + NG + q, :],
                                                start=True, stop=True)
                    last.then_inc(scores, 1)

                    def decay_rows(q):
                        for d in range(2):
                            if q:
                                pe.wait_ge(decays, i * (2 * NG) + (2 * q - 1 + d))
                            out = half[4 + d].rearrange("p (h s) -> p h s", h=4)
                            nc.tensor.matmul(out, t["ident_16"][:, :], mask_t[d][:, :].unsqueeze(1).to_broadcast([P, 4, P]),
                                             start=True, stop=False)
                            for h in range(4):
                                c = d * HS + q * 4 + h
                                last = nc.tensor.matmul(out[:, h, :], g[:, G_NACS + c:G_NACS + c + 1].to_broadcast([P, P]),
                                                        t["nident"][:, :], start=False, stop=(h == 3))
                            last.then_inc(decay, 1)

                    decay_rows(0)
                    pe.wait_ge(xs_ready, i + 1)
                    for q in range(NG):
                        if q + 1 < NG:
                            decay_rows(q + 1)
                        pe.wait_ge(W_ready, i * NG + (q + 1))
                        for h in range(4):
                            c = (q * 4 + h) * PS
                            last = nc.tensor.matmul(bank[3][:, c:c + PS], W[:, q % 2, h, :], xs[:, c:c + PS], start=True, stop=True)
                        last.then_inc(y_mm, 1)
                    if prior:
                        pe.wait_ge(state_in, 32)
                        pe.wait_ge(H_in, i * 16 + 16)
                        for d in range(2):
                            for q in range(NG):
                                last = nc.tensor.matmul(bank[d][:, q * 256:(q + 1) * 256], xbcT[:, KT + NG + q, :],
                                                        H[d][:, q * 256:(q + 1) * 256], start=True, stop=True)
                            last.then_inc(yoff_mm[d], 1)
                pe.wait_ge(B_ready, i + 1)
                pe.wait_ge(xw_ready, i + 1)
                for n, d in enumerate(steps):
                    if n == 0 and full:
                        pe.wait_ge(decays, i * (2 * NG) + 2 * NG)
                    if n == 1:
                        pe.wait_ge(xs_ready, i + 1)
                        if full and prior:
                            pe.wait_ge(yoff_used[0], i + 1)
                    to = bank[(2, 0)[n]]
                    for q in range(NG):
                        last = nc.tensor.matmul(to[:, q * 256:(q + 1) * 256], Bt[:, q, :], xw[:, d, q * 256:(q + 1) * 256],
                                                start=True, stop=True)
                    last.then_inc(state_mm[d], 1)
                if full and prior:
                    pe.wait_ge(yoff_used[1], i + 1)
                if full:
                    pe.wait_ge(W_ready, i * NG + NG)
                pe.wait_ge(qk_in, i * 16 + 16)
                for k in range(KT):
                    last = nc.tensor.transpose(bank[1][:, k * P:(k + 1) * P], qkT[:, KT + k, :], ident[:, :])
                last.then_inc(K_turned, 1)
                if kind == "back":
                    modulation(i, 0)
                pe.wait_ge(H_new[steps[0]], i + 1)
                for d in dirs:
                    for h in range(HM):
                        c = G_E + d * HM + h
                        last = nc.tensor.matmul(half[4 + d][:, h * P:(h + 1) * P], g[:, c:c + 1].to_broadcast([P, P]), ident[:, :],
                                                start=True, stop=True)
                last.then_inc(E_rows, 1)
                if kind == "back":
                    modulation(i, 1)
                if full:
                    pe.wait_ge(y_read, i + 1)
                    for h in range(HM):
                        for k in range(2):
                            last = nc.tensor.matmul(half[6][:, h * P:(h + 1) * P], qkT[:, 2 * h + k, :], qkT[:, KT + 2 * h + k, :],
                                                    start=(k == 0), stop=(k == 1))
                    last.then_inc(qk_mm, 1)
                    if prior:
                        if len(steps) == 2:
                            pe.wait_ge(H_new[steps[1]], i + 1)
                        pe.wait_ge(K_ready, i + 1)
                        pe.wait_ge(C_in, i * 16 + 16)
                        pe.wait_ge(norms_ready, i + 1)
                        for h in range(HM):
                            for k in range(2):
                                last = nc.tensor.matmul(half[7][:, 2 * h:2 * h + 2], qkT[:, 2 * h + k, :], norms[:, h, k, :],
                                                        start=(k == 0), stop=(k == 1))
                        last.then_inc(norm_mm, 1)
                        for d in range(2):
                            for h in range(HM):
                                for k in range(2):
                                    last = nc.tensor.matmul(bank[d][:, h * DM:(h + 1) * DM], qkT[:, 2 * h + k, :], C[d][:, h, k, 0:DM],
                                                            start=(k == 0), stop=(k == 1))
                        last.then_inc(inter_mm, 1)
                    pe.wait_ge(P_mixed, i + 1)
                    for h in range(HM):
                        last = nc.tensor.transpose(half[4][:, h * P:(h + 1) * P], Pc[:, h, :], ident[:, :])
                    last.then_inc(P_turned, 1)
                    pe.wait_ge(PT_ready, i + 1)
                    pe.wait_ge(v_in, i * 16 + 16)
                    for h in range(HM):
                        last = nc.tensor.matmul(bank[3][:, h * DM:(h + 1) * DM], PcT[:, h, :], v[:, h, 0:DM],
                                                start=True, stop=True)
                    last.then_inc(hv_mm, 1)
                    if prior:
                        pe.wait_ge(inter_used, i + 1)
                pe.wait_ge(Ks_ready, i + 1)
                if not full:
                    pe.wait_ge(v_in, i * 16 + 16)
                if kind == "prompt":
                    pe.wait_ge(H_new[1], i + 1)
                for u in range(2 * NM):
                    d, h, k = steps[u // (2 * HM)], u // 2 % HM, u % 2
                    if u >= 4:
                        pe.wait_ge(C_new, i * (2 * NM) + (u - 3))
                    nc.tensor.matmul(half[u % 4][:, 0:CE], Ks[:, d, h, k * P:(k + 1) * P], v[:, h, :],
                                     start=True, stop=True).then_inc(mstate_mm, 1)

            loop(pe, body)
            if kind == "back":
                for j in range(2):
                    modulation(N, j)

        @block.scalar
        def _(act):
            def body(i):
                act.wait_ge(xs_turned, i + 1)
                nc.scalar.copy(xs[:, :], bank[0][:, :]).then_inc(xs_ready, 1)
                act.wait_ge(B_turned, i + 1)
                nc.scalar.copy(Bt[:, :, :].rearrange("p q n -> p (q n)"), half[2]).then_inc(B_ready, 1)
                if full:
                    for q in range(NG):
                        if q >= 2:
                            act.wait_ge(W_ready, i * NG + (q - 1))
                        for d in range(2):
                            act.wait_ge(decay, i * (2 * NG) + (2 * q + d + 1))
                            for h in range(4):
                                c = G_NACS + d * HS + q * 4 + h
                                last = nc.scalar.activation(L[:, q % 2, d, h, :], half[4 + d][:, h * P:(h + 1) * P], ACT.Exp,
                                                            bias=g[:, c:c + 1])
                            last.then_inc(decays, 1)
                act.wait_ge(K_turned, i + 1)
                nc.scalar.copy(Kt[:, :, :].rearrange("p h c -> p (h c)"), bank[1][:, :]).then_inc(K_ready, 1)
                act.wait_ge(args_ready, i + 1)
                nc.scalar.activation(ex[:, :, :, :], args[:, :, :, :], ACT.Exp).then_inc(ex_ready, 1)
                if full:
                    for d in range(2):
                        for h in range(HM):
                            last = nc.scalar.activation(Em[:, d, h, :], Em[:, d, h, :], ACT.Exp, bias=nmx[:, d, h:h + 1])
                    last.then_inc(X_ready, 1)
                    act.wait_ge(P_turned, i + 1)
                    nc.scalar.copy(PcT[:, :, :].rearrange("p h s -> p (h s)"), half[4]).then_inc(PT_ready, 1)

            loop(act, body)

        @block.vector
        def _(dve):
            if kind == "back":
                nc.vector.tensor_copy(mp[:, 1, :], t["rows"][:, R_M0 + HM:R_M0 + 2 * HM])
            elif kind == "sample":
                nc.vector.tensor_copy(mp[:, 0, :], t["rows"][:, R_M0:R_M0 + HM])
            else:
                nc.vector.memset(mp[:, :, :], 0.0)
                nc.vector.memset(v[:, :, DM:CE], 1.0)
            nc.vector.memset(args[:, :, :, :], 0.0)
            dve.drain()
            dve.sem_inc(init_ready, 1)
            dve.sem_inc(chunk_done, 1)
            if full:
                dve.sem_inc(y_out, 16)
                dve.sem_inc(hm_out, 16)
            if kind == "back":
                dve.sem_inc(mod_bank_free, 2)
            sd = slice(dirs[0], dirs[-1] + 1)

            def biased(i, j):
                dve.wait_ge(mod_par, 32)
                dve.wait_ge(mod_mm, i * 2 + (j + 1))
                dve.sem_inc(dve_passed, 1)
                start = i * 1024 + 512 * j
                at = slice(start, start + 512) if isinstance(i, int) else bass.ds(start, 512)
                nc.vector.tensor_tensor(m_rows[:, at], half[6 + j][0:2, :], m_bias[:, at], ALU.add).then_inc(mod_bank_free, 1)

            def heads(ap):
                return ap.rearrange("p (h c) -> p h c", c=PS)

            def body(i):
                b = i if kind == "prompt" else dve.snap(blk(i))
                G = t["gates"]
                nc.vector.tensor_copy(g[:, :], G[:, 0, :] if kind == "prompt" else G[:, bass.ds(b, 1), :].rearrange(
                    "p o n -> p (o n)"))
                dve.drain()
                dve.sem_inc(cur_ready, 1)
                dve.wait_ge(xs_ready, i + 1)
                for d in steps:
                    c = G_WD + d * HS
                    nc.vector.tensor_tensor(heads(xw[:, d, :]), heads(xs[:, :]), bc_last(g[:, c:c + HS], PS), ALU.mult)
                dve.drain()
                dve.sem_inc(xw_ready, 1)
                if full:
                    for q in range(NG):
                        dve.wait_ge(decays, i * (2 * NG) + (2 * q + 2))
                        dve.wait_ge(scores, i + 1)
                        if q >= 2:
                            dve.wait_ge(y_mm, i * NG + (q - 1))
                        dt = lambda d, h: g[:, G_DT + d * HS + q * 4 + h:G_DT + d * HS + q * 4 + h + 1]
                        for h in range(4):
                            nc.vector.tensor_scalar(L[:, q % 2, 0, h, :], L[:, q % 2, 0, h, :], dt(0, h), None, ALU.mult)
                        dve.drain()
                        for h in range(4):
                            nc.vector.scalar_tensor_tensor(L[:, q % 2, 1, h, :], L[:, q % 2, 1, h, :], dt(1, h), L[:, q % 2, 0, h, :],
                                                           ALU.mult, ALU.add)
                        dve.drain()
                        last = nc.vector.tensor_tensor(W[:, q % 2], L[:, q % 2, 1],
                                                       half[3][:, q * P:(q + 1) * P].unsqueeze(1).to_broadcast([P, 4, P]), ALU.mult)
                        last.then_inc(W_ready, 1)
                    nc.vector.tensor_tensor(heads(yt[:, :]), heads(xs[:, :]), bc_last(t["skip"][:, :], PS), ALU.mult)
                    dve.drain()
                    dve.wait_ge(y_mm, i * NG + NG)
                    dve.wait_ge(y_out, i * 16 + 16)
                    nc.vector.tensor_tensor(y[:, :], yt[:, :], bank[3][:, :], ALU.add).then_inc(y_read, 1)
                    if prior:
                        for d in range(2):
                            dve.drain()
                            dve.wait_ge(yoff_mm[d], i + 1)
                            c = G_EA + d * HS
                            nc.vector.tensor_tensor(heads(yt[:, :]), heads(bank[d][:, :]), bc_last(g[:, c:c + HS], PS),
                                                    ALU.mult).then_inc(yoff_used[d], 1)
                            dve.drain()
                            nc.vector.tensor_tensor(y[:, :], y[:, :], yt[:, :], ALU.add)
                    dve.drain()
                    dve.sem_inc(y_done, 1)
                if prior:
                    dve.wait_ge(state_in, 32)
                if kind == "back":
                    dve.wait_ge(stored, i * 48 + 48)
                for n, d in enumerate(steps):
                    c = G_ED + d * HS
                    dve.wait_ge(state_mm[d], i + 1)
                    if prior:
                        nc.vector.tensor_tensor(heads(H[d][:, :]), heads(H[d][:, :]), bc_last(g[:, c:c + HS], PS), ALU.mult)
                        dve.drain()
                        nc.vector.tensor_tensor(H[d][:, :], H[d][:, :], bank[(2, 0)[n]][:, :], ALU.add).then_inc(H_new[d], 1)
                    else:
                        nc.vector.tensor_copy(H[d][:, :], bank[(2, 0)[n]][:, :]).then_inc(H_new[d], 1)
                if kind == "sample":
                    dve.wait_ge(C_in, i * 16 + 16)
                    for d in range(2):
                        nc.vector.tensor_copy(norms[:, :, :, d:d + 1], C[d][:, :, :, DM:CE])
                    dve.drain()
                    dve.sem_inc(norms_ready, 1)
                dve.wait_ge(E_rows, i + 1)
                if kind == "sample":
                    dve.wait_ge(m_in, i * 16 + 16)
                for d in dirs:
                    E = half[4 + d].rearrange("p (h s) -> p h s", h=HM)
                    nc.vector.tensor_reduce(emax[:, d, :], E, AX, ALU.max)
                    if full:
                        nc.vector.tensor_tensor(Em[:, d, :, :], E, mask[d][:, :].unsqueeze(1).to_broadcast([P, HM, P]), ALU.add)
                        dve.drain()
                        nc.vector.tensor_reduce(me[:, d, :], Em[:, d, :, :], AX, ALU.max)
                dve.drain()
                nc.vector.tensor_tensor(mn[:, sd, :], mp[:, sd, :], emax[:, sd, :], ALU.max)
                if full:
                    nc.vector.tensor_tensor(mx[:, :, :], mp[:, :, :], me[:, :, :], ALU.max)
                dve.drain()
                gd = lambda c: g[:, c:c + 2 * HM].rearrange("p (d h) -> p d h", d=2)[:, sd, :]
                nc.vector.tensor_tensor(args[:, WA, sd, :], mp[:, sd, :], mn[:, sd, :], ALU.subtract)
                nc.vector.tensor_tensor(args[:, KW, sd, :], gd(G_E), mn[:, sd, :], ALU.subtract)
                if full:
                    nc.vector.tensor_scalar(nmx[:, :, :], mx[:, :, :], -1.0, None, ALU.mult)
                    nc.vector.tensor_tensor(args[:, WI, :, :], mp[:, :, :], mx[:, :, :], ALU.subtract)
                    dve.drain()
                    nc.vector.tensor_tensor(args[:, DN, :, :], nmx[:, :, :], gd(G_BC), ALU.subtract)
                dve.drain()
                nc.vector.tensor_tensor(mp[:, sd, :], mn[:, sd, :], gd(G_TOT), ALU.add)
                dve.drain()
                dve.sem_inc(args_ready, 1)
                dve.wait_ge(ex_ready, i + 1)
                dve.wait_ge(K_ready, i + 1)
                for d in steps:
                    nc.vector.scalar_tensor_tensor(Ks[:, d], Kt[:, :, :], DM ** -0.5, bc_last(ex[:, KW, d, :], DM), ALU.mult, ALU.mult)
                dve.drain()
                dve.sem_inc(Ks_ready, 1)
                if full:
                    dve.wait_ge(qk_mm, i + 1)
                    dve.wait_ge(X_ready, i + 1)
                    for d in range(2):
                        for h in range(HM):
                            nc.vector.scalar_tensor_tensor(Em[:, d, h, :], half[6][:, h * P:(h + 1) * P], DM ** -0.5, Em[:, d, h, :],
                                                           ALU.mult, ALU.mult, accum_out=rs[:, d, h:h + 1])
                    dve.drain()
                    if prior:
                        dve.wait_ge(norm_mm, i + 1)
                        nc.vector.tensor_tensor(den[:, :, :], half[7][:, 0:2 * HM].rearrange("p (h d) -> p d h", d=2),
                                                ex[:, WI, :, :], ALU.mult)
                        dve.drain()
                        nc.vector.tensor_tensor(rs[:, :, :], rs[:, :, :], den[:, :, :], ALU.add)
                        dve.drain()
                    nc.vector.scalar_tensor_tensor(den[:, :, :], rs[:, :, :], -1.0, rs[:, :, :], ALU.mult, ALU.max)
                    dve.drain()
                    nc.vector.tensor_tensor(den[:, :, :], den[:, :, :], ex[:, DN, :, :], ALU.max)
                    dve.drain()
                    nc.vector.reciprocal(r[:, :, :], den[:, :, :])
                    dve.drain()
                    nc.vector.tensor_tensor(rw[:, :, :], r[:, :, :], ex[:, WI, :, :], ALU.mult)
                    for h in range(HM):
                        nc.vector.tensor_scalar(Pc[:, h, :], Em[:, 0, h, :], r[:, 0, h:h + 1], None, ALU.mult)
                    dve.drain()
                    for h in range(HM):
                        nc.vector.scalar_tensor_tensor(Pc[:, h, :], Em[:, 1, h, :], r[:, 1, h:h + 1], Pc[:, h, :], ALU.mult, ALU.add)
                    dve.drain()
                    dve.sem_inc(P_mixed, 1)
                    dve.wait_ge(hm_out, i * 16 + 16)
                    if prior:
                        dve.wait_ge(inter_mm, i + 1)
                        for h in range(HM):
                            nc.vector.tensor_scalar(hm[:, h, :], bank[0][:, h * DM:(h + 1) * DM], rw[:, 0, h:h + 1], None, ALU.mult)
                        dve.drain()
                        for h in range(HM):
                            nc.vector.scalar_tensor_tensor(hm[:, h, :], bank[1][:, h * DM:(h + 1) * DM], rw[:, 1, h:h + 1],
                                                           hm[:, h, :], ALU.mult, ALU.add)
                        dve.drain()
                        dve.sem_inc(inter_used, 1)
                    dve.wait_ge(hv_mm, i + 1)
                    hv = bank[3][:, :].rearrange("p (h c) -> p h c", c=DM)
                    if prior:
                        nc.vector.tensor_tensor(hm[:, :, :], hm[:, :, :], hv, ALU.add).then_inc(hm_done, 1)
                    else:
                        nc.vector.tensor_copy(hm[:, :, :], hv).then_inc(hm_done, 1)
                for u in range(2 * NM):
                    d, h, k = steps[u // (2 * HM)], u // 2 % HM, u % 2
                    dve.wait_ge(mstate_mm, i * (2 * NM) + (u + 1))
                    if prior:
                        nc.vector.scalar_tensor_tensor(C[d][:, h, k, :], C[d][:, h, k, :], ex[:, WA, d, h:h + 1], half[u % 4][:, 0:CE],
                                                       ALU.mult, ALU.add).then_inc(C_new, 1)
                    else:
                        nc.vector.tensor_copy(C[d][:, h, k, :], half[u % 4][:, 0:CE]).then_inc(C_new, 1)
                dve.drain()
                dve.sem_inc(chunk_done, 1)
                if kind == "back":
                    for j in range(2):
                        biased(i, j)

            loop(dve, body)
            if kind == "back":
                for j in range(2):
                    biased(N, j)
                dve.drain()
                for vector, plus, gain in ((V_GATE_A, 0.0, 0), (V_SCALE_F, 1.0, 1), (V_GATE_F, 0.0, 2)):
                    at = slice(vector * D, (vector + 1) * D)
                    nc.vector.scalar_tensor_tensor(m_rows[:, at], m_rows[:, at], plus, m_gain[:, gain, :], ALU.add, ALU.mult)


def merge(nc, dr, t):
    with ExitStack() as ctx:
        sb = lambda n, s, d=F32: ctx.enter_context(nc.sbuf_tensor("m_" + n, s, d))
        sem = semaphores(nc, ctx, "m_")
        wts = sb("w", [P, 3, KT, D])
        y, z, hm, o = sb("y", [P, D]), sb("z", [P, D]), sb("hm", [P, HM, DM]), sb("o", [P, HM, DM])
        sz, yn, hn = sb("sz", [P, D]), sb("yn", [P, D]), sb("hn", [P, HM, DM])
        yT, hT = sb("yT", [P, KT, P]), sb("hT", [P, KT, P])
        mg, x = sb("mg", [P, 2, D]), sb("x", [P, D])
        rows = sb("rows", [P, 3, D])
        mix, mixT, gated, h2 = sb("mix", [P, D]), sb("mixT", [P, KT, P]), sb("gated", [P, D]), sb("h2", [P, D])
        sq = sb("sq", [P, D])
        ss, root, rr = sb("ss", [P, 7]), sb("root", [P, 7]), sb("rr", [P, 7])
        bank = [ctx.enter_context(nc.psum_tensor(f"m_bank{i}", [P, 1024], F32)) for i in range(4)]
        w_in = [sem(f"w_in{k}") for k in range(3)]
        head_in = sem("head_in")
        branches_in, gates_in, x_in = sem("branches_in"), sem("gates_in"), sem("x_in")
        branch_sig, gate_sig, y_gated, branch_sums, branch_ms, branch_root, normed, turned, gained = (
            sem("branch_sig"), sem("gate_sig"), sem("y_gated"), sem("branch_sums"), sem("branch_ms"), sem("branch_root"),
            sem("normed"), sem("turned"), sem("gained"))
        branch_mm, mixed, mix_turned, mixT_ready, out_mm = sem("branch_mm"), sem("mixed"), sem("mix_turned"), sem("mixT_ready"), sem("out_mm")
        out_sums, out_ms, out_root, x1_ready, x1_sums, x1_ms, x1_root, h2_ready = (
            sem("out_sums"), sem("out_ms"), sem("out_root"), sem("x1_ready"), sem("x1_sums"), sem("x1_ms"), sem("x1_root"), sem("h2_ready"))
        x1_out, h2_out, sp_passed = sem("x1_out"), sem("h2_out"), sem("sp_passed")
        out_free = sem("out_free")
        block = ctx.enter_context(nc.Block())
        flat = lambda ap: ap.rearrange("p h c -> p (h c)")

        def turns(eng, ahead, turn):
            ahead(0)
            with eng.Fori(0, BLOCKS - 1) as i:
                turn(i, True)
            turn(BLOCKS - 1, False)

        @block.sync
        def _(sp):
            def of(ap, b):
                return ap[b] if isinstance(b, int) else row(ap[bass.ds(b, 1)])

            def load_branches(b):
                pr = of(dr["proj"], b)
                sp.dma_start(y[:, :], of(dr["y_ssd"], b)).then_inc(branches_in, 16)
                sp.dma_start(z[:, :], pr[:, COL_Z:COL_Z + D]).then_inc(branches_in, 16)
                sp.dma_start(flat(hm[:, :, :]), of(dr["y_mlstm"], b)).then_inc(branches_in, 16)
                sp.dma_start(flat(o[:, :, :]), pr[:, COL_O:COL_O + D]).then_inc(branches_in, 16)

            def load_gates(b):
                sp.dma_start(flat(mg[:, :, :]), of(dr["proj"], b)[:, COL_M:COL_M + 2 * D]).then_inc(gates_in, 16)

            def load_x(b):
                sp.dma_start(x[:, :], of(dr["x"], b)).then_inc(x_in, 16)
                r = of(dr["mod_rows"], b)[0:1, V_GATE_A * D:(V_SCALE_F + 1) * D]
                sp.dma_start(flat(rows[:, :, :]), r.partition_broadcast(P)).then_inc(x_in, 16)

            def turn(b, two_more, one_more):
                if two_more:
                    sp.wait_ge(normed, b + 2)
                    sp.sem_inc(sp_passed, 1)
                    load_branches(b + 2)
                if one_more:
                    sp.wait_ge(mixed, b + 1)
                    sp.sem_inc(sp_passed, 1)
                    load_gates(b + 1)
                sp.wait_ge(x1_ready, b + 1)
                sp.sem_inc(sp_passed, 1)
                sp.dma_start(of(dr["x1"], b), x[:, :]).then_inc(x1_out, 16)
                sp.wait_ge(h2_ready, b + 1)
                sp.sem_inc(sp_passed, 1)
                sp.dma_start(of(dr["h2"], b), h2[:, :]).then_inc(h2_out, 16)
                sp.wait_ge(x1_out, b * 16 + 16)
                sp.sem_inc(sp_passed, 1)
                if one_more:
                    load_x(b + 1)

            load_branches(0)
            sp.dma_start(wts[:, 0], dr["w_out3"][0]).then_inc(w_in[0], 16)
            load_gates(0)
            sp.wait_ge(normed, 1)
            load_branches(1)
            sp.dma_start(wts[:, 1], dr["w_out3"][1]).then_inc(w_in[1], 16)
            sp.dma_start(wts[:, 2], dr["w_out3"][2]).then_inc(w_in[2], 16)
            load_x(0)
            sp.dma_start(t["w_head"][:, :, :], dr["w_q"][:, :, (HP - 1) * 2 * P:HP * 2 * P]).then_inc(head_in, 16)
            sp.dma_start(t["keys"][:, :, :], dr["keysT"]).then_inc(head_in, 16)
            with sp.Fori(0, BLOCKS - 2) as i:
                turn(sp.snap(i + 0), True, True)
            turn(BLOCKS - 2, False, True)
            turn(BLOCKS - 1, False, False)
            sp.wait_ge(h2_out, BLOCKS * 16 + 16)
            sp.wait_ge(head_in, 32)

        @block.scalar
        def _(act):
            def ahead(b):
                act.wait_ge(branches_in, b * 64 + 64)
                nc.scalar.activation(sz[:, :], z[:, :], ACT.Sigmoid)
                nc.scalar.activation(o[:, :, :], o[:, :, :], ACT.Sigmoid).then_inc(branch_sig, 1)
                for h in range(HM):
                    nc.scalar.activation(sq[:, h * DM:(h + 1) * DM], hm[:, h, :], ACT.Square, accum_out=ss[:, 1 + h:2 + h])
                act.drain()
                act.wait_ge(y_gated, b + 1)
                nc.scalar.activation(sq[:, :], yn[:, :], ACT.Square, accum_out=ss[:, 0:1])
                act.drain()
                act.sem_inc(branch_sums, 1)
                act.wait_ge(branch_ms, b + 1)
                nc.scalar.activation(root[:, 0:5], ss[:, 0:5], ACT.Sqrt).then_inc(branch_root, 1)

            def turn(b, more):
                act.wait_ge(gates_in, b * 16 + 16)
                nc.scalar.activation(mg[:, :, :], mg[:, :, :], ACT.Sigmoid).then_inc(gate_sig, 1)
                if more:
                    ahead(b + 1)
                act.wait_ge(mix_turned, b + 1)
                nc.scalar.copy(flat(mixT[:, :, :]), bank[2][:, :]).then_inc(mixT_ready, 1)
                act.wait_ge(out_mm, b + 1)
                nc.scalar.activation(sq[:, :], bank[3][:, :], ACT.Square, accum_out=ss[:, 5:6])
                act.drain()
                act.sem_inc(out_sums, 1)
                act.wait_ge(out_ms, b + 1)
                nc.scalar.activation(root[:, 5:6], ss[:, 5:6], ACT.Sqrt).then_inc(out_root, 1)
                act.wait_ge(x1_ready, b + 1)
                nc.scalar.activation(sq[:, :], x[:, :], ACT.Square, accum_out=ss[:, 6:7])
                act.drain()
                act.sem_inc(x1_sums, 1)
                act.wait_ge(x1_ms, b + 1)
                nc.scalar.activation(root[:, 6:7], ss[:, 6:7], ACT.Sqrt).then_inc(x1_root, 1)

            turns(act, ahead, turn)

        @block.tensor
        def _(pe):
            def ahead(b):
                pe.wait_ge(normed, b + 1)
                for k in range(KT):
                    nc.tensor.transpose(bank[0][:, k * P:(k + 1) * P], yn[:, k * P:(k + 1) * P], t["ident"][:, :])
                for k in range(KT):
                    last = nc.tensor.transpose(bank[1][:, k * P:(k + 1) * P], flat(hn[:, :, :])[:, k * P:(k + 1) * P], t["ident"][:, :])
                last.then_inc(turned, 1)

            def product(to, src, n):
                for c in range(2):
                    for k in range(KT):
                        last = nc.tensor.matmul(to[:, c * 512:(c + 1) * 512], src[:, k, :],
                                                wts[:, n, k, c * 512:(c + 1) * 512], start=(k == 0), stop=(k == KT - 1))
                return last

            def turn(b, more):
                pe.wait_ge(gained, b + 1)
                pe.wait_ge(w_in[0], 16)
                product(bank[2], yT, 0)
                pe.wait_ge(out_free, b + 1)
                pe.wait_ge(w_in[1], 16)
                product(bank[3], hT, 1).then_inc(branch_mm, 1)
                if more:
                    ahead(b + 1)
                pe.wait_ge(mixed, b + 1)
                for k in range(KT):
                    last = nc.tensor.transpose(bank[2][:, k * P:(k + 1) * P], mix[:, k * P:(k + 1) * P], t["ident"][:, :])
                last.then_inc(mix_turned, 1)
                pe.wait_ge(mixT_ready, b + 1)
                pe.wait_ge(w_in[2], 16)
                product(bank[3], mixT, 2).then_inc(out_mm, 1)

            turns(pe, ahead, turn)

        @block.vector
        def _(dve):
            dve.sem_inc(out_free, 1)
            dve.sem_inc(h2_out, 16)

            def ahead(b):
                dve.wait_ge(branches_in, b * 64 + 64)
                nc.vector.tensor_tensor(yn[:, :], y[:, :], z[:, :], ALU.mult)
                dve.drain()
                dve.wait_ge(branch_sig, b + 1)
                nc.vector.tensor_tensor(yn[:, :], yn[:, :], sz[:, :], ALU.mult).then_inc(y_gated, 1)
                dve.wait_ge(branch_sums, b + 1)
                nc.vector.tensor_scalar(ss[:, 0:1], ss[:, 0:1], 1.0 / D, EPS, ALU.mult, ALU.add)
                nc.vector.tensor_scalar(ss[:, 1:5], ss[:, 1:5], 1.0 / DM, EPS, ALU.mult, ALU.add)
                dve.drain()
                dve.sem_inc(branch_ms, 1)
                dve.wait_ge(branch_root, b + 1)
                nc.vector.reciprocal(rr[:, 0:5], root[:, 0:5])
                dve.drain()
                nc.vector.tensor_scalar(yn[:, :], yn[:, :], rr[:, 0:1], None, ALU.mult)
                for h in range(HM):
                    nc.vector.scalar_tensor_tensor(hn[:, h, :], hm[:, h, :], rr[:, 1 + h:2 + h], o[:, h, :], ALU.mult, ALU.mult)
                dve.drain()
                dve.sem_inc(normed, 1)

            def gain(b):
                dve.wait_ge(turned, b + 1)
                nc.vector.tensor_tensor(yT[:, :, :], bank[0][:, :].rearrange("p (k t) -> p k t", t=P), bc_last(t["gains"][:, 4, :], P), ALU.mult)
                nc.vector.tensor_tensor(hT[:, :, :], bank[1][:, :].rearrange("p (k t) -> p k t", t=P), bc_last(t["gains"][:, 5, :], P), ALU.mult)
                dve.drain()
                dve.sem_inc(gained, 1)

            def inverse_root(b, n, sums, ms, roots):
                dve.wait_ge(sums, b + 1)
                nc.vector.tensor_scalar(ss[:, n:n + 1], ss[:, n:n + 1], 1.0 / D, EPS, ALU.mult, ALU.add).then_inc(ms, 1)
                dve.wait_ge(roots, b + 1)
                nc.vector.reciprocal(rr[:, n:n + 1], root[:, n:n + 1])
                dve.drain()

            def turn(b, more):
                if more:
                    ahead(b + 1)
                dve.wait_ge(gate_sig, b + 1)
                dve.wait_ge(branch_mm, b + 1)
                nc.vector.tensor_tensor(mix[:, :], mg[:, 0, :], bank[2][:, :], ALU.mult)
                nc.vector.tensor_tensor(gated[:, :], mg[:, 1, :], bank[3][:, :], ALU.mult)
                dve.drain()
                nc.vector.tensor_tensor(mix[:, :], mix[:, :], gated[:, :], ALU.add)
                dve.drain()
                dve.sem_inc(mixed, 1)
                if more:
                    gain(b + 1)
                inverse_root(b, 5, out_sums, out_ms, out_root)
                dve.wait_ge(x_in, b * 32 + 32)
                nc.vector.scalar_tensor_tensor(gated[:, :], bank[3][:, :], rr[:, 5:6], rows[:, V_GATE_A, :], ALU.mult, ALU.mult)
                dve.drain()
                dve.sem_inc(out_free, 1)
                nc.vector.tensor_tensor(x[:, :], x[:, :], gated[:, :], ALU.add).then_inc(x1_ready, 1)
                inverse_root(b, 6, x1_sums, x1_ms, x1_root)
                dve.wait_ge(h2_out, b * 16 + 16)
                nc.vector.scalar_tensor_tensor(h2[:, :], x[:, :], rr[:, 6:7], rows[:, V_SCALE_F, :], ALU.mult, ALU.mult)
                dve.drain()
                nc.vector.tensor_tensor(h2[:, :], h2[:, :], rows[:, V_SHIFT_F, :], ALU.add).then_inc(h2_ready, 1)

            ahead(0)
            gain(0)
            with dve.Fori(0, BLOCKS - 1) as i:
                turn(i, True)
            turn(BLOCKS - 1, False)


def channel_mixer(nc, dr, t):
    HALF, RING, AHEAD = 8, 8, 2
    GROUP = 2
    GH = HALF // GROUP
    QUERIES_AT = 1
    with ExitStack() as ctx:
        sb = lambda n, s, d=F32: ctx.enter_context(nc.sbuf_tensor("e_" + n, s, d))
        sem = semaphores(nc, ctx, "e_")
        wq, keys, w_head = sb("wq", [P, KT, 2 * HP * P]), t["keys"], t["w_head"]
        h2, h2T, qT = sb("h2", [P, D]), sb("h2T", [P, KT, P]), sb("qT", [P, 2, P])
        S, S2 = sb("S", [P, 2, P]), sb("S2", [P, 2, P])
        v16, i16, i16f = sb("v16", [P, 2, TOPK]), sb("i16", [P, 2, TOPK], U32), sb("i16f", [P, 2, TOPK])
        cand, cand2 = sb("cand", [P, TOPK, TOPK]), sb("cand2", [P, TOPK, TOPK])
        best, place = sb("best", [P, TOPK]), sb("place", [P, TOPK], U32)
        pick, pickf = sb("pick", [P, 2, TOPK], U32), sb("pickf", [P, 2, TOPK])
        hot, number = sb("hot", [P, 2, TOPK, TOPK]), sb("number", [P, 2, TOPK])
        arg, expo, total = sb("arg", [P, TOPK]), sb("expo", [P, TOPK]), sb("total", [P, 2])
        expert = sb("expert", [P, RING, 2 * D])
        num = sb("num", [P, 2, HALF], U32)
        x_next, xb, x1, row_f, f = sb("x_next", [P, D]), sb("xb", [P, D]), sb("x1", [P, D]), sb("row_f", [P, D]), sb("f", [P, D])
        dots, act_v, coef = sb("dots", [P, 2, HALF]), sb("act", [P, 2, HALF]), sb("coef", [P, 2, HALF])
        diag, zero = sb("diag", [P, HALF, P]), sb("zero", [P, P])
        ss, root, rr = sb("ss", [P, 1]), sb("root", [P, 1]), sb("rr", [P, 1])
        acc = ctx.enter_context(nc.psum_tensor("e_acc", [P, D], F32))
        sq = ctx.enter_context(nc.psum_tensor("e_sq", [P, D], F32))
        qb = [ctx.enter_context(nc.psum_tensor(f"e_q{i}", [P, 512], F32)) for i in range(2)]
        turn = ctx.enter_context(nc.psum_tensor("e_turn", [P, D], F32))
        w_in = sem("w_in")
        h2_in, turned, h2T_ready = sem("h2_in"), sem("turned"), sem("h2T_ready")
        w_copied, q_mm, q_moved, s_mm, S_moved, scored = sem("w_copied"), sem("q_mm"), sem("q_moved"), sem("s_mm"), sem("S_moved"), sem("scored")
        arg_ready, exp_ready, chosen = sem("arg_ready"), sem("exp_ready"), sem("chosen")
        in_slot = [sem(f"in_slot{j}") for j in range(RING)]
        slot_free = sem("slot_free")
        dots_ready, act_ready, coef_ready, diag_ready = sem("dots_ready"), sem("act_ready"), sem("coef_ready"), sem("diag_ready")
        num_ready, zero_ready = sem("num_ready"), sem("zero_ready")
        x_copied, x1_in, f_mm, acc_free, f_free, ms_ready, root_ready, ss_ready, y_ready, y_out = (
            sem("x_copied"), sem("x1_in"), sem("f_mm"), sem("acc_free"), sem("f_free"), sem("ms_ready"),
            sem("root_ready"), sem("ss_ready"), sem("y_ready"), sem("y_out"))
        passed, pe_passed, pool_passed, sp_passed = sem("passed"), sem("pe_passed"), sem("pool_passed"), sem("sp_passed")
        block = ctx.enter_context(nc.Block())

        def schedule(eng, prepare, begin, body, end):
            prepare(0)
            with eng.Fori(0, AHEAD) as k:
                body(None, (k, 0))
            with eng.Fori(0, BLOCKS - 1) as b:
                begin(b)
                with eng.Fori(0, HP - AHEAD) as k:
                    body((k, b), (k + AHEAD, b))
                prepare(b + 1)
                with eng.Fori(0, AHEAD) as k:
                    body((k + (HP - AHEAD), b), (k, b + 1))
                end(b)
            b = BLOCKS - 1
            begin(b)
            with eng.Fori(0, HP - AHEAD) as k:
                body((k, b), (k + AHEAD, b))
            with eng.Fori(0, AHEAD) as k:
                body((k + (HP - AHEAD), b), None)
            end(b)

        def of(ap, b):
            return ap[b] if isinstance(b, int) else row(ap[bass.ds(b, 1)])

        @block.sync
        def _(sp):
            sp.dma_start(h2[:, :], dr["h2"][0]).then_inc(h2_in, 16)
            sp.dma_start(wq[:, :, :], dr["w_q"]).then_inc(w_in, 16)

            sp.wait_ge(x_copied, 1)
            sp.dma_start(h2[:, :], dr["h2"][1]).then_inc(h2_in, 16)

            def run(b, more):
                if more:
                    sp.wait_ge(x_copied, b + 2)
                    sp.sem_inc(sp_passed, 1)
                    sp.dma_start(h2[:, :], of(dr["h2"], b + 2)).then_inc(h2_in, 16)
                sp.dma_start(x1[:, :], of(dr["x1"], b)).then_inc(x1_in, 16)
                r = of(dr["mod_rows"], b)[0:1, V_GATE_F * D:(V_GATE_F + 1) * D]
                sp.dma_start(row_f[:, :], r.partition_broadcast(P)).then_inc(x1_in, 16)
                sp.wait_ge(y_ready, b + 1)
                sp.sem_inc(sp_passed, 1)
                sp.dma_start(of(dr["out_y"], b), x1[:, :]).then_inc(y_out, 16)
                sp.wait_ge(y_out, b * 16 + 16)
                sp.sem_inc(sp_passed, 1)

            with sp.Fori(0, BLOCKS - 2) as b:
                run(b, True)
            run(BLOCKS - 2, False)
            run(BLOCKS - 1, False)

        @block.gpsimd
        def _(pool):
            with pool.Fori(0, BLOCKS) as b:
                with pool.Fori(0, HP) as k:
                    pool.wait_ge(chosen, b * HP + k + 1)
                    for half in range(2):
                        s = (b * HP + k) * (2 * HALF) + half * HALF
                        pool.wait_ge(slot_free, s + 1)
                        pool.sem_inc(pool_passed, 1)
                        nc.gpsimd.tensor_copy(num[:, half, :], t["idx"][:, :, :].rearrange("p b n -> p (b n)")[:, bass.ds(s, HALF)]).then_inc(num_ready, 1)
                        pool.wait_ge(num_ready, (b * HP + k) * 2 + (half + 1))
                        for j in range(HALF):
                            pool.wait_ge(slot_free, s + (j + 1))
                            pool.sem_inc(pool_passed, 1)
                            nc.gpsimd.indirect_dma_start(expert[:, j, :], None, dr["peer_uv"], bass.IndirectOffsetOnAxis(num[:, half, j:j + 1], 0)).then_inc(in_slot[j], 16)

        @block.vector
        def _(dve):
            dve.sem_inc(f_free, 1)
            dve.sem_inc(scored, 1)
            nc.vector.memset(zero[:, :], 0.0).then_inc(zero_ready, 1)

            def group_dots(k, b, half, q):
                seen = (b * HP + k) * 2 + half
                for j in range(GROUP * q, GROUP * (q + 1)):
                    dve.wait_ge(in_slot[j], seen * 16 + 16)
                    nc.vector.tensor_tensor_reduce(expert[:, j, 0:D], expert[:, j, 0:D], xb[:, :], 1.0, 0.0, ALU.mult, ALU.add,
                                                   dots[:, half, j:j + 1])
                dve.drain()
                dve.sem_inc(dots_ready, 1)

            def group_gates(k, b, half, q):
                seen = (b * HP + k) * 2 + half
                dve.wait_ge(act_ready, seen * GH + (q + 1))
                dve.sem_inc(passed, 1)
                w = slice(GROUP * q, GROUP * (q + 1))
                gates = t["gate"][:, :, :].rearrange("p b n -> p (b n)")
                nc.vector.tensor_tensor(coef[:, half, w], act_v[:, half, w],
                                        gates[:, bass.ds(seen * HALF + GROUP * q, GROUP)], ALU.mult).then_inc(coef_ready, 1)

            def best16(values, scratch, v, index):
                n = len(values)
                for a in range(n):
                    nc.vector.max(v[a][:, 0:8], values[a])
                dve.drain()
                for a in range(n):
                    nc.vector.match_replace(scratch[a], v[a][:, 0:8], values[a], -3.0e38)
                dve.drain()
                for a in range(n):
                    nc.vector.max(v[a][:, 8:16], scratch[a])
                    nc.vector.max_index(index[a][:, 0:8], v[a][:, 0:8], values[a])
                dve.drain()
                for a in range(n):
                    nc.vector.max_index(index[a][:, 8:16], v[a][:, 8:16], scratch[a])
                dve.drain()

            flat = lambda ap: ap.rearrange("p a b -> p (a b)")

            def keys_of_head(k, c):
                turn_no = c * HP + k
                dve.wait_ge(S_moved, turn_no + 1)
                dve.sem_inc(passed, 1)
                best16([S[:, n, :] for n in range(2)], [S2[:, n, :] for n in range(2)], [v16[:, n, :] for n in range(2)],
                       [i16[:, n, :] for n in range(2)])
                dve.sem_inc(scored, 1)
                nc.vector.tensor_copy(i16f[:, :, :], i16[:, :, :])
                nc.vector.tensor_tensor(cand[:, :, :], bc_last(v16[:, 0, :], TOPK),
                                        v16[:, 1, :].unsqueeze(1).to_broadcast([P, TOPK, TOPK]), ALU.add)
                dve.drain()

            def sums_of_head(k, c):
                best16([flat(cand[:, :, :])], [flat(cand2[:, :, :])], [best[:, :]], [place[:, :]])
                nc.vector.tensor_scalar(arg[:, :], best[:, :], best[:, 0:1], None, ALU.subtract).then_inc(arg_ready, 1)

            def experts_of_head(k, c):
                turn_no = c * HP + k
                nc.vector.tensor_scalar(pick[:, 0, :], place[:, :], 4, None, ALU.logical_shift_right)
                nc.vector.tensor_scalar(pick[:, 1, :], place[:, :], 15, None, ALU.bitwise_and)
                dve.drain()
                nc.vector.tensor_copy(pickf[:, :, :], pick[:, :, :])
                dve.drain()
                nc.vector.tensor_tensor(hot[:, :, :, :].rearrange("p c k j -> p (c k) j"), bc_last(flat(pickf[:, :, :]), TOPK),
                                        t["iota"][:, :].unsqueeze(1).to_broadcast([P, 2 * TOPK, TOPK]), ALU.is_equal)
                dve.drain()
                nc.vector.tensor_tensor(hot[:, :, :, :], hot[:, :, :, :], i16f[:, :, :].unsqueeze(2).to_broadcast([P, 2, TOPK, TOPK]), ALU.mult)
                dve.drain()
                nc.vector.tensor_reduce(number[:, :, :], hot[:, :, :, :], AX, ALU.add)
                dve.drain()
                dve.wait_ge(exp_ready, turn_no + 1)
                nc.vector.scalar_tensor_tensor(number[:, 0, :], number[:, 0, :], float(P), number[:, 1, :], ALU.mult, ALU.add)
                nc.vector.tensor_reduce(total[:, 0:1], expo[:, :], AX, ALU.add)
                dve.drain()
                nc.vector.reciprocal(total[:, 1:2], total[:, 0:1])
                at = bass.ds(turn_no * TOPK, TOPK)
                nc.vector.tensor_copy(flat(t["idx"][:, :, :])[:, at], number[:, 0, :])
                dve.drain()
                nc.vector.tensor_scalar(flat(t["gate"][:, :, :])[:, at], expo[:, :], total[:, 1:2], None, ALU.mult)
                dve.drain()
                dve.sem_inc(chosen, 1)

            def prepare(c):
                dve.wait_ge(turned, c + 1)
                nc.vector.tensor_copy(x_next[:, :], h2[:, :]).then_inc(x_copied, 1)

            def begin(b):
                dve.drain()
                nc.vector.tensor_copy(xb[:, :], x_next[:, :])
                dve.drain()

            def body(run, choose):
                for n in range(2 * GH):
                    half, q, step = n // GH, n % GH, {2 * GH - 3: keys_of_head, 2 * GH - 1: sums_of_head}.get(n)
                    if run:
                        group_dots(*run, half, q)
                        group_gates(*run, half, q)
                    if choose and step:
                        step(*choose)
                if choose:
                    experts_of_head(*choose)

            def end(b):
                dve.wait_ge(ss_ready, b + 1)
                nc.vector.tensor_scalar(ss[:, :], ss[:, :], 1.0 / D, EPS, ALU.mult, ALU.add).then_inc(ms_ready, 1)
                dve.wait_ge(root_ready, b + 1)
                nc.vector.reciprocal(rr[:, :], root[:, :])
                dve.drain()
                dve.wait_ge(x1_in, b * 32 + 32)
                nc.vector.scalar_tensor_tensor(f[:, :], f[:, :], rr[:, 0:1], row_f[:, :], ALU.mult, ALU.mult)
                dve.drain()
                nc.vector.tensor_tensor(x1[:, :], x1[:, :], f[:, :], ALU.add)
                dve.drain()
                dve.sem_inc(y_ready, 1)
                dve.sem_inc(f_free, 1)

            schedule(dve, prepare, begin, body, end)

        @block.scalar
        def _(act):
            act.sem_inc(acc_free, 1)
            act.sem_inc(w_copied, 1)

            def prepare(c):
                act.wait_ge(turned, c + 1)
                nc.scalar.copy(h2T[:, :, :].rearrange("p k t -> p (k t)"), turn[:, :]).then_inc(h2T_ready, 1)

            def head_weights(k):
                act.wait_ge(w_in, 16)
                nc.scalar.copy(w_head[:, :, :], wq[:, :, bass.ds(k * (2 * P), 2 * P)]).then_inc(w_copied, 1)

            def queries(k, c):
                j = c * HP + k
                act.wait_ge(q_mm, j + 1)
                for n in range(2):
                    last = nc.scalar.copy(qT[:, n, :], qb[n][:, 0:P])
                last.then_inc(q_moved, 1)

            def scores(k, c):
                j = c * HP + k
                act.wait_ge(s_mm, j + 1)
                act.wait_ge(scored, j + 1)
                nc.scalar.copy(S[:, :, :].rearrange("p n k -> p (n k)"), turn[:, 0:2 * P]).then_inc(S_moved, 1)

            def exponentials(k, c):
                j = c * HP + k
                act.wait_ge(arg_ready, j + 1)
                nc.scalar.activation(expo[:, :], arg[:, :], ACT.Exp).then_inc(exp_ready, 1)

            def gelus(k, b, half, q):
                seen = (b * HP + k) * 2 + half
                w = slice(GROUP * q, GROUP * (q + 1))
                act.wait_ge(dots_ready, seen * GH + (q + 1))
                nc.scalar.activation(act_v[:, half, w], dots[:, half, w], ACT.Gelu).then_inc(act_ready, 1)

            def diagonals(k, b, half, q):
                seen = (b * HP + k) * 2 + half
                act.wait_ge(coef_ready, seen * GH + (q + 1))
                act.wait_ge(slot_free, seen * HALF + GROUP * (q + 1))
                for j in range(GROUP):
                    at = GROUP * q + j
                    last = nc.scalar.mul(diag[:, at, :], t["ident"][:, :], coef[:, half, at:at + 1])
                last.then_inc(diag_ready, 1)

            def body(run, choose):
                for n in range(2 * GH):
                    if run:
                        gelus(*run, n // GH, n % GH)
                        diagonals(*run, n // GH, n % GH)
                    if choose and n == QUERIES_AT + 2:
                        queries(*choose)
                        if run:
                            head_weights(choose[0])
                    if choose and n == QUERIES_AT + 3:
                        scores(*choose)
                        if not run:
                            head_weights(choose[0])
                    if choose and n == 2 * GH - 1:
                        exponentials(*choose)

            def end(b):
                act.wait_ge(f_mm, b + 1)
                act.wait_ge(f_free, b + 1)
                nc.scalar.copy(f[:, :], acc[:, :])
                act.drain()
                act.sem_inc(acc_free, 1)
                nc.scalar.activation(sq[:, :], f[:, :], ACT.Square, accum_out=ss[:, :])
                act.drain()
                act.sem_inc(ss_ready, 1)
                act.wait_ge(ms_ready, b + 1)
                nc.scalar.activation(root[:, :], ss[:, :], ACT.Sqrt).then_inc(root_ready, 1)

            schedule(act, prepare, lambda b: None, body, end)

        @block.tensor
        def _(pe):
            pe.sem_inc(slot_free, RING)
            pe.wait_ge(zero_ready, 1)
            z512 = zero[:, :].unsqueeze(1).to_broadcast([P, 4, P])

            def prepare(c):
                pe.wait_ge(h2_in, c * 16 + 16)
                if not isinstance(c, int):
                    pe.wait_ge(S_moved, c * HP)
                for k in range(KT):
                    last = nc.tensor.transpose(turn[:, k * P:(k + 1) * P], h2[:, k * P:(k + 1) * P], t["ident"][:, :])
                last.then_inc(turned, 1)
                pe.wait_ge(h2T_ready, c + 1)
                pe.sem_inc(pe_passed, 1)

            def begin(b):
                pe.wait_ge(acc_free, b + 1)
                for half in range(2):
                    nc.tensor.matmul(acc[:, half * 512:(half + 1) * 512], zero[:, :], z512, start=True, stop=False)

            def group_products(k, b, half, q):
                seen = (b * HP + k) * 2 + half
                pe.wait_ge(diag_ready, seen * GH + (q + 1))
                for j in range(GROUP * q, GROUP * (q + 1)):
                    pe.wait_ge(in_slot[j], seen * 16 + 16)
                    for c in range(2):
                        last = nc.tensor.matmul(acc[:, c * 512:(c + 1) * 512], diag[:, j, :],
                                                expert[:, j, D + c * 512:D + (c + 1) * 512], start=False, stop=False)
                    last.then_inc(slot_free, 1)

            def query(k, c, n):
                if n == 0:
                    pe.wait_ge(w_copied, c * HP + k + 1)
                for m in range(KT):
                    last = nc.tensor.matmul(qb[n][:, 0:P], w_head[:, m, n * P:(n + 1) * P], h2T[:, m, :],
                                            start=(m == 0), stop=(m == KT - 1))
                if n == 1:
                    last.then_inc(q_mm, 1)

            def score(k, c):
                pe.wait_ge(q_moved, c * HP + k + 1)
                for n in range(2):
                    last = nc.tensor.matmul(turn[:, n * P:(n + 1) * P], qT[:, n, :], keys[:, n, :], start=True, stop=True)
                last.then_inc(s_mm, 1)

            def body(run, choose):
                for n in range(2 * GH):
                    if run:
                        group_products(*run, n // GH, n % GH)
                    if choose and QUERIES_AT <= n < QUERIES_AT + 2:
                        query(*choose, n - QUERIES_AT)
                    if choose and n == QUERIES_AT + 2:
                        score(*choose)

            def end(b):
                for c in range(2):
                    last = nc.tensor.matmul(acc[:, c * 512:(c + 1) * 512], zero[:, :], z512, start=False, stop=True)
                last.then_inc(f_mm, 1)

            schedule(pe, prepare, begin, body, end)


def programme(nc, dr):
    with ExitStack() as ctx:
        sb = lambda n, s, d=F32: ctx.enter_context(nc.sbuf_tensor(n, s, d))
        t = {n: sb(n, [P, P]) for n in ("ones", "triF", "triB", "ident", "nident", "maskF", "maskB")}
        t.update({n: sb(n, [P, P], BF16) for n in ("ident_16", "maskF_16", "maskB_16")})
        t["iota_i"], t["iota"] = sb("iota_i", [P, TOPK], mybir.dt.int32), sb("iota", [P, TOPK])
        t["rows"], t["skip"], t["gains"] = sb("rows", [P, R_N]), sb("skip", [P, HS]), sb("gains", [P, 6, KT])
        t["small"], t["gates"] = sb("small", [P, BLOCKS, 48]), sb("gates", [P, BLOCKS, G_N])
        t["idx"], t["gate"] = sb("idx", [P, BLOCKS, SLOTS], U32), sb("gate", [P, BLOCKS, SLOTS])
        t["cv"] = sb("cv", [P, KT, 2])
        with nc.sbuf_tensor("hT", [P, KT, TOK], F32) as hT:
            modulate_and_normalise(nc, dr, t, hT)
            project(nc, dr, t, hT)
        with ExitStack() as scans:
            sc = lambda n, s: scans.enter_context(nc.sbuf_tensor(n, s, F32))
            t["scan_xbcT"], t["scan_qkT"], t["scan_v"] = sc("xbcT", [P, 16, P]), sc("qkT", [P, 16, P]), sc("v", [P, HM, CE])
            t["scan_H"], t["scan_C"] = [sc(f"H{d}", [P, D]) for d in range(2)], [sc(f"C{d}", [P, HM, 2, CE]) for d in range(2)]
            t["scan_m"] = sc("m", [P, 2, HM])
            t["mod_rows"] = sc("mod_rows", [2, V_ROWS * D])
            with nc.sbuf_tensor("wm_later", [P, 2, KT, 512], F32) as t["wm"]:
                scan(nc, dr, t, "prompt")
                scan(nc, dr, t, "back")
            scan(nc, dr, t, "sample")
        t["w_head"], t["keys"] = sb("w_head", [P, KT, 2 * P]), sb("keys", [P, 2, P])
        merge(nc, dr, t)
        channel_mixer(nc, dr, t)


def cat(*a, axis=-1):
    import numpy as np
    return np.concatenate(a, axis=axis)


def tiles(w, n=512):
    import numpy as np
    rows, columns = w.shape
    return np.ascontiguousarray(w.reshape(rows // P, P, columns // n, n).transpose(2, 1, 0, 3))


def cols(v):
    import numpy as np
    v = v.reshape(*v.shape[:-1], v.shape[-1] // P, P)
    return np.ascontiguousarray(np.moveaxis(v, -1, 0))


def layout(i):
    import numpy as np
    w = i["w_in"][0]
    z, xbc, dt, q, k, v, o, g, m = np.split(w, np.cumsum([1024, 2048, 32, 1024, 1024, 1024, 1024, 16]), axis=1)
    g = g.reshape(1024, 2, 2, 4).transpose(0, 2, 1, 3).reshape(1024, 16)
    out = {}
    out["x"] = cat(i["x_prompt"].reshape(1, 128, 1024), i["x_sample"].reshape(4, 128, 1024), axis=0)
    out["cvT"] = np.ascontiguousarray(np.moveaxis(cols(cat(i["c_ctx"][None], i["c"], axis=0)), 1, 2))
    out["w_mod"] = tiles(i["w_mod"][0])
    out["b_mod"] = i["b_mod"]
    out["gain_rows"] = cat(*[i[n] for n in ("g_mix_pre", "g_mix_post", "g_ffn_pre", "g_ffn_post")])
    out["gains"] = cols(np.stack([i[n][0] for n in ("g_mix_pre", "g_mix_post", "g_ffn_pre", "g_ffn_post", "ssd_norm_g", "mlstm_norm_g")]))
    out["small_rows"] = cat(*[i[n].reshape(1, -1) for n in ("ssd_a_log", "ssd_dt_bias", "ssd_d", "mlstm_i_bias", "mlstm_f_bias", "state_mlstm_m")])
    out["w_big"] = tiles(cat(z, v, o, m, xbc, q, k))
    out["w_small"] = tiles(cat(dt, g), 48)[0]
    out["convT"] = cols(cat(i["conv_w"][0], i["conv_b"], axis=0))
    out["w_out3"] = np.stack([tiles(i[n][0], 1024)[0] for n in ("w_ssd_out", "w_mlstm_out", "w_out")])
    out["w_q"] = tiles(cat(i["peer_w_q"][0][:, 256:], i["peer_w_q"][0][:, :256]), 2048)[0]
    out["keysT"] = np.ascontiguousarray(np.stack([i["peer_keys1"][0].T, i["peer_keys2"][0].T], axis=1))
    out["peer_uv"] = cat(i["peer_u"][0], i["peer_v"][0])
    out["state_ssd"] = np.ascontiguousarray(i["state_ssd"].reshape(2, 1024, 128).transpose(0, 2, 1))
    c = cat(i["state_mlstm_c"].reshape(2, 4, 2, 128, 256), i["state_mlstm_n"].reshape(2, 4, 2, 128, 1))
    out["state_c"] = np.ascontiguousarray(c.transpose(0, 3, 1, 2, 4)).reshape(2, 128, 8 * 257)
    return out


SCRATCH = {
    "mod_rows": (BLOCKS, 1, V_ROWS * D), "proj": (BLOCKS, P, COLS_T), "xbcT": (16, P, TOK), "qkT": (16, P, TOK),
    "back_ssd": (CHUNKS, P, D), "back_c": (CHUNKS, P, HM * 2 * CE), "back_m": (CHUNKS, P, HM),
    "y_ssd": (BLOCKS, P, D), "y_mlstm": (BLOCKS, P, D), "x1": (BLOCKS, P, D), "h2": (BLOCKS, P, D),
}
OUTPUTS = {"out_y": (BLOCKS, P, D), "out_ssd": (2, P, D), "out_c": (2, P, HM * 2 * CE), "out_m": (1, 2 * HM)}


def kernel(**inputs):
    import numpy as np
    import concourse.bacc as bacc
    from concourse.bass_utils import run_bass_kernel_spmd

    nc = bacc.Bacc("TRN2", target_bir_lowering=False, num_devices=1)
    arrays, dr = {}, {}
    for name, a in layout({k: np.asarray(v) for k, v in inputs.items()}).items():
        arrays["in_" + name] = np.ascontiguousarray(a)
        dr[name] = nc.dram_tensor("in_" + name, a.shape, F32, kind="ExternalInput").ap()
    for name, shape in SCRATCH.items():
        dr[name] = nc.dram_tensor("scratch_" + name, shape, F32, kind="Internal").ap()
    for name, shape in OUTPUTS.items():
        dr[name] = nc.dram_tensor(name, shape, F32, kind="ExternalOutput").ap()
    programme(nc, dr)
    got = run_bass_kernel_spmd(nc, [arrays], core_ids=[0]).results[0]
    y = got["out_y"]
    ssd = got["out_ssd"].transpose(0, 2, 1).reshape(1, 1, 2, HS, PS, P)
    c = got["out_c"].reshape(2, P, HM, 2, CE).transpose(0, 2, 3, 1, 4).reshape(1, 1, 2, HM, DM, CE)
    return (y[0:1].reshape(1, P, D), y[1:].reshape(1, LAT, D), np.ascontiguousarray(ssd), np.ascontiguousarray(c[..., :DM]),
            np.ascontiguousarray(c[..., DM]), got["out_m"].reshape(1, 1, 2, HM))
```
